# Optimizing a Trainium2 kernel written in Bass

```python
import jax, jax.numpy as jnp
from jax import lax
import numpy as np
import math

D_MODEL = 1024
BATCH = 1
SEQ = 256
DEPTH = 1

EPS = 1e-6
D_FF = 2816
MLA_HEADS = 8
MLA_Q_RANK = 384
MLA_KV_RANK = 256
MLA_NOPE = 64
MLA_ROPE = 32
MLA_V = 64
MLA_THETA = 10000.0
MLA_WIDTH = MLA_HEADS * MLA_V
DIL_HEADS = 8
DIL_HEAD_DIM = 64
DIL_PATTERNS = ((128, 1), (512, 4), (2048, 16))
DIL_WIDTH = DIL_HEADS * DIL_HEAD_DIM
ROPE_THETA = 500000.0
ROPE_DIM = DIL_HEAD_DIM // 4
N_BRANCH = 2
Q_BLOCK = 128
NEG = -1e30
IN_SPLITS = (MLA_Q_RANK, MLA_KV_RANK, MLA_ROPE, DIL_WIDTH, DIL_WIDTH, DIL_WIDTH, N_BRANCH * D_MODEL)
IN_DIM = int(sum(IN_SPLITS))


def rms_norm(x, g):
    xf = x.astype(jnp.float32)
    y = xf * lax.rsqrt(jnp.mean(xf * xf, axis=-1, keepdims=True) + EPS)
    return (y * g.astype(jnp.float32)).astype(x.dtype)

def rope(x, positions, theta, rot_dim):
    half = rot_dim // 2
    inv = 1.0 / (jnp.float32(theta) ** (jnp.arange(half, dtype=jnp.float32) / half))
    ang = positions.astype(jnp.float32)[:, :, None] * inv
    cos = jnp.cos(ang)[:, :, None, :]
    sin = jnp.sin(ang)[:, :, None, :]
    xr = x[..., :rot_dim].astype(jnp.float32)
    x1, x2 = xr[..., :half], xr[..., half:]
    rot = jnp.concatenate([x1 * cos - x2 * sin, x2 * cos + x1 * sin], axis=-1).astype(x.dtype)
    return jnp.concatenate([rot, x[..., rot_dim:]], axis=-1)

def swiglu(x, w_gate, w_up, w_down):
    return (jax.nn.silu(x @ w_gate) * (x @ w_up)) @ w_down

def dense_attention(q, k, v):
    B, S, H, Dk = q.shape
    scale = Dk ** -0.5
    nqb = S // Q_BLOCK
    qb = q.reshape(B, nqb, Q_BLOCK, H, Dk).transpose(1, 0, 2, 3, 4)

    def block(qi):
        s = jnp.einsum('bqhd,bkhd->bhqk', qi, k, preferred_element_type=jnp.float32) * scale
        p = jax.nn.softmax(s, axis=-1)
        return jnp.einsum('bhqk,bkhd->bqhd', p, v.astype(jnp.float32)).astype(v.dtype)

    o = lax.map(block, qb)
    return o.transpose(1, 0, 2, 3, 4).reshape(B, S, H, v.shape[-1])

def dilated_pattern(q, k, v, window, dilation):
    B, S, H, D = q.shape
    half = window // (2 * dilation)
    blk = half
    L = -(-S // dilation)
    Sp = L * dilation
    nb = -(-L // blk)
    Lp = nb * blk

    def split(t):
        t = jnp.pad(t, ((0, 0), (0, Sp - S), (0, 0), (0, 0)))
        return t.reshape(B, L, dilation, H, t.shape[-1]).transpose(0, 2, 3, 1, 4)

    def pad_l(t, lo, hi):
        return jnp.pad(t, ((0, 0), (0, 0), (0, 0), (lo, hi), (0, 0)))

    qs = pad_l(split(q), 0, Lp - L).reshape(B, dilation, H, nb, blk, D)

    def windows(t):
        dt = t.shape[-1]
        t = pad_l(split(t), blk, Lp - L + blk).reshape(B, dilation, H, nb + 2, blk, dt)
        return jnp.concatenate([t[:, :, :, :-2], t[:, :, :, 1:-1], t[:, :, :, 2:]], axis=-2)

    kw = windows(k)
    vw = windows(v)
    s = jnp.einsum('brhnqd,brhnkd->brhnqk', qs, kw, preferred_element_type=jnp.float32) * (D ** -0.5)
    a = jnp.arange(blk)[:, None]
    c = jnp.arange(3 * blk)[None, :]
    band = jnp.abs(c - blk - a) <= half
    jk = jnp.arange(nb)[:, None] * blk - blk + jnp.arange(3 * blk)[None, :]
    pos_k = jk[None] * dilation + jnp.arange(dilation)[:, None, None]
    valid = (jk[None] >= 0) & (pos_k < S)
    mask = band[None, None] & valid[:, :, None, :]
    s = jnp.where(mask[None, :, None], s, NEG)
    m = jnp.max(s, axis=-1, keepdims=True)
    p = jnp.exp(s - m)
    den = jnp.sum(p, axis=-1, keepdims=True)
    num = jnp.einsum('brhnqk,brhnkd->brhnqd', p, vw.astype(jnp.float32))

    def merge(t):
        x_ = t.shape[-1]
        t = t.reshape(B, dilation, H, Lp, x_)[:, :, :, :L]
        return t.transpose(0, 3, 1, 2, 4).reshape(B, Sp, H, x_)[:, :S]

    return merge(m), merge(den), merge(num)

def dilated_mixture(q, k, v):
    parts = [dilated_pattern(q, k, v, w, d) for (w, d) in DIL_PATTERNS]
    m_all = jnp.max(jnp.concatenate([pm for pm, _, _ in parts], axis=-1), axis=-1, keepdims=True)
    num = None
    den = None
    for pm, ps, pn in parts:
        wgt = jnp.exp(pm - m_all)
        num = wgt * pn if num is None else num + wgt * pn
        den = wgt * ps if den is None else den + wgt * ps
    return (num / den).astype(q.dtype)

def hybrid_mixer(u, positions, w_in, b_gate, q_norm_g, w_uq, kv_norm_g, w_uk, w_uv,
                 w_branch_a, w_branch_b, w_out):
    B, S, _ = u.shape
    proj = u @ w_in
    cq, ckv, kr, dq, dk, dv, g = jnp.split(proj, np.cumsum(IN_SPLITS)[:-1].tolist(), axis=-1)

    q = (rms_norm(cq, q_norm_g) @ w_uq).reshape(B, S, MLA_HEADS, MLA_NOPE + MLA_ROPE)
    q = jnp.concatenate([q[..., :MLA_NOPE], rope(q[..., MLA_NOPE:], positions, MLA_THETA, MLA_ROPE)], axis=-1)
    k_rope = rope(kr[:, :, None, :], positions, MLA_THETA, MLA_ROPE)
    c_kv = rms_norm(ckv, kv_norm_g)
    k_nope = (c_kv @ w_uk).reshape(B, S, MLA_HEADS, MLA_NOPE)
    v_a = (c_kv @ w_uv).reshape(B, S, MLA_HEADS, MLA_V)
    k_a = jnp.concatenate([k_nope, jnp.broadcast_to(k_rope, (B, S, MLA_HEADS, MLA_ROPE))], axis=-1)
    o_a = dense_attention(q, k_a, v_a).reshape(B, S, MLA_WIDTH)

    qd = rope(dq.reshape(B, S, DIL_HEADS, DIL_HEAD_DIM), positions, ROPE_THETA, ROPE_DIM)
    kd = rope(dk.reshape(B, S, DIL_HEADS, DIL_HEAD_DIM), positions, ROPE_THETA, ROPE_DIM)
    vd = dv.reshape(B, S, DIL_HEADS, DIL_HEAD_DIM)
    o_b = dilated_mixture(qd, kd, vd).reshape(B, S, DIL_WIDTH)

    gates = jax.nn.sigmoid((g + b_gate).reshape(B, S, N_BRANCH, D_MODEL))
    merged = gates[:, :, 0] * (o_a @ w_branch_a) + gates[:, :, 1] * (o_b @ w_branch_b)
    return merged @ w_out

def first_inputs(seed: int = 0) -> dict:
    key = jax.random.key(seed)
    ks = iter(jax.random.split(key, 32))

    def w(shape, fan_in):
        return jax.random.normal(next(ks), (DEPTH,) + shape, jnp.float32) * (fan_in ** -0.5)

    def gain(n):
        return 1.0 + 0.05 * jax.random.normal(next(ks), (DEPTH, n), jnp.float32)

    x = jax.random.normal(next(ks), (BATCH, SEQ, D_MODEL), jnp.float32)
    offset = jax.random.randint(next(ks), (BATCH, 1), 0, 4096, dtype=jnp.int32)
    positions = (offset + jnp.arange(SEQ, dtype=jnp.int32)[None, :]).astype(jnp.int32)
    return {
        'x': x,
        'positions': positions,
        'ffn1_pre_g': gain(D_MODEL),
        'ffn1_post_g': gain(D_MODEL),
        'ffn1_w_gate': w((D_MODEL, D_FF), D_MODEL),
        'ffn1_w_up': w((D_MODEL, D_FF), D_MODEL),
        'ffn1_w_down': w((D_FF, D_MODEL), D_FF),
        'mix_pre_g': gain(D_MODEL),
        'w_in': w((D_MODEL, IN_DIM), D_MODEL),
        'b_gate': 0.1 * jax.random.normal(next(ks), (DEPTH, N_BRANCH * D_MODEL), jnp.float32),
        'q_norm_g': gain(MLA_Q_RANK),
        'w_uq': w((MLA_Q_RANK, MLA_HEADS * (MLA_NOPE + MLA_ROPE)), MLA_Q_RANK),
        'kv_norm_g': gain(MLA_KV_RANK),
        'w_uk': w((MLA_KV_RANK, MLA_HEADS * MLA_NOPE), MLA_KV_RANK),
        'w_uv': w((MLA_KV_RANK, MLA_HEADS * MLA_V), MLA_KV_RANK),
        'w_branch_a': w((MLA_WIDTH, D_MODEL), MLA_WIDTH),
        'w_branch_b': w((DIL_WIDTH, D_MODEL), DIL_WIDTH),
        'w_out': w((D_MODEL, D_MODEL), D_MODEL),
        'mix_post_g': gain(D_MODEL),
        'ffn2_pre_g': gain(D_MODEL),
        'ffn2_post_g': gain(D_MODEL),
        'ffn2_w_gate': w((D_MODEL, D_FF), D_MODEL),
        'ffn2_w_up': w((D_MODEL, D_FF), D_MODEL),
        'ffn2_w_down': w((D_FF, D_MODEL), D_FF),
    }

def first_block(x, positions, ffn1_pre_g, ffn1_post_g, ffn1_w_gate, ffn1_w_up, ffn1_w_down,
              mix_pre_g, w_in, b_gate, q_norm_g, w_uq, kv_norm_g, w_uk, w_uv,
              w_branch_a, w_branch_b, w_out, mix_post_g,
              ffn2_pre_g, ffn2_post_g, ffn2_w_gate, ffn2_w_up, ffn2_w_down):
    h = x
    for l in range(DEPTH):
        f1 = swiglu(rms_norm(h, ffn1_pre_g[l]), ffn1_w_gate[l], ffn1_w_up[l], ffn1_w_down[l])
        h = h + 0.5 * rms_norm(f1, ffn1_post_g[l])
        mix = hybrid_mixer(rms_norm(h, mix_pre_g[l]), positions, w_in[l], b_gate[l],
                           q_norm_g[l], w_uq[l], kv_norm_g[l], w_uk[l], w_uv[l],
                           w_branch_a[l], w_branch_b[l], w_out[l])
        h = h + rms_norm(mix, mix_post_g[l])
        f2 = swiglu(rms_norm(h, ffn2_pre_g[l]), ffn2_w_gate[l], ffn2_w_up[l], ffn2_w_down[l])
        h = h + 0.5 * rms_norm(f2, ffn2_post_g[l])
    return h


GRID_W = 64
CTX_LEN = 256
CONV_W = 3
M_HEADS = 4
M_HEAD_DIM = 128
M_WIDTH = M_HEADS * M_HEAD_DIM
M_CHUNK = 64
A_HEADS = 4
A_SUB_DIM = 64
A_V_DIM = 2 * A_SUB_DIM
A_WIDTH = A_HEADS * A_V_DIM
ROPE_BASE = 10000.0
ROPE_FREQS = A_SUB_DIM // 4
S_HEADS = 8
S_HEAD_DIM = 64
S_WIDTH = S_HEADS * S_HEAD_DIM
S_GROUPS = 2
S_STATE = 128
S_CHUNK = 64
S_CONV_DIM = S_WIDTH + 2 * S_GROUPS * S_STATE
N_BRANCH_2 = 3
N_MOD = 6
IN_SPLITS_2 = (2 * M_WIDTH, M_WIDTH, M_WIDTH, 4 * M_HEADS, A_WIDTH, A_WIDTH, A_WIDTH, S_WIDTH, S_CONV_DIM, 2 * S_HEADS, N_BRANCH_2 * D_MODEL)
D_IN = sum(IN_SPLITS_2)
NORM_EPS = 1e-6


def rmsnorm(x, g):
    xf = x.astype(jnp.float32)
    y = xf * lax.rsqrt(jnp.mean(xf * xf, axis=-1, keepdims=True) + NORM_EPS)
    return (y * g.astype(jnp.float32)).astype(x.dtype)

def modulate(h, shift, scale):
    return h * (1.0 + scale) + shift

def dwconv(x, w, b=None):
    k = w.shape[0]
    y = lax.conv_general_dilated(x, w[:, None, :].astype(x.dtype), window_strides=(1,),
                                 padding=[(k // 2, k // 2)], dimension_numbers=('NWC', 'WIO', 'NWC'),
                                 feature_group_count=x.shape[-1])
    if b is not None:
        y = y + b.astype(x.dtype)
    return y

def to_chunks(a, axis, size):
    shp = a.shape
    a = a.reshape(shp[:axis] + (shp[axis] // size, size) + shp[axis + 1:])
    return jnp.moveaxis(a, axis, 0)

def from_chunks(a, axis):
    a = jnp.moveaxis(a, 0, axis)
    shp = a.shape
    return a.reshape(shp[:axis] + (shp[axis] * shp[axis + 1],) + shp[axis + 2:])

def rev(a, axis, on):
    return jnp.flip(a, axis=axis) if on else a

def mlstm_scan(q, k, v, ig, lf, state, emit):
    L = M_CHUNK
    causal = jnp.tril(jnp.ones((L, L), dtype=bool))

    def step(carry, inp):
        C, n, m = carry
        qc, kc, vc, ic, fc = inp
        b = jnp.cumsum(fc, axis=-1)
        g_prev = b + m[..., None]
        d_mat = jnp.where(causal, b[..., :, None] - b[..., None, :] + ic[..., None, :], -jnp.inf)
        m_t = jnp.maximum(g_prev, jnp.max(d_mat, axis=-1))
        m_new = m_t[..., -1]
        w_s = jnp.exp(b[..., -1:] - b + ic - m_new[..., None])
        decay = jnp.exp(b[..., -1] + m - m_new)
        C_new = decay[..., None, None] * C + jnp.einsum('bhs,bhsk,bhsv->bhkv', w_s, kc, vc)
        n_new = decay[..., None] * n + jnp.einsum('bhs,bhsk->bhk', w_s, kc)
        if not emit:
            return (C_new, n_new, m_new), None
        w_prev = jnp.exp(g_prev - m_t)
        w = jnp.exp(d_mat - m_t[..., None]) * jnp.einsum('bhtk,bhsk->bhts', qc, kc)
        num = w_prev[..., None] * jnp.einsum('bhtk,bhkv->bhtv', qc, C) + jnp.einsum('bhts,bhsv->bhtv', w, vc)
        den = w_prev * jnp.einsum('bhtk,bhk->bht', qc, n) + jnp.sum(w, axis=-1)
        h = num / jnp.maximum(jnp.abs(den), jnp.exp(-m_t))[..., None]
        return (C_new, n_new, m_new), h

    xs = (to_chunks(q, 2, L), to_chunks(k, 2, L), to_chunks(v, 2, L), to_chunks(ig, 2, L), to_chunks(lf, 2, L))
    state, h = lax.scan(step, state, xs)
    return (from_chunks(h, 2) if emit else None), state

def mlstm_prep(qk_pre, v_pre, gate_pre, conv_w, conv_b, ig_b, fg_b):
    bsz, t = v_pre.shape[:2]
    qk = jax.nn.silu(dwconv(qk_pre, conv_w, conv_b)).astype(jnp.float32)
    q, k = jnp.split(qk, 2, axis=-1)

    def heads(a):
        return a.astype(jnp.float32).reshape(bsz, t, M_HEADS, M_HEAD_DIM).transpose(0, 2, 1, 3)

    g = gate_pre.astype(jnp.float32).reshape(bsz, t, 2, 2, M_HEADS)
    ig = (g[:, :, :, 0] + ig_b).transpose(2, 0, 3, 1)
    lf = jax.nn.log_sigmoid(g[:, :, :, 1] + fg_b).transpose(2, 0, 3, 1)
    return heads(q), heads(k) * M_HEAD_DIM ** -0.5, heads(v_pre), ig, lf

def mlstm_out(h, o_pre, norm_g):
    bsz, t = o_pre.shape[:2]
    h = rmsnorm(h.transpose(0, 2, 1, 3), norm_g.reshape(M_HEADS, M_HEAD_DIM)).reshape(bsz, t, M_WIDTH)
    return (jax.nn.sigmoid(o_pre.astype(jnp.float32)) * h).astype(o_pre.dtype)

def mlstm_mixer(lat, ctx, conv_w, conv_b, ig_b, fg_b, norm_g, emit_ctx):
    q, k, v, ig, lf = mlstm_prep(lat[0], lat[1], lat[3], conv_w, conv_b, ig_b, fg_b)
    qc, kc, vc, igc, lfc = mlstm_prep(ctx[0], ctx[1], ctx[3], conv_w, conv_b, ig_b, fg_b)
    bsz = q.shape[0]
    zeros = (jnp.zeros((bsz, M_HEADS, M_HEAD_DIM, M_HEAD_DIM), jnp.float32),
             jnp.zeros((bsz, M_HEADS, M_HEAD_DIM), jnp.float32),
             jnp.zeros((bsz, M_HEADS), jnp.float32))
    h_lat, h_ctx = 0.0, 0.0
    for d in range(2):
        hc, st = mlstm_scan(rev(qc, 2, d), rev(kc, 2, d), rev(vc, 2, d), rev(igc[d], 2, d), rev(lfc[d], 2, d), zeros, emit_ctx)
        hl, _ = mlstm_scan(rev(q, 2, d), rev(k, 2, d), rev(v, 2, d), rev(ig[d], 2, d), rev(lf[d], 2, d), st, True)
        h_lat = h_lat + rev(hl, 2, d)
        if emit_ctx:
            h_ctx = h_ctx + rev(hc, 2, d)
    out_l = mlstm_out(h_lat, lat[2], norm_g)
    out_c = mlstm_out(h_ctx, ctx[2], norm_g) if emit_ctx else None
    return out_l, out_c

def rope_2d(x, cos, sin):
    shp = x.shape
    xr = x.reshape(shp[:-1] + (2, 2, ROPE_FREQS))
    x1, x2 = xr[..., 0, :], xr[..., 1, :]
    cb, sb = cos[None, :, None, None], sin[None, :, None, None]
    return jnp.stack([x1 * cb - x2 * sb, x2 * cb + x1 * sb], axis=-2).reshape(shp)

def diff_attention(q, k, v, qc, kc, vc, qn_g, kn_g, lam_p, subln_g, lam_init, cos, sin, emit_ctx):
    def heads_qk(a, g, rot):
        bsz, t = a.shape[:2]
        a = rmsnorm(a.reshape(bsz, t, A_HEADS, 2, A_SUB_DIM), g).astype(jnp.float32)
        if rot:
            a = rope_2d(a, cos, sin)
        return a.transpose(0, 2, 3, 1, 4)

    def heads_v(a):
        bsz, t = a.shape[:2]
        return a.reshape(bsz, t, A_HEADS, A_V_DIM).transpose(0, 2, 1, 3).astype(jnp.float32)

    lam_p = lam_p.astype(jnp.float32)
    lam = jnp.exp(jnp.sum(lam_p[0] * lam_p[1])) - jnp.exp(jnp.sum(lam_p[2] * lam_p[3])) + lam_init
    scale = A_SUB_DIM ** -0.5

    def attend(qb, kk, vv):
        s = jnp.einsum('bhjqd,bhjkd->bhjqk', qb, kk) * scale
        p = jax.nn.softmax(s, axis=-1)
        return jnp.einsum('bhqk,bhkv->bhqv', p[:, :, 0] - lam * p[:, :, 1], vv)

    k_ctx, v_ctx = heads_qk(kc, kn_g, False), heads_v(vc)
    k_all = jnp.concatenate([heads_qk(k, kn_g, True), k_ctx], axis=3)
    v_all = jnp.concatenate([heads_v(v), v_ctx], axis=2)
    q_blocks = to_chunks(heads_qk(q, qn_g, True), 3, Q_BLOCK)
    o_lat = from_chunks(lax.map(lambda qb: attend(qb, k_all, v_all), q_blocks), 2)

    def post(o):
        o = rmsnorm(o.transpose(0, 2, 1, 3), subln_g) * (1.0 - lam_init)
        return o.reshape(o.shape[0], o.shape[1], A_WIDTH).astype(q.dtype)

    out_c = post(attend(heads_qk(qc, qn_g, False), k_ctx, v_ctx)) if emit_ctx else None
    return post(o_lat), out_c

def ssd_scan(x, dt, a_coef, bm, cm, state, emit):
    L = S_CHUNK
    rep = S_HEADS // S_GROUPS
    causal = jnp.tril(jnp.ones((L, L), dtype=bool))[None, :, :, None]

    def step(h, inp):
        xk, dtk, bk, ck = inp
        s = jnp.cumsum(dtk * a_coef, axis=1)
        bh = jnp.repeat(bk, rep, axis=2)
        xdt = xk * dtk[..., None]
        h_new = (jnp.exp(s[:, -1])[..., None, None] * h
                 + jnp.einsum('bsh,bshp,bshn->bhpn', jnp.exp(s[:, -1:] - s), xdt, bh))
        if not emit:
            return h_new, None
        ch = jnp.repeat(ck, rep, axis=2)
        seg = jnp.exp(jnp.where(causal, s[:, :, None] - s[:, None], -jnp.inf))
        y = (jnp.einsum('btsh,bshp->bthp', jnp.einsum('bthn,bshn->btsh', ch, bh) * seg, xdt)
             + jnp.exp(s)[..., None] * jnp.einsum('bthn,bhpn->bthp', ch, h))
        return h_new, y

    xs = (to_chunks(x, 1, L), to_chunks(dt, 1, L), to_chunks(bm, 1, L), to_chunks(cm, 1, L))
    state, y = lax.scan(step, state, xs)
    return (from_chunks(y, 1) if emit else None), state

def ssd_prep(xbc_pre, dt_pre, conv_w, conv_b, dt_bias):
    bsz, t = xbc_pre.shape[:2]
    xbc = jax.nn.silu(dwconv(xbc_pre, conv_w, conv_b)).astype(jnp.float32)
    xs, bm, cm = jnp.split(xbc, [S_WIDTH, S_WIDTH + S_GROUPS * S_STATE], axis=-1)
    dt = jax.nn.softplus(dt_pre.astype(jnp.float32).reshape(bsz, t, 2, S_HEADS) + dt_bias)
    return (xs.reshape(bsz, t, S_HEADS, S_HEAD_DIM), bm.reshape(bsz, t, S_GROUPS, S_STATE),
            cm.reshape(bsz, t, S_GROUPS, S_STATE), dt)

def ssd_out(y, xs, z, d_skip, norm_g):
    bsz, t = z.shape[:2]
    y = (y + d_skip.astype(jnp.float32)[:, None] * xs).reshape(bsz, t, S_WIDTH) * jax.nn.silu(z.astype(jnp.float32))
    y = rmsnorm(y.reshape(bsz, t, S_GROUPS, S_WIDTH // S_GROUPS), norm_g.reshape(S_GROUPS, S_WIDTH // S_GROUPS))
    return y.reshape(bsz, t, S_WIDTH).astype(z.dtype)

def ssd_mixer(z, xbc_pre, dt_pre, zc, xbcc_pre, dtc_pre, conv_w, conv_b, dt_bias, a_log, d_skip, norm_g, emit_ctx):
    a_coef = -jnp.exp(a_log.astype(jnp.float32))
    x, bm, cm, dt = ssd_prep(xbc_pre, dt_pre, conv_w, conv_b, dt_bias)
    xc, bc, cc, dtc = ssd_prep(xbcc_pre, dtc_pre, conv_w, conv_b, dt_bias)
    zeros = jnp.zeros((x.shape[0], S_HEADS, S_HEAD_DIM, S_STATE), jnp.float32)
    y_lat, y_ctx = 0.0, 0.0
    for d in range(2):
        yc, st = ssd_scan(rev(xc, 1, d), rev(dtc[:, :, d], 1, d), a_coef[d], rev(bc, 1, d), rev(cc, 1, d), zeros, emit_ctx)
        yl, _ = ssd_scan(rev(x, 1, d), rev(dt[:, :, d], 1, d), a_coef[d], rev(bm, 1, d), rev(cm, 1, d), st, True)
        y_lat = y_lat + rev(yl, 1, d)
        if emit_ctx:
            y_ctx = y_ctx + rev(yc, 1, d)
    out_l = ssd_out(y_lat, x, z, d_skip, norm_g)
    out_c = ssd_out(y_ctx, xc, zc, d_skip, norm_g) if emit_ctx else None
    return out_l, out_c

def gated_merge(y_m, y_a, y_s, gate_pre, w_m, w_a, w_s, w_o):
    g_m, g_a, g_s = jnp.split(jax.nn.sigmoid(gate_pre), N_BRANCH_2, axis=-1)
    return (g_m * (y_m @ w_m) + g_a * (y_a @ w_a) + g_s * (y_s @ w_s)) @ w_o

def conv_ffn(h, w_up, conv_w, w_down):
    a, g = jnp.split(dwconv(h @ w_up, conv_w), 2, axis=-1)
    return (jax.nn.silu(g) * a) @ w_down

def second_inputs(seed: int = 0) -> dict:
    key = jax.random.key(seed)
    ks = jax.random.split(key, 32)
    f32 = jnp.float32

    def nrm(i, shape, scale):
        return scale * jax.random.normal(ks[i], shape, f32)

    def gain(i, shape):
        return 1.0 + nrm(i, shape, 0.05)

    dt0 = jnp.exp(jax.random.uniform(ks[20], (DEPTH, 2, S_HEADS), f32, math.log(1e-3), math.log(1e-1)))
    return {
        "x": nrm(0, (BATCH, SEQ, D_MODEL), 1.0),
        "c": nrm(1, (BATCH, D_MODEL), 1.0),
        "ctx": nrm(2, (BATCH, CTX_LEN, D_MODEL), 1.0),
        "c_ctx": nrm(3, (D_MODEL,), 1.0),
        "w_mod": nrm(4, (DEPTH, D_MODEL, N_MOD * D_MODEL), 0.5 * D_MODEL ** -0.5),
        "b_mod": nrm(5, (DEPTH, N_MOD * D_MODEL), 0.02),
        "norm1_g": gain(6, (DEPTH, D_MODEL)),
        "norm2_g": gain(7, (DEPTH, D_MODEL)),
        "w_in": nrm(8, (DEPTH, D_MODEL, D_IN), D_MODEL ** -0.5),
        "m_conv_w": nrm(9, (DEPTH, CONV_W, 2 * M_WIDTH), CONV_W ** -0.5),
        "m_conv_b": nrm(10, (DEPTH, 2 * M_WIDTH), 0.02),
        "m_igate_b": nrm(11, (DEPTH, 2, M_HEADS), 0.1),
        "m_fgate_b": jnp.linspace(3.0, 6.0, M_HEADS, dtype=f32) + nrm(12, (DEPTH, 2, M_HEADS), 0.1),
        "m_norm_g": gain(13, (DEPTH, M_WIDTH)),
        "a_qnorm_g": gain(14, (DEPTH, A_SUB_DIM)),
        "a_knorm_g": gain(15, (DEPTH, A_SUB_DIM)),
        "a_lambda": nrm(16, (DEPTH, 4, A_SUB_DIM), 0.1),
        "a_subln_g": gain(17, (DEPTH, A_V_DIM)),
        "s_conv_w": nrm(18, (DEPTH, CONV_W, S_CONV_DIM), CONV_W ** -0.5),
        "s_conv_b": nrm(19, (DEPTH, S_CONV_DIM), 0.02),
        "s_dt_bias": dt0 + jnp.log(-jnp.expm1(-dt0)),
        "s_a_log": jnp.log(jax.random.uniform(ks[21], (DEPTH, 2, S_HEADS), f32, 1.0, 16.0)),
        "s_d": gain(22, (DEPTH, S_HEADS)),
        "s_norm_g": gain(23, (DEPTH, S_WIDTH)),
        "w_branch_m": nrm(24, (DEPTH, M_WIDTH, D_MODEL), M_WIDTH ** -0.5),
        "w_branch_a": nrm(25, (DEPTH, A_WIDTH, D_MODEL), A_WIDTH ** -0.5),
        "w_branch_s": nrm(26, (DEPTH, S_WIDTH, D_MODEL), S_WIDTH ** -0.5),
        "w_out": nrm(27, (DEPTH, D_MODEL, D_MODEL), D_MODEL ** -0.5),
        "w_up": nrm(28, (DEPTH, D_MODEL, 2 * D_FF), D_MODEL ** -0.5),
        "ffn_conv_w": nrm(29, (DEPTH, CONV_W, 2 * D_FF), CONV_W ** -0.5),
        "w_down": nrm(30, (DEPTH, D_FF, D_MODEL), D_FF ** -0.5),
    }

def second_block(x, c, ctx, c_ctx, w_mod, b_mod, norm1_g, norm2_g, w_in, m_conv_w, m_conv_b, m_igate_b, m_fgate_b,
              m_norm_g, a_qnorm_g, a_knorm_g, a_lambda, a_subln_g, s_conv_w, s_conv_b, s_dt_bias, s_a_log, s_d,
              s_norm_g, w_branch_m, w_branch_a, w_branch_s, w_out, w_up, ffn_conv_w, w_down):
    t = x.shape[1]
    rows = t // GRID_W
    row = jnp.repeat(jnp.arange(rows), GRID_W)
    col = jnp.tile(jnp.arange(GRID_W), rows)
    inv_freq = ROPE_BASE ** (-jnp.arange(ROPE_FREQS, dtype=jnp.float32) / ROPE_FREQS)
    ang = jnp.stack([row, col], axis=-1).astype(jnp.float32)[..., None] * inv_freq
    cos, sin = jnp.cos(ang), jnp.sin(ang)
    split_pts = [int(p) for p in np.cumsum(IN_SPLITS_2)[:-1]]

    xc = ctx
    for l in range(DEPTH):
        emit = l < DEPTH - 1
        lam_init = 0.8 - 0.6 * math.exp(-0.3 * l)
        mod = jnp.split(jax.nn.silu(c) @ w_mod[l] + b_mod[l], N_MOD, axis=-1)
        modc = jnp.split(jax.nn.silu(c_ctx) @ w_mod[l] + b_mod[l], N_MOD, axis=-1)

        h = modulate(rmsnorm(x, norm1_g[l]), mod[0][:, None], mod[1][:, None])
        hc = modulate(rmsnorm(xc, norm1_g[l]), modc[0], modc[1])
        u = jnp.split(h @ w_in[l], split_pts, axis=-1)
        uc = jnp.split(hc @ w_in[l], split_pts, axis=-1)
        y_m, y_mc = mlstm_mixer(u[0:4], uc[0:4], m_conv_w[l], m_conv_b[l], m_igate_b[l], m_fgate_b[l], m_norm_g[l], emit)
        y_a, y_ac = diff_attention(u[4], u[5], u[6], uc[4], uc[5], uc[6], a_qnorm_g[l], a_knorm_g[l], a_lambda[l],
                                   a_subln_g[l], lam_init, cos, sin, emit)
        y_s, y_sc = ssd_mixer(u[7], u[8], u[9], uc[7], uc[8], uc[9], s_conv_w[l], s_conv_b[l], s_dt_bias[l],
                              s_a_log[l], s_d[l], s_norm_g[l], emit)
        x = x + mod[2][:, None] * gated_merge(y_m, y_a, y_s, u[10], w_branch_m[l], w_branch_a[l], w_branch_s[l], w_out[l])

        h2 = modulate(rmsnorm(x, norm2_g[l]), mod[3][:, None], mod[4][:, None])
        x = x + mod[5][:, None] * conv_ffn(h2, w_up[l], ffn_conv_w[l], w_down[l])

        if emit:
            xc = xc + modc[2] * gated_merge(y_mc, y_ac, y_sc, uc[10], w_branch_m[l], w_branch_a[l], w_branch_s[l], w_out[l])
            hc2 = modulate(rmsnorm(xc, norm2_g[l]), modc[3], modc[4])
            xc = xc + modc[5] * conv_ffn(hc2, w_up[l], ffn_conv_w[l], w_down[l])
    return x


def setup_inputs(seed=0):
    out = dict(first_inputs(seed))
    for name, value in second_inputs(seed + 1).items():
        if name != "x":
            out[name + "_2"] = value
    return out


def reference(
    x, positions, ffn1_pre_g, ffn1_post_g, ffn1_w_gate, ffn1_w_up, ffn1_w_down, mix_pre_g, w_in,
    b_gate, q_norm_g, w_uq, kv_norm_g, w_uk, w_uv, w_branch_a, w_branch_b, w_out, mix_post_g,
    ffn2_pre_g, ffn2_post_g, ffn2_w_gate, ffn2_w_up, ffn2_w_down, c_2, ctx_2, c_ctx_2, w_mod_2,
    b_mod_2, norm1_g_2, norm2_g_2, w_in_2, m_conv_w_2, m_conv_b_2, m_igate_b_2, m_fgate_b_2,
    m_norm_g_2, a_qnorm_g_2, a_knorm_g_2, a_lambda_2, a_subln_g_2, s_conv_w_2, s_conv_b_2,
    s_dt_bias_2, s_a_log_2, s_d_2, s_norm_g_2, w_branch_m_2, w_branch_a_2, w_branch_s_2,
    w_out_2, w_up_2, ffn_conv_w_2, w_down_2,
):
    x = first_block(
        x, positions, ffn1_pre_g, ffn1_post_g, ffn1_w_gate, ffn1_w_up, ffn1_w_down, mix_pre_g,
        w_in, b_gate, q_norm_g, w_uq, kv_norm_g, w_uk, w_uv, w_branch_a, w_branch_b, w_out,
        mix_post_g, ffn2_pre_g, ffn2_post_g, ffn2_w_gate, ffn2_w_up, ffn2_w_down,
    )
    return second_block(
        x, c_2, ctx_2, c_ctx_2, w_mod_2, b_mod_2, norm1_g_2, norm2_g_2, w_in_2, m_conv_w_2,
        m_conv_b_2, m_igate_b_2, m_fgate_b_2, m_norm_g_2, a_qnorm_g_2, a_knorm_g_2, a_lambda_2,
        a_subln_g_2, s_conv_w_2, s_conv_b_2, s_dt_bias_2, s_a_log_2, s_d_2, s_norm_g_2,
        w_branch_m_2, w_branch_a_2, w_branch_s_2, w_out_2, w_up_2, ffn_conv_w_2, w_down_2,
    )


_drawn_inputs = setup_inputs


def setup_inputs(seed=0):
    import zlib

    import numpy as np

    out = dict(_drawn_inputs(seed))
    spreads = {}
    factors = {'ffn2_post_g': 3.69,
     'b_mod_2': 3.35,
     'norm1_g_2': 6.407,
     'norm2_g_2': 5.452,
     'm_conv_w_2': 3.408,
     'm_conv_b_2': 200.0,
     'm_igate_b_2': 200.0,
     'm_fgate_b_2': 2.906,
     'm_norm_g_2': 21.651,
     'a_qnorm_g_2': 8.0,
     'a_knorm_g_2': 8.0,
     'a_lambda_2': 8.0,
     'a_subln_g_2': 22.159,
     's_conv_b_2': 25.104,
     's_d_2': 200.0,
     's_norm_g_2': 8.0}
    for name, (base, spread) in spreads.items():
        noise = np.random.default_rng([zlib.crc32(name.encode()), seed]).standard_normal(out[name].shape)
        drawn = base * np.exp(spread * noise) if base else spread * noise
        out[name] = __import__('jax').numpy.asarray(drawn.astype(out[name].dtype))
    for name, factor in factors.items():
        out[name] = (out[name] * factor).astype(out[name].dtype)
    return out
```

```python
from contextlib import ExitStack

import numpy as np

import concourse.bass as bass
from concourse import mybir

F32 = mybir.dt.float32
F32R = mybir.dt.float32r
I32 = mybir.dt.int32
ALU = mybir.AluOpType
ACT = mybir.ActivationFunctionType
AX_X = mybir.AxisListType.X

P = 128
T = 256
TT = 2 * T
D = 1024
DC = D // P
FF = 2816
FC = FF // P
TILE = 1024
RING = 6
EPS = 1e-6
NEG = -1e30
HEADS = 8
Q_RANK, KV_RANK, NOPE, ROPE_D = 384, 256, 64, 32
SCALE_MLA = float(NOPE + ROPE_D) ** -0.5
SCALE_64 = 64.0 ** -0.5
SCALE_M = 128.0 ** -0.5
LAM_INIT = 0.8 - 0.6
CHUNK = 64
TWO_PI = 2.0 * np.pi
MAGIC = 12582912.0


def weight_order():
    order = []

    def ffn(gate, up, down):
        order.extend([(gate, "cols", 0), (up, "cols", 0), (gate, "cols", 1), (up, "cols", 1)])
        for f in range(2, FC):
            order.extend([(down, "down", f - 2), (gate, "cols", f), (up, "cols", f)])
        order.extend([(down, "down", FC - 2), (down, "down", FC - 1)])

    ffn("gate1", "up1", "down1")
    order.extend(("mod", "cols", n) for n in range(18))
    order.extend(("cq", "cols", n) for n in range(3))
    order.extend(("ckv", "cols", n) for n in range(2))
    order.extend(("dq", "cols", n) for n in range(4))
    order.extend(("dk", "cols", n) for n in range(4))
    order.extend(("dv", "wide", n) for n in range(4))
    order.extend([("uk", "small", 0), ("uv", "small", 0)])
    order.extend(("g1", "cols", n) for n in range(16))
    for n in range(4):
        order.extend([("wa", "pair", n), ("wb", "pair", n)])
    order.extend(("out1", "cols", n) for n in range(8))
    order.extend(("mod", "cols", n) for n in range(18, 36))
    ffn("gate2", "up2", "down2")
    order.extend(("mod", "cols", n) for n in range(36, 48))
    order.append(("rows", "cols", 0))
    order.extend(("mk", "cols", n) for n in range(4))
    order.extend(("mq", "cols", n) for n in range(4))
    order.extend(("mv", "wide", n) for n in range(4))
    order.extend(("mo", "cols", n) for n in range(4))
    order.extend(("sx", "cols", n) for n in range(4))
    order.extend(("sb", "cols", n) for n in range(2))
    order.extend(("sc", "cols", n) for n in range(2))
    order.extend(("sz", "cols", n) for n in range(4))
    order.extend(("g2", "cols", n) for n in range(8))
    order.extend(("g2", "cols", n) for n in range(8, 16))
    order.extend(("aq", "cols", n) for n in range(4))
    order.extend(("ak", "cols", n) for n in range(4))
    order.extend(("av", "wide", n) for n in range(4))
    order.extend(("g2", "cols", n) for n in range(16, 24))
    for n in range(4):
        order.extend([("wm", "pair", n), ("wat", "pair", n), ("ws", "pair", n)])
    order.extend(("out2", "cols", n) for n in range(8))
    ffn("gate3", "up3", "down3")
    return order


ORDER = weight_order()
NT = len(ORDER)
AT = {(m, n): t for t, (m, _, n) in enumerate(ORDER)}


def columns(names):
    at, n = {}, 0
    for name, width in names:
        at[name] = n
        n += width
    return at, n


VEC, NVEC = columns([
    ("ffn1_pre", 8), ("ffn1_post", 8), ("mix_pre", 8), ("mix_post", 8), ("ffn2_pre", 8), ("ffn2_post", 8),
    ("bgate", 16), ("q_norm", 3), ("kv_norm", 2), ("norm1", 8), ("norm2", 8), ("bmod", 48),
    ("mconv", 24), ("mconv_b", 8), ("mnorm", 4), ("aqn", 1), ("akn", 1), ("subln", 1),
    ("sconv", 24), ("sconv_b", 8), ("sskip", 4), ("snorm", 4), ("fconv", 3 * 2 * FC),
    ("row_bias", 1), ("row_ibias", 1), ("row_alog", 1), ("cond", 16)])

CST, NCST = columns([
    ("ident", P), ("rot_mla", ROPE_D), ("rot_dil", P), ("rot_att", P), ("cos_att", T), ("sin_att", T),
    ("freq", 2), ("dil_bias", 2 * T), ("sign", 1), ("reset", T), ("sel_k", 32), ("sel_kt", 4 * P), ("half", 2)])

ROW_F = (0, 32)
ROW_I = (16, 48)
ROW_DT = (64, 96)


def table_constants():
    c = np.zeros((P, NCST), np.float32)
    put = lambda name, a: c.__setitem__((slice(0, a.shape[0]), slice(CST[name], CST[name] + a.shape[1])), a)
    put("ident", np.eye(P, dtype=np.float32))
    r = np.zeros((P, ROPE_D), np.float32)
    half = ROPE_D // 2
    for m in range(half):
        r[64 + m + half, m] = -1.0
        r[64 + m, m + half] = 1.0
    put("rot_mla", r)
    r = np.zeros((P, P), np.float32)
    for base in (0, 64):
        for m in range(8):
            r[base + m + 8, base + m] = -1.0
            r[base + m, base + m + 8] = 1.0
    put("rot_dil", r)
    r = np.zeros((P, P), np.float32)
    for base in range(0, P, 32):
        for m in range(16):
            r[base + m + 16, base + m] = -1.0
            r[base + m, base + m + 16] = 1.0
    put("rot_att", r)
    grid_w, freqs = 64, 16
    inv = (np.float32(10000.0) ** (-np.arange(freqs, dtype=np.float32) / freqs)).astype(np.float32)
    t = np.arange(T)
    place = np.stack([t // grid_w, t % grid_w]).astype(np.float32)
    p = np.arange(P)
    ang = place[(p % 64) // 32][:, :] * inv[p % 16][:, None]
    put("cos_att", np.cos(ang).astype(np.float32))
    put("sin_att", np.sin(ang).astype(np.float32))
    f = np.zeros((P, 2), np.float32)
    inv_m = 1.0 / (10000.0 ** (np.arange(16) / 16.0))
    f[64:80, 0] = f[80:96, 0] = inv_m
    inv_d = 1.0 / (500000.0 ** (np.arange(8) / 8.0))
    for base in (0, 64):
        f[base:base + 8, 1] = f[base + 8:base + 16, 1] = inv_d
    put("freq", f)
    i = np.arange(T)[:, None]
    j = np.arange(T)[None, :]
    count = (abs(i - j) <= 64) * 1.0 + ((i - j) % 4 == 0) * (abs(i - j) <= 256) + ((i - j) % 16 == 0)
    bias = np.where(count > 0, np.log(np.maximum(count, 1.0)), NEG).astype(np.float32)
    put("dil_bias", bias.reshape(2, P, T).transpose(1, 0, 2).reshape(P, 2 * T))
    s = np.ones((P, 1), np.float32)
    s[0:64] = -1.0
    put("sign", s)
    m = np.ones((P, T), np.float32)
    m[:96, 0::CHUNK] = 0.0
    m[96:, CHUNK - 1::CHUNK] = 0.0
    put("reset", m)
    k = np.zeros((P, 4, 8), np.float32)
    for n in range(4):
        for b in range(2):
            k[64 * b:64 * b + 64, n, 2 * n + b] = 1.0
    put("sel_k", k.reshape(P, 32))
    put("sel_kt", k.transpose(2, 1, 0).reshape(8, 4 * P))
    h = np.zeros((P, 2), np.float32)
    h[0:64, 0] = h[64:, 1] = 1.0
    put("half", h)
    return c


def regions(names, start=0):
    at, n = {}, start
    for name, width in names:
        at[name] = (n, width)
        n += width
    return at, n


MEM, END_COMMON = regions([
    ("ring", RING * TILE), ("h", DC * T), ("u", DC * TT), ("vec", NVEC), ("cst", NCST),
    ("hidden", 2 * T), ("silu", 2 * T), ("root", T), ("inv", T), ("ones", P), ("small", 448), ("modc", 96),
    ("scratch", 4096), ("gates", 24 * T)])
SPLIT_AT = MEM["gates"][0]
ARENA_1, END_1 = regions([
    ("cq", 768), ("ckv", 512), ("q", 2048), ("kh", 2048), ("qd", 1024), ("kd", 1024), ("va", 1024),
    ("vd", 1024), ("p", 1024), ("pt", 1024), ("oa", 1024), ("ob", 1024), ("merged1", 2048),
    ("tab", 1024), ("sb", 1024), ("rt", 512), ("kr", 256), ("wuq", 2304), ("wkr", 256)], END_COMMON)
ARENA_2, END_2 = regions([
    ("mq", 1024), ("mk", 2048), ("mv", 2048), ("mo", 1024), ("mst", 1536), ("ym", 1024),
    ("sx", 2048), ("sB", 1024), ("sC", 512), ("sz", 1024), ("ys", 1024), ("xdt", 4096), ("sg", 3072),
    ("t0", 512), ("tc", 1024), ("rowm", 512), ("rowl", 256)], END_COMMON)
ATT, _ = regions([("aq", 1024), ("ak", 2048), ("av", 2048), ("mo", 1024), ("ya", 1024)], ARENA_2["mq"][0])
ROWS, END_ROWS = regions([
    ("raw", 512), ("z", 512), ("sp", 512), ("da", 512), ("b", 512), ("m", 512), ("r0", 512),
    ("colr", 2048)], ARENA_2["xdt"][0])

PARTS, END_PARTS = regions([("ring_hi", RING * TILE), ("ring_lo", RING * TILE), ("u_hi", DC * T), ("u_lo", DC * T),
                            ("hidden_hi", 2 * T), ("hidden_lo", 2 * T)], 0)
assert SPLIT_AT + END_PARTS <= min(ARENA_1["tab"][0], ARENA_2["sz"][0])


NORMS = ["ffn1_pre", "ffn1_post", "mix_pre", "q_norm", "kv_norm", "mix_post", "ffn2_pre", "ffn2_post",
         "ctx", "norm1", "norm2"]
NORM_AT = {name: i for i, name in enumerate(NORMS)}
SQUARES = {"q_norm": 3, "kv_norm": 2}
SQ_BASE = {name: sum(SQUARES.get(m, 4) for m in NORMS[:i]) for i, name in enumerate(NORMS)}
SCALED = ["ffn1_pre", "mix_pre", "ffn2_pre", "norm2"]
POSTS = ["ffn1_post", "mix_post", "ffn2_post"]
FFNS = ["1", "2", "3"]

BANKED = ([f"cq{n}" for n in range(3)] + [f"ckv{n}" for n in range(2)] + ["kr"]
          + [f"dq{n}" for n in range(4)] + [f"dk{n}" for n in range(4)]
          + ["rdq0", "rdq1", "rdk0", "rdk1"] + [f"uk{n}" for n in range(4)] + [f"uq{n}" for n in range(4)]
          + [f"ruq{n}" for n in range(4)] + ["rkr"] + [f"g1_{n}" for n in range(16)]
          + [f"m1_{n}" for n in range(8)]
          + ["rows"] + [f"mk{n}" for n in range(4)] + [f"mq{n}" for n in range(4)] + ["ish"]
          + [f"mo{n}" for n in range(4)] + [f"sx{n}" for n in range(4)] + [f"sb{n}" for n in range(2)]
          + [f"sc{n}" for n in range(2)] + [f"sz{n}" for n in range(4)] + [f"g2_{n}" for n in range(16)]
          + [f"aq{n}" for n in range(4)] + [f"ak{n}" for n in range(4)]
          + ["krow", "rq", "g2_16", "kb0", "kb1", "kb2", "kb3", "raq0", "raq1", "rak0", "rak1"]
          + [f"g2_{n}" for n in range(17, 24)]
          + [f"m2_{n}{s}" for n in range(8) for s in "ab"])
BANK_AT = {name: i for i, name in enumerate(BANKED)}
SMALL = ["kr", "rdq0", "rdq1", "rdk0", "rdk1", "uk0", "uk1", "uk2"] + [f"uq{n}" for n in range(4)] + [
    f"ruq{n}" for n in range(4)] + ["rkr"] + [f"m1_{n}" for n in (0, 2, 4, 6)] + [
    "ish", "krow", "rq", "kb0", "kb1", "kb2", "kb3", "raq0", "raq1", "rak0", "rak1"] + [
    f"m2_{n}a" for n in range(0, 8)] + [f"m2_{n}b" for n in (0, 2, 4, 6)]
SMALL.sort(key=lambda n: BANK_AT[n])
SMALL_AT = {name: i for i, name in enumerate(SMALL)}
CONV = ([("mk", n, 4 + n) for n in range(4)] + [("mq", n, n) for n in range(4)]
        + [("sx", n, n) for n in range(4)] + [("sb", n, 4 + n) for n in range(2)]
        + [("sc", n, 6 + n) for n in range(2)])


def tile_of(name):
    for m in ("g1_", "g2_"):
        if name.startswith(m):
            return AT[(m[:2], int(name[3:]))]
    if name == "uk3":
        return AT[("uk", 0)]
    if name.startswith("m1_"):
        return AT[("wb", int(name[3:]) // 2)]
    if name.startswith("m2_"):
        return AT[("ws", int(name[3]) // 2)]
    if name == "rows":
        return AT[("rows", 0)]
    return AT[(name.rstrip("0123456789"), int(name[len(name.rstrip("0123456789")):]))]


def two_blocks(nc, dram):
    with ExitStack() as ctx:
        start = -(-nc.sbuf_base // 32) * 32
        low = ctx.enter_context(nc.sbuf_tensor("low", [P, SPLIT_AT], F32))
        high = ctx.enter_context(nc.sbuf_tensor("high", [P, END_2 - SPLIT_AT], F32))
        parts = nc.alloc_sbuf_tensor_at("parts", [P, END_PARTS], F32R, offset=start + 4 * SPLIT_AT)
        psum = ctx.enter_context(nc.psum_tensor("psum", [P, 8, 512], F32))
        sems = {}

        def S(name):
            if name not in sems:
                sems[name] = ctx.enter_context(nc.semaphore(name))
            return sems[name]

        def place(at, width):
            if at < SPLIT_AT:
                return low[:, at:at + width]
            return high[:, at - SPLIT_AT:at - SPLIT_AT + width]

        def view(table, name, n=None, m=None):
            at, width = table[name]
            v = place(at, width)
            if m is not None:
                return v.rearrange("p (a b c) -> p a b c", a=n, b=m)
            return v if n is None else v.rearrange("p (a b) -> p a b", a=n)

        ring = view(MEM, "ring", RING)
        h = view(MEM, "h", DC)
        u1 = place(MEM["u"][0], DC * T).rearrange("p (a b) -> p a b", a=DC)
        u2 = view(MEM, "u", DC)
        vec = view(MEM, "vec")
        cst = view(MEM, "cst")
        gates = view(MEM, "gates", 24)
        ctx_raw = place(ARENA_2["sz"][0], DC * T).rearrange("p (a b) -> p a b", a=DC)
        hidden = view(MEM, "hidden", 2)
        silu = view(MEM, "silu", 2)
        ring_hi, ring_lo, u_hi, u_lo, hidden_hi, hidden_lo = (
            parts[:, a:a + width].rearrange("p (a b) -> p a b", a=n)
            for (a, width), n in zip(PARTS.values(), (RING, RING, DC, DC, 2, 2)))
        root = view(MEM, "root")
        inv = view(MEM, "inv")
        ones = view(MEM, "ones")
        small = view(MEM, "small")
        modc = view(MEM, "modc", 48)
        sq = place(MEM["scratch"][0], 2048).rearrange("p (a b) -> p a b", a=DC)
        tmp = place(MEM["scratch"][0] + 2048, 2048).rearrange("p (a b) -> p a b", a=DC)
        cond = small[:, 0:16].rearrange("p (c b) -> p c b", b=2)
        bhalf = small[:, 16:32]
        negmax = small[:, 32:48]
        den = small[:, 48:64]
        rden = small[:, 64:80]
        gmod = small[:, 80:104]
        row_bias = small[:, 104:105]
        row_coef = small[:, 105:106]
        lam = small[:, 106:112]
        g_half = small[:, 112:116]
        g_sub = small[:, 116:117]
        rq = small[:, 120:136]
        dmax = small[:, 136:144]
        bh2 = small[:, 160:184]
        mhalf = small[:, 144:152]
        lam_p = small[:, 184:440]
        eps = small[:, 440:441]
        row_exp = small[:, 441:442]
        ident = cst[:, CST["ident"]:CST["ident"] + P]

        def c(name, width, a=0, b=P):
            return cst[a:b, CST[name]:CST[name] + width]

        def v(name, i=0, a=0, b=P):
            return vec[a:b, VEC[name] + i:VEC[name] + i + 1]

        def half_bank(b, n):
            return psum[:, b, n * T:(n + 1) * T]

        acc = [half_bank(n // 2, n % 2) for n in range(DC)]
        PJ = (4, 5)
        SUMS, MOD = 6, 7

        A1 = lambda name, *n: view(ARENA_1, name, *n)
        A2 = lambda name, *n: view(ARENA_2, name, *n)
        cq, ckv, kr = A1("cq", 3), A1("ckv", 2), A1("kr")
        wuq, wkr = A1("wuq", 3), A1("wkr", 8)
        q, kh, qd, kd = A1("q", 8), A1("kh", 8), A1("qd", 4), A1("kd", 4)
        va, vd = A1("va", 2), A1("vd", 2)
        prob, probt = A1("p", 2, 2), A1("pt", 2, 2)
        oa, ob, tab, sbias, rt = A1("oa", 4), A1("ob", 4), A1("tab", 4), A1("sb", 2, 2), A1("rt")
        merged1 = A1("merged1", 8)
        merged2 = tmp
        mq, mk, mv, mo = A2("mq", 4), A2("mk", 4), A2("mv", 4), A2("mo", 4)
        mst, ym = A2("mst", 6), A2("ym", 4)
        sx, sB, sC, sz, ys = A2("sx", 4), A2("sB", 2), A2("sC", 2), A2("sz", 4), A2("ys", 4)
        xdt = A2("xdt").rearrange("p (d s f) -> p d s f", d=2, s=4)
        sg = A2("sg").rearrange("p (g s t) -> p g s t", g=2, s=6)
        t0, tc = A2("t0", 4), A2("tc").rearrange("p (j s r) -> p j s r", j=4, s=4)
        rowm, rowl = A2("rowm", 2), A2("rowl")
        conv_dst = {"mk": mk, "mq": mq, "sx": sx, "sb": sB, "sc": sC}
        aq, ak, av, ya = (view(ATT, n, 4) for n in ("aq", "ak", "av", "ya"))
        raw, z, sp, da, bsum, mrow, r0 = (view(ROWS, n) for n in ("raw", "z", "sp", "da", "b", "m", "r0"))
        colr = view(ROWS, "colr", 4)
        sc0 = MEM["scratch"][0]
        arg = low[:, sc0:sc0 + 2048].rearrange("p (x s t) -> p x s t", x=2, s=4)
        wgt = low[:, sc0 + 2048:sc0 + 4096].rearrange("p (x s t) -> p x s t", x=2, s=4)
        prob2 = low[:, sc0:sc0 + 2048].rearrange("p (x b k) -> p x b k", x=2, b=2)
        probt2 = low[:, sc0 + 2048:sc0 + 3072].rearrange("p (x s t) -> p x s t", x=2, s=4)
        sqa = low[:, sc0:sc0 + 2048].rearrange("p (a b) -> p a b", a=4)
        sqq = low[:, sc0 + 2048:sc0 + 3072].rearrange("p (a b) -> p a b", a=4)
        krow_r = low[0:8, sc0 + 3072:sc0 + 3584]
        krow_i = low[0:8, sc0 + 3584:sc0 + 4096]
        pos_i = A1("kr").bitcast(I32)
        ang = A1("sb", 2, 2)
        posf = rt[:, 0:T]
        cg, ca = (place(ARENA_2["sz"][0] + n * TT, TT).rearrange("p (a b) -> p a b", a=2)
                  for n in range(2))

        def bank_free(eng, name):
            i = BANK_AT[name]
            if i >= 2:
                eng.wait_ge(S(f"bank{i % 2}_read"), i // 2)

        def product_ready(eng, name):
            if name in SMALL_AT:
                eng.wait_ge(S("small_products"), SMALL_AT[name] + 1)
            else:
                eng.wait_ge(S("tiles_used"), tile_of(name) + 1)

        def evacuated(eng, *names):
            for name in names:
                i = BANK_AT[name]
                eng.wait_ge(S(f"bank{i % 2}_read"), i // 2 + 1)

        def bank(name):
            return psum[:, PJ[BANK_AT[name] % 2], :]

        def read_done(name):
            return S(f"bank{BANK_AT[name] % 2}_read")

        block = ctx.enter_context(nc.Block())

        @block.sync
        def _(sp_):
            sp_.dma_start(h, dram["x"]).then_inc(S("x_loaded"), 16)
            for s in range(RING):
                sp_.dma_start(ring[:, s, :], dram["stream"][s]).then_inc(S(f"slot{s}_loaded"), 16)
            with sp_.Fori(1, NT // RING) as i:
                for s in range(RING):
                    sp_.wait_ge(S("tiles_used"), (i - 1) * RING + s + 1)
                    sp_.dma_start(ring[:, s, :], dram["stream"][bass.ds(i * RING + s, 1)].rearrange("a p n -> (a p) n"))\
                       .then_inc(S(f"slot{s}_loaded"), 16)
            for t in range(NT // RING * RING, NT):
                sp_.wait_ge(S("tiles_used"), t - RING + 1)
                sp_.dma_start(ring[:, t % RING, :], dram["stream"][t]).then_inc(S(f"slot{t % RING}_loaded"), 16)
            for n in range(DC):
                sp_.wait_ge(S("result_ready"), n + 1)
                sp_.dma_start(dram["out"][n], h[:, n, :]).then_inc(S("stored"), 16)
            sp_.wait_ge(S("stored"), 16 * DC)

        @block.tensor
        def _(pe):
            def tile_wait(t, more=0):
                pe.wait_ge(S(f"slot{t % RING}_loaded"), more * 16 + 16 * (t // RING + 1))
                return ring[:, t % RING, :]

            def cols(t, out, rhs, more=0, chunk_ready=lambda k: None):
                w = tile_wait(t, more)
                for k in range(DC):
                    chunk_ready(k)
                    mm = pe.matmul(out, w[:, k * P:(k + 1) * P], rhs(k), start=k == 0, stop=k == DC - 1)
                mm.then_inc(S("tiles_used"), 1)

            def split_tile(k, j, more=0):
                pe.wait_ge(S("lower_ready"), more * RING + (3 * FC * k + j + 1))
                return ring_hi[:, j % RING, :], ring_lo[:, j % RING, :]

            def split_product(out, w, cols_, x, start, stop, **kw):
                (w_hi, w_lo), (x_hi, x_lo) = w, x
                pe.matmul(out, w_hi[:, cols_], x_hi, start=start, stop=False, **kw)
                pe.matmul(out, w_hi[:, cols_], x_lo, start=False, stop=False, **kw)
                return pe.matmul(out, w_lo[:, cols_], x_hi, start=False, stop=stop, **kw)

            def sums(name, chunk, n):
                i = NORM_AT[name]
                if i:
                    pe.wait_ge(S("roots"), i)
                for k in range(n):
                    step = k if name in SQUARES else k // 2
                    pe.wait_ge(S("squares"), SQ_BASE[name] + step + 1)
                    mm = pe.matmul(half_bank(SUMS, 0), ones, chunk(k), start=k == 0, stop=k == n - 1)
                mm.then_inc(S("sums"), 1)

            def sums_wide(name):
                sums(name, lambda k: sq[:, k, :], DC)

            def ffn(k):
                base = FC * k

                def gate_up(par, t, more=0, hid=None):
                    if hid is not None:
                        pe.wait_ge(S("hidden_ready"), hid)
                    for a in range(2):
                        w = split_tile(k, t + a, more)
                        for c_ in range(DC):
                            if t < 2:
                                pe.wait_ge(S("input_split"), DC * k + c_ + 1)
                            mm = split_product(half_bank(PJ[par], a), w, slice(c_ * P, (c_ + 1) * P),
                                               (u_hi[:, c_, :], u_lo[:, c_, :]),
                                               c_ == 0, c_ == DC - 1)
                        mm.then_inc(S("tiles_used"), 1)

                def down(par, t, hid, first, last, more=0):
                    w = split_tile(k, t, more)
                    pe.wait_ge(S("hidden_split"), hid)
                    for n in range(DC):
                        mm = split_product(acc[n], w, slice(n * P, (n + 1) * P),
                                           (hidden_hi[:, par, :], hidden_lo[:, par, :]),
                                           first and n % 2 == 0, last, skip_group_check=True)
                    mm.then_inc(S("tiles_used"), 1)

                for par in range(2):
                    gate_up(par, 2 * par)
                if k == 1:
                    pe.wait_ge(S("residual"), 16)
                if k == 2:
                    pe.wait_ge(S("added"), 8)
                down(0, 4, base + 1, True, False)
                gate_up(0, 5, hid=base + 1)
                down(1, 7, base + 2, False, False)
                gate_up(1, 8, hid=base + 2)
                with pe.Fori(1, FC // 2 - 1) as i:
                    down(0, 4, i * 2 + (base + 1), False, False, i)
                    gate_up(0, 5, i, i * 2 + (base + 1))
                    down(1, 7, i * 2 + (base + 2), False, False, i)
                    gate_up(1, 8, i, i * 2 + (base + 2))
                down(0, 3 * FC - 2, base + FC - 1, False, False)
                down(1, 3 * FC - 1, base + FC, False, True)

            def modulation(n0, n1, group):
                if group == 0:
                    pe.wait_ge(S("cond_ready"), 1)
                else:
                    pe.wait_ge(S("mod_ready"), group)
                if group == 1:
                    pe.wait_ge(S("outs_copied"), 16)
                t = AT[("mod", n0)]
                with pe.Fori(0, (n1 - n0) // RING) as i:
                    for s in range(RING):
                        cols(t + s, psum[:, MOD, bass.ds(i * (2 * RING) + 2 * (n0 + s), 2)],
                             lambda k: cond[:, k, :], i)

            def wide(name, toks, lhs, banks):
                for kk in range(4):
                    w = tile_wait(AT[(name, kk)])
                    for n in range(toks):
                        for j in range(2):
                            mm = pe.matmul(psum[:, banks[n], :], lhs(2 * kk + j, n), w[:, j * 512:(j + 1) * 512],
                                           start=kk + j == 0, stop=kk + j == 4)
                    mm.then_inc(S("tiles_used"), 1)

            pe.wait_ge(S("ones_ready"), 1)
            sums_wide("ffn1_pre")
            ffn(0)
            sums_wide("ffn1_post")
            pe.wait_ge(S("tables_loaded"), 64)
            modulation(0, 18, 0)
            sums_wide("mix_pre")

            u1k = lambda k: u1[:, k, :]

            def project(name, out=None, rhs=u1k, **kw):
                bank_free(pe, name)
                cols(tile_of(name), bank(name)[:, 0:T] if out is None else out, rhs, **kw)

            for n in range(3):
                project(f"cq{n}", chunk_ready=lambda k: pe.wait_ge(S("scaled"), DC + k + 1))
            for n in range(2):
                project(f"ckv{n}")
            bank_free(pe, "kr")
            pe.wait_ge(S("small_weights"), 32)
            for k in range(DC):
                mm = pe.matmul(bank("kr")[64:96, 0:T], wkr[:, k, :], u1[:, k, :], start=k == 0, stop=k == DC - 1)
            mm.then_inc(S("small_products"), 1)
            sums("q_norm", lambda k: sq[:, k, :], 3)
            for n in range(4):
                project(f"dq{n}")
            sums("kv_norm", lambda k: sq[:, 3 + k, :], 2)
            for n in range(4):
                project(f"dk{n}")
            pe.wait_ge(S("residual"), 8)
            wide("dv", 2, lambda k, n: u1[:, k, n * P:(n + 1) * P], (0, 1))
            for n, (x, name) in enumerate([(qd, "rdq0"), (qd, "rdq1"), (kd, "rdk0"), (kd, "rdk1")]):
                bank_free(pe, name)
                evacuated(pe, *(f"{name[1:3]}{2 * (n % 2) + a}" for a in range(2)))
                pe.matmul(bank(name), c("rot_dil", P), x[:, 2 * (n % 2):2 * (n % 2) + 2, :],
                          start=True, stop=True).then_inc(S("small_products"), 1)
            w = tile_wait(AT[("uk", 0)])
            pe.wait_ge(S("kv_scaled"), 2)
            for n in range(4):
                bank_free(pe, f"uk{n}")
                for a in range(2):
                    hd = 2 * n + a
                    for k in range(2):
                        mm = pe.matmul(bank(f"uk{n}")[0:64, a * T:(a + 1) * T],
                                       w[:, k * 512 + hd * 64:k * 512 + (hd + 1) * 64], ckv[:, k, :],
                                       start=k == 0, stop=k == 1)
                mm.then_inc(S("tiles_used" if n == 3 else "small_products"), 1)
            w = tile_wait(AT[("uv", 0)])
            for n in range(2):
                for k in range(2):
                    mm = pe.matmul(psum[:, 2 + n, :], ckv[:, k, n * P:(n + 1) * P], w[:, k * 512:(k + 1) * 512],
                                   start=k == 0, stop=k == 1)
            mm.then_inc(S("tiles_used"), 1)
            pe.wait_ge(S("q_scaled"), 3)
            for n in range(4):
                bank_free(pe, f"uq{n}")
                for a in range(2):
                    hd = 2 * n + a
                    for k in range(3):
                        mm = pe.matmul(bank(f"uq{n}")[0:96, a * T:(a + 1) * T], wuq[:, k, hd * 96:(hd + 1) * 96],
                                       cq[:, k, :], start=k == 0, stop=k == 2)
                mm.then_inc(S("small_products"), 1)
            for n in range(4):
                bank_free(pe, f"ruq{n}")
                evacuated(pe, f"uq{n}")
                pe.matmul(bank(f"ruq{n}")[64:96, :], c("rot_mla", ROPE_D, 64, 96), q[64:96, 2 * n:2 * n + 2, :],
                          start=True, stop=True).then_inc(S("small_products"), 1)
            bank_free(pe, "rkr")
            pe.matmul(bank("rkr")[64:96, 0:T], c("rot_mla", ROPE_D, 64, 96), kr[64:96, :],
                      start=True, stop=True).then_inc(S("small_products"), 1)

            def scores(k):
                if k == 0:
                    pe.wait_ge(S("vd_copied"), 2)
                    pe.wait_ge(S("dil_roped"), 4)
                if k == 8:
                    pe.wait_ge(S("mla_roped"), 5)
                if k >= 2:
                    pe.wait_ge(S("exps"), 2 * (k - 1))
                for j in range(2):
                    if k < 8:
                        r = slice(64 * (k % 2), 64 * (k % 2) + 64)
                        a, b = qd[r, k // 2, j * P:(j + 1) * P], kd[r, k // 2, :]
                    else:
                        a, b = q[0:96, k - 8, j * P:(j + 1) * P], kh[0:96, k - 8, :]
                    mm = pe.matmul(psum[:, k % 2, j * T:(j + 1) * T], a, b, start=True, stop=True)
                mm.then_inc(S("scores"), 1)

            def turn(k):
                pe.wait_ge(S("probs"), 2 * k + 2)
                if k >= 2:
                    pe.wait_ge(S("turned_copied"), k - 1)
                else:
                    pe.wait_ge(S("va_copied"), 2)
                for s in range(2):
                    for j in range(2):
                        mm = pe.transpose(psum[:, 2 + k % 2, s * T + j * P:s * T + (j + 1) * P],
                                          prob[:, k % 2, j, s * P:(s + 1) * P], ident)
                mm.then_inc(S("turned"), 1)

            def values(k):
                pe.wait_ge(S("turned_copied"), k + 1)
                if k >= 2:
                    pe.wait_ge(S("outs_copied"), k - 1)
                elif k == 1:
                    pe.wait_ge(S("mod_ready"), 1)
                else:
                    pe.wait_ge(S("roots"), NORM_AT["kv_norm"] + 1)
                x, hd = (vd, k) if k < 8 else (va, k - 8)
                r = 64 * (k % 2)
                for s in range(2):
                    mm = pe.matmul(psum[r:r + 64, 6 + k % 2, 0:T], x[:, s, hd * 64:(hd + 1) * 64],
                                   probt[:, k % 2, s, :], start=s == 0, stop=s == 1)
                mm.then_inc(S("outs"), 1)

            scores(0)
            for k in range(16):
                if k < 15:
                    scores(k + 1)
                project(f"g1_{k}")
                turn(k)
                if k:
                    values(k - 1)
            values(15)

            for n in range(8):
                name = f"m1_{n}"
                bank_free(pe, name)
                for s, (m, o, last) in enumerate([("wa", oa, n % 2), ("wb", ob, n % 2)]):
                    w = tile_wait(AT[(m, n // 2)])
                    if n == 0 and s == 0:
                        pe.wait_ge(S("outs_copied"), 16)
                    for k in range(4):
                        mm = pe.matmul(bank(name)[:, s * T:(s + 1) * T],
                                       w[:, (n % 2 * 4 + k) * P:(n % 2 * 4 + k + 1) * P], o[:, k, :],
                                       start=k == 0, stop=k == 3)
                    if last:
                        mm.then_inc(S("tiles_used"), 1)
                if not n % 2:
                    mm.then_inc(S("small_products"), 1)
            pe.wait_ge(S("turned_copied"), 16)
            for n in range(8):
                pe.wait_ge(S("merged"), 8)
                cols(AT[("out1", n)], acc[n], lambda k: merged1[:, k, :])
            sums_wide("mix_post")
            modulation(18, 36, 1)
            sums_wide("ffn2_pre")

            ffn(1)
            sums_wide("ffn2_post")
            sums_wide("ctx")
            modulation(36, 48, 2)
            sums_wide("norm1")

            both = lambda k: u2[:, k, :]
            lat = lambda k: u2[:, k, T:TT]
            project("rows", bank("rows"), both, chunk_ready=lambda k: pe.wait_ge(S("modulated"), DC + k + 1))
            for n in range(4):
                project(f"mk{n}", bank(f"mk{n}"), both)
            for n in range(4):
                project(f"mq{n}", None, lat)
            bank_free(pe, "ish")
            evacuated(pe, "rows")
            pe.matmul(bank("ish")[0:64, :], ident[:, 16:80], raw[:, :], start=True, stop=True)\
              .then_inc(S("small_products"), 1)
            pe.wait_ge(S("residual"), 24)
            wide("mv", 4, lambda k, n: u2[:, k, n * P:(n + 1) * P], (0, 1, 2, 3))
            for n in range(4):
                project(f"mo{n}", None, lat)
            for n in range(4):
                project(f"sx{n}", bank(f"sx{n}"), both)
            for n in range(2):
                project(f"sb{n}", bank(f"sb{n}"), both)
            for n in range(2):
                project(f"sc{n}", None, lat)
            pe.wait_ge(S("mv_copied"), 4)
            pe.wait_ge(S("cols_in"), 1)
            for s in range(4):
                mm = pe.transpose(psum[:, 0, s * P:(s + 1) * P], r0[:, s * P:(s + 1) * P], ident)
            mm.then_inc(S("cols_turned"), 1)
            pe.wait_ge(S("cols_in"), 2)
            for j in range(4):
                for s in range(4):
                    i = 4 * j + s
                    mm = pe.transpose(psum[:, 1 + i // 8, i % 8 * 64:i % 8 * 64 + 64],
                                      colr[64:P, j, s * P:(s + 1) * P], ident[64:P, 64:P])
            mm.then_inc(S("cols_turned"), 1)
            for n in range(4):
                project(f"sz{n}", None, lat)

            def m_scores(hd):
                if hd == 0:
                    pe.wait_ge(S("conv_done"), 8)
                    pe.wait_ge(S("cols_copied"), 3)
                else:
                    pe.wait_ge(S("m_scores_copied"), hd)
                for s in range(4):
                    mm = pe.matmul(psum[:, 2 + s // 2, s % 2 * T:(s % 2 + 1) * T], mk[:, hd, s * P:(s + 1) * P],
                                   mq[:, hd, :], start=True, stop=True)
                mm.then_inc(S("m_scores"), 1)

            def m_rows(i):
                hd, d = i // 2, i % 2
                if i >= 2:
                    pe.wait_ge(S("m_floor"), i - 1)
                row = 32 * d + hd
                for x in range(2):
                    mm = pe.matmul(psum[:, i % 2, x * T:(x + 1) * T], ident[0:64, row:row + 1].broadcast_to([64, P]),
                                   rowm[0:64, x, :], start=True, stop=True)
                mm.then_inc(S("m_rows"), 1)

            def m_sums(i):
                hd, d = i // 2, i % 2
                pe.wait_ge(S("m_weights"), i + 1)
                if i >= 2:
                    pe.wait_ge(S("m_out"), i - 1)
                for x in range(2):
                    for s in range(4):
                        blk = (s + 2 * d) % 4
                        lhs = ones if x else mv[:, blk, hd * P:(hd + 1) * P]
                        mm = pe.matmul(psum[:, 6 + i % 2, x * T:(x + 1) * T], lhs, wgt[:, i % 2, s, :],
                                       start=s == 0, stop=s == 3)
                mm.then_inc(S("m_sums"), 1)

            m_scores(0)
            m_rows(0)
            for i in range(8):
                if i < 7:
                    m_rows(i + 1)
                if i % 2 == 1 and i < 7:
                    m_scores(i // 2 + 1)
                project(f"g2_{i}", None, lat)
                m_sums(i)

            pe.wait_ge(S("m_scores_copied"), 4)
            pe.wait_ge(S("conv_done"), 16)
            for g in range(2):
                if g:
                    pe.wait_ge(S("sg_copied"), 1)
                for s in range(4):
                    mm = pe.matmul(psum[:, 2 + s // 2, s % 2 * T:(s % 2 + 1) * T], sB[:, g, s * P:(s + 1) * P],
                                   sC[:, g, :], start=True, stop=True)
                mm.then_inc(S("sg_ready"), 1)
            pe.wait_ge(S("m_floor"), 8)
            for s in range(4):
                if s >= 2:
                    pe.wait_ge(S("xdt_ready"), 2 * (s - 1))
                for f in range(4):
                    mm = pe.transpose(psum[:, s % 2, f * P:(f + 1) * P], sx[:, f, s * P:(s + 1) * P], ident)
                mm.then_inc(S("x_turned"), 1)

            def s_rows(hd):
                if hd < 2:
                    pe.wait_ge(S("xdt_ready"), 8)
                else:
                    pe.wait_ge(S("s_args"), 2 * (hd - 1))
                for d in range(2):
                    row = 32 * d + hd
                    mm = pe.matmul(psum[:, hd % 2, d * T:(d + 1) * T],
                                   ident[64:P, 64 + row:65 + row].broadcast_to([64, P]), rowl[64:P, :],
                                   start=True, stop=True)
                mm.then_inc(S("s_rows"), 1)

            def s_sums(hd):
                r = 64 * (hd % 2)
                if hd >= 2:
                    pe.wait_ge(S("s_out"), hd - 1)
                else:
                    pe.wait_ge(S("m_out"), 7 + hd)
                for d in range(2):
                    pe.wait_ge(S("s_weights"), 2 * hd + d + 1)
                    for s in range(4):
                        blk = (s + 2 * d) % 4
                        mm = pe.matmul(psum[r:r + 64, 6 + hd % 2, 0:T], xdt[:, d, blk, hd * 64:(hd + 1) * 64],
                                       wgt[:, d, s, :], start=d == 0 and s == 0, stop=d == 1 and s == 3)
                mm.then_inc(S("s_sums"), 1)

            s_rows(0)
            for hd in range(8):
                if hd < 7:
                    s_rows(hd + 1)
                project(f"g2_{8 + hd}", None, lat)
                s_sums(hd)

            def memory_sums():
                pe.wait_ge(S("branch_squares"), 1)
                for hd in range(4):
                    mm = pe.matmul(psum[:, 2 + hd // 2, hd % 2 * T:(hd % 2 + 1) * T], ones, sq[:, hd, :],
                                   start=True, stop=True)
                mm.then_inc(S("branch_sums"), 1)

            def space_sums():
                pe.wait_ge(S("branch_squares"), 2)
                for f in range(4):
                    mm = pe.matmul(psum[:, 6, f // 2 * T:(f // 2 + 1) * T], ones, tmp[:, f, :],
                                   start=f % 2 == 0, stop=f % 2 == 1)
                mm.then_inc(S("branch_sums"), 1)

            for n in range(4):
                project(f"aq{n}", None, lat)
                if n == 1:
                    memory_sums()
                elif n == 2:
                    space_sums()
            for n in range(4):
                project(f"ak{n}", bank(f"ak{n}"), both)
            pe.wait_ge(S("s_args"), 16)
            pe.wait_ge(S("sg_copied"), 2)
            wide("av", 4, lambda k, n: u2[:, k, n * P:(n + 1) * P], (0, 1, 2, 3))
            bank_free(pe, "krow")
            pe.wait_ge(S("a_squares"), 2)
            for n in range(4):
                mm = pe.matmul(bank("krow")[0:8, :], c("sel_k", 32)[:, 8 * n:8 * n + 8], sqa[:, n, :],
                               start=n == 0, stop=n == 3)
            mm.then_inc(S("small_products"), 1)
            bank_free(pe, "rq")
            for hd in range(4):
                for j in range(2):
                    i = 2 * hd + j
                    mm = pe.matmul(bank("rq")[:, 2 * i:2 * i + 2], sqq[:, hd, j * P:(j + 1) * P], c("half", 2),
                                   start=True, stop=True)
            mm.then_inc(S("small_products"), 1)
            project("g2_16", None, lat)
            pe.wait_ge(S("k_inverse"), 1)
            for n in range(4):
                bank_free(pe, f"kb{n}")
                pe.matmul(bank(f"kb{n}"), cst[0:8, CST["sel_kt"] + n * P:CST["sel_kt"] + (n + 1) * P], krow_i,
                          start=True, stop=True).then_inc(S("small_products"), 1)
            for n in range(2):
                bank_free(pe, f"raq{n}")
                pe.wait_ge(S("aq_scaled"), 1)
                pe.matmul(bank(f"raq{n}"), c("rot_att", P), aq[:, 2 * n:2 * n + 2, :], start=True, stop=True)\
                  .then_inc(S("small_products"), 1)
            for n in range(2):
                bank_free(pe, f"rak{n}")
                evacuated(pe, "kb2", "kb3")
                pe.matmul(bank(f"rak{n}"), c("rot_att", P), ak[:, 2 * n:2 * n + 2, T:TT], start=True, stop=True)\
                  .then_inc(S("small_products"), 1)

            def a_scores(i):
                hd, j = i // 2, i % 2
                if i < 2:
                    pe.wait_ge(S("att_roped"), 4)
                    pe.wait_ge(S("av_copied"), 4)
                    pe.wait_ge(S("s_out"), 8)
                else:
                    pe.wait_ge(S("a_exps"), 2 * (i - 1))
                for b in range(2):
                    mm = pe.matmul(psum[:, (0 if i % 2 == 0 else 6) + b, :], aq[64 * b:64 * b + 64, hd, j * P:(j + 1) * P],
                                   ak[64 * b:64 * b + 64, hd, :], start=True, stop=True)
                mm.then_inc(S("a_scores"), 1)

            def a_turn(i):
                pe.wait_ge(S("a_probs"), i + 1)
                if i:
                    pe.wait_ge(S("a_turned_copied"), i)
                for s in range(4):
                    mm = pe.transpose(psum[:, 2, s * P:(s + 1) * P], prob2[:, i % 2, 0, s * P:(s + 1) * P], ident)
                mm.then_inc(S("a_turned"), 1)

            def a_values(i):
                pe.wait_ge(S("a_turned_copied"), i + 1)
                if i:
                    pe.wait_ge(S("a_out"), i)
                for s in range(4):
                    mm = pe.matmul(psum[:, 3, 0:P], av[:, s, i // 2 * P:(i // 2 + 1) * P], probt2[:, i % 2, s, :],
                                   start=s == 0, stop=s == 3)
                mm.then_inc(S("a_values"), 1)

            def head_sums(hd):
                pe.wait_ge(S("branch_squares"), 3 + hd)
                pe.matmul(half_bank((0, 1, 6, 7)[hd], 0), ones, sq[:, hd, :], start=True, stop=True)\
                  .then_inc(S("branch_sums"), 1)

            a_scores(0)
            for i in range(8):
                if i < 7:
                    a_scores(i + 1)
                if i < 7:
                    project(f"g2_{17 + i}", None, lat)
                a_turn(i)
                if i:
                    a_values(i - 1)
                if i == 7:
                    for hd in range(3):
                        head_sums(hd)
            a_values(7)
            head_sums(3)

            for n in range(8):
                for s, (m, o) in enumerate([("wm", ym), ("wat", ya), ("ws", ys)]):
                    name = f"m2_{n}{'aab'[s]}"
                    if not n:
                        pe.wait_ge(S("branches"), (1, 9, 5)[s])
                    if s != 1:
                        bank_free(pe, name)
                    w = tile_wait(AT[(m, n // 2)])
                    for k in range(4):
                        mm = pe.matmul(bank(name)[:, s % 2 * T:(s % 2 + 1) * T],
                                       w[:, (n % 2 * 4 + k) * P:(n % 2 * 4 + k + 1) * P], o[:, k, :],
                                       start=k == 0, stop=k == 3)
                    if s == 0 and n % 2:
                        mm.then_inc(S("tiles_used"), 1)
                    if s == 1:
                        mm.then_inc(S("small_products"), 1)
                    if s == 2:
                        if n % 2:
                            mm.then_inc(S("tiles_used"), 2)
                        else:
                            mm.then_inc(S("small_products"), 1)
            pe.wait_ge(S("branch_roots"), 3)
            for n in range(8):
                pe.wait_ge(S("merged"), 16)
                cols(AT[("out2", n)], acc[n], lambda k: merged2[:, k, :])
            sums_wide("norm2")

            ffn(2)

        @block.scalar
        def _(act):
            steps = [0]

            def link(ins):
                steps[0] += 1
                ins.then_inc(S("scalar_steps"), 1)
                act.wait_ge(S("scalar_steps"), steps[0])

            def squares(name, chunk2, ready, scale=1.0):
                for k in range(4):
                    ready(k)
                    act.activation(sq[:, 2 * k:2 * k + 2, :], chunk2(k), ACT.Square, scale=scale).then_inc(S("squares"), 1)

            def take_root(name, features):
                i = NORM_AT[name]
                act.wait_ge(S("sums"), i + 1)
                if i:
                    act.wait_ge(S("inverses"), i)
                act.activation(root, half_bank(SUMS, 0), ACT.Sqrt, scale=1.0 / features, bias=eps)\
                   .then_inc(S("roots"), 1)

            def input_uppers(k, name, count, before=lambda n: None):
                for n in range(DC):
                    before(n)
                    act.wait_ge(S(name), count + n + 1)
                    act.activation(u_hi[:, n, :], u1[:, n, :], ACT.Copy).then_inc(S("input_upper"), 1)

            def uppers(k, first, last):
                for j in range(first, last):
                    upper(k, j)

            def upper(k, j, more=0):
                t = AT[(f"gate{FFNS[k]}", 0)] + j
                act.wait_ge(S(f"slot{t % RING}_loaded"), more * 16 + 16 * (t // RING + 1))
                if k or j >= RING or not isinstance(more, int):
                    act.wait_ge(S("tiles_used"), more * RING + (t - RING + 1))
                act.activation(ring_hi[:, j % RING, :], ring[:, t % RING, :], ACT.Copy)\
                   .then_inc(S("upper_ready"), 1)

            def upper_hidden(par, count):
                act.wait_ge(S("hidden_ready"), count + 1)
                act.activation(hidden_hi[:, par, :], hidden[:, par, :], ACT.Copy)\
                   .then_inc(S("hidden_upper"), 1)

            def feed_forward(k, gate):
                for par in range(2):
                    gate(par, par, k > 0)
                    upper(k, 6 + 3 * par)
                    upper_hidden(par, FC * k + par)
                    upper(k, 7 + 3 * par)
                    upper(k, 8 + 3 * par)
                with act.Fori(0, FC // 2 - 2) as i:
                    for par in range(2):
                        gate(par, i * 2 + (2 + par), True, i)
                        upper(k, 12 + 3 * par, i)
                        upper_hidden(par, i * 2 + (FC * k + 2 + par))
                        upper(k, 13 + 3 * par, i)
                        upper(k, 14 + 3 * par, i)
                for par in range(2):
                    gate(par, FC - 2 + par, True)
                    upper_hidden(par, FC * k + FC - 2 + par)

            def ffn(k):
                base = FC * k

                def gate(par, f, reuse, more=None):
                    used = AT[(f"up{FFNS[k]}", f)] + 1 if more is None else \
                        more * RING + (AT[(f"up{FFNS[k]}", 2 + par)] + 1)
                    act.wait_ge(S("tiles_used"), used)
                    if reuse:
                        act.wait_ge(S("hidden_ready"), f + (base - 1))
                    act.activation(silu[:, par, :], half_bank(PJ[par], 0), ACT.Silu).then_inc(S("silus"), 1)

                feed_forward(k, gate)

            def ffn_conv():
                base = 2 * FC

                def gate(par, f, reuse, more=None):
                    used = AT[("up3", f)] + 1 if more is None else more * RING + (AT[("up3", 2 + par)] + 1)
                    act.wait_ge(S("tiles_used"), used)
                    act.wait_ge(S("hidden_ready"), f + (base - 1))
                    for s, dst in enumerate((cg, ca)):
                        act.activation(dst[:, par, :], half_bank(PJ[par], s), ACT.Identity,
                                       scale=vec[:, bass.ds(f + (VEC["fconv"] + FC * (2 + s)), 1)])\
                           .then_inc(S("conv_centers"), 1)
                    act.wait_ge(S("conv_sides"), f * 4 + 3)
                    act.activation(silu[:, par, :], cg[:, par, :], ACT.Silu).then_inc(S("silus"), 1)

                feed_forward(2, gate)

            def copy_bank(name, dst, src=None, func=ACT.Copy, **kw):
                product_ready(act, name)
                act.activation(dst, bank(name)[:, 0:T] if src is None else src, func, **kw).then_inc(read_done(name), 1)

            act.dma_start(vec, dram["vec"]).then_inc(S("tables_loaded"), 16)
            act.dma_start(cst, dram["cst"]).then_inc(S("tables_loaded"), 16)
            act.dma_start(lam_p, dram["lam"].partition_broadcast(P)).then_inc(S("tables_loaded"), 16)
            act.dma_start(pos_i, dram["pos"].partition_broadcast(P)).then_inc(S("tables_loaded"), 16)
            act.preload_act_table(ACT.Sqrt)
            act.wait_ge(S("x_loaded"), 16)
            act.wait_ge(S("ones_ready"), 1)
            squares("ffn1_pre", lambda k: h[:, 2 * k:2 * k + 2, :], lambda k: None)
            uppers(0, 0, 1)
            take_root("ffn1_pre", D)
            input_uppers(0, "scaled", 0)
            uppers(0, 1, RING)
            act.dma_start(wuq, dram["wuq"]).then_inc(S("small_weights"), 16)
            act.dma_start(wkr, dram["wkr"]).then_inc(S("small_weights"), 16)
            act.wait_ge(S("tables_loaded"), 64)
            act.activation(cond, vec[:, VEC["cond"]:VEC["cond"] + 16], ACT.Silu).then_inc(S("cond_ready"), 1)
            act.preload_act_table(ACT.Silu)
            ffn(0)

            def post_squares(name, last_tile, scale=1.0):
                squares(name, lambda k: psum[:, k, :], lambda k: act.wait_ge(S("tiles_used"), last_tile + 1), scale)
                take_root(name, D)

            post_squares("ffn1_post", AT[("down1", FC - 1)])
            squares("mix_pre", lambda k: h[:, 2 * k:2 * k + 2, :], lambda k: act.wait_ge(S("residual"), 2 * k + 2))
            act.activation(row_exp, v("row_alog"), ACT.Exp).then_inc(S("early"), 1)
            act.wait_ge(S("lam_sums"), 1)
            act.activation(lam[:, 2:4], lam[:, 0:2], ACT.Exp).then_inc(S("early"), 1)
            act.wait_ge(S("angles_ready"), 1)
            act.activation(tab, ang, ACT.Sin).then_inc(S("tab_ready"), 1)
            act.preload_act_table(ACT.Sqrt)
            take_root("mix_pre", D)

            for n in range(3):
                product_ready(act, f"cq{n}")
                act.activation(sq[:, n, :], bank(f"cq{n}")[:, 0:T], ACT.Square).then_inc(S("squares"), 1)
                copy_bank(f"cq{n}", cq[:, n, :])
            for n in range(2):
                product_ready(act, f"ckv{n}")
                act.activation(sq[:, 3 + n, :], bank(f"ckv{n}")[:, 0:T], ACT.Square).then_inc(S("squares"), 1)
                copy_bank(f"ckv{n}", ckv[:, n, :])
            copy_bank("kr", kr[64:96, :], bank("kr")[64:96, 0:T])
            take_root("q_norm", Q_RANK)
            for n in range(4):
                copy_bank(f"dq{n}", qd[:, n, :])
            take_root("kv_norm", KV_RANK)
            for n in range(4):
                copy_bank(f"dk{n}", kd[:, n, :])
            act.wait_ge(S("tiles_used"), AT[("dv", 3)] + 1)
            for n in range(2):
                act.activation(vd[:, n, :], psum[:, n, :], ACT.Copy).then_inc(S("vd_copied"), 1)
            for n in range(4):
                copy_bank(f"uk{n}", kh[0:64, 2 * n:2 * n + 2, :], bank(f"uk{n}")[0:64, :])
            act.wait_ge(S("tiles_used"), AT[("uv", 0)] + 1)
            for n in range(2):
                act.activation(va[:, n, :], psum[:, 2 + n, :], ACT.Copy).then_inc(S("va_copied"), 1)
            for n in range(4):
                copy_bank(f"uq{n}", q[0:96, 2 * n:2 * n + 2, :], bank(f"uq{n}")[0:96, :])

            def exps(k):
                act.wait_ge(S("negmax"), k + 1)
                if k >= 2:
                    act.wait_ge(S("turned"), k - 1)
                x = 2 * (k % 2)
                for j in range(2):
                    src = sbias[:, k % 2, j, :] if k < 8 else psum[:, k % 2, j * T:(j + 1) * T]
                    act.activation(prob[:, k % 2, j, :], src, ACT.Exp, bias=negmax[:, x + j:x + j + 1],
                                   scale=1.0 if k < 8 else SCALE_MLA, accum_out=den[:, x + j:x + j + 1])\
                       .then_inc(S("exps"), 1)

            def turned(k):
                act.wait_ge(S("turned"), k + 1)
                if k >= 2:
                    act.wait_ge(S("outs"), k - 1)
                act.activation(probt[:, k % 2, :, :], psum[:, 2 + k % 2, :], ACT.Copy).then_inc(S("turned_copied"), 1)

            exps(0)
            for k in range(16):
                copy_bank(f"g1_{k}", gates[:, k, :], None, ACT.Tanh, scale=0.5, bias=bhalf[:, k:k + 1])
                if k < 15:
                    exps(k + 1)
                turned(k)

            post_squares("mix_post", AT[("out1", 7)], 0.5)
            squares("ffn2_pre", lambda k: h[:, 2 * k:2 * k + 2, :], lambda k: act.wait_ge(S("residual"), 8 + 2 * k + 2))
            uppers(1, 0, 2)
            take_root("ffn2_pre", D)
            input_uppers(1, "scaled", 16)
            uppers(1, 2, RING)
            act.preload_act_table(ACT.Silu)
            ffn(1)
            post_squares("ffn2_post", AT[("down2", FC - 1)])

            act.wait_ge(S("ctx_loaded"), 16)
            squares("ctx", lambda k: ctx_raw[:, 2 * k:2 * k + 2, :], lambda k: act.wait_ge(S("sums"), 8))
            take_root("ctx", D)

            def shift_half(s):
                for n in range(DC):
                    act.wait_ge(S("prescaled"), 8 * s + n + 1)
                    x = u2[:, n, s * T:(s + 1) * T]
                    act.activation(x, x, ACT.Identity, bias=modc[:, n, 1 - s:2 - s]).then_inc(S("modulated"), 1)

            squares("norm1", lambda k: h[:, 2 * k:2 * k + 2, :], lambda k: act.wait_ge(S("residual"), 16 + 2 * k + 2))
            shift_half(0)
            take_root("norm1", D)
            shift_half(1)

            def conv(i, between=None):
                m, n, wt = CONV[i]
                name = f"{m}{n}"
                wide_ = m in ("mk", "sx") or m == "sb"
                product_ready(act, name)
                table = "mconv" if m in ("mk", "mq") else "sconv"
                dst = conv_dst[m][:, n, :]
                src = bank(name) if wide_ else bank(name)[:, 0:T]
                act.activation(dst, src, ACT.Identity, scale=v(table, 8 + wt)).then_inc(S("conv_center2"), 1)
                evacuated(act, name)
                act.activation(dst, dst, ACT.Silu, bias=v(table + "_b", wt)).then_inc(S("conv_done"), 1)

            for i in range(8):
                conv(i)
            act.wait_ge(S("rows_z"), 1)
            link(act.activation(sp, z, ACT.Abs))
            link(act.activation(sp, sp, ACT.Exp, scale=-1.0))
            act.activation(sp, sp, ACT.Ln, bias=1.0).then_inc(S("rows_log"), 1)
            act.wait_ge(S("tiles_used"), AT[("mv", 3)] + 1)
            for n in range(4):
                act.activation(mv[:, n, :], psum[:, n, :], ACT.Copy).then_inc(S("mv_copied"), 1)
            for n in range(4):
                copy_bank(f"mo{n}", mo[:, n, :], None, ACT.Tanh, scale=0.5)
            for i in range(8, 16):
                conv(i)
            act.wait_ge(S("cols_turned"), 1)
            act.activation(t0, psum[:, 0, :], ACT.Copy).then_inc(S("cols_copied"), 1)
            act.wait_ge(S("cols_turned"), 2)
            for n in range(2):
                act.activation(tc[:, 2 * n:2 * n + 2], psum[:, 1 + n, :], ACT.Copy).then_inc(S("cols_copied"), 1)
            for n in range(4):
                copy_bank(f"sz{n}", sz[:, n, :], None, ACT.Silu)

            def m_scores(hd):
                act.wait_ge(S("m_scores"), hd + 1)
                if hd:
                    act.wait_ge(S("m_weights"), 2 * hd)
                act.activation(mst[:, 0:4, :], psum[:, 2:4, :], ACT.Copy, scale=SCALE_M).then_inc(S("m_scores_part"), 1)
                act.activation(mst[:, 4:6, :], psum[:, 2, :], ACT.Copy, scale=SCALE_M).then_inc(S("m_scores_copied"), 1)

            def m_exps(i):
                act.wait_ge(S("m_masked"), i + 1)
                if i >= 2:
                    act.wait_ge(S("m_sums"), i - 1)
                act.activation(wgt[:, i % 2], arg[:, i % 2], ACT.Exp).then_inc(S("m_exps"), 1)
                if i >= 2:
                    act.wait_ge(S("m_out"), i - 1)
                act.activation(hidden[:, i % 2, :], psum[:, i % 2, T:TT], ACT.Exp).then_inc(S("m_floor"), 1)

            m_scores(0)
            m_exps(0)
            for i in range(8):
                if i < 7:
                    m_exps(i + 1)
                copy_bank(f"g2_{i}", gates[:, i, :], None, ACT.Tanh, scale=0.5)
                if i % 2 == 1 and i < 7:
                    m_scores(i // 2 + 1)
                act.wait_ge(S("m_sums"), i + 1)
                act.activation(silu[:, i % 2, :], psum[:, 6 + i % 2, T:TT], ACT.Abs).then_inc(S("m_abs"), 1)

            for g in range(2):
                act.wait_ge(S("sg_ready"), g + 1)
                act.activation(sg[:, g, 0:4, :], psum[:, 2:4, :], ACT.Copy).then_inc(S("sg_part"), 1)
                act.activation(sg[:, g, 4:6, :], psum[:, 2, :], ACT.Copy).then_inc(S("sg_copied"), 1)

            def s_exps(hd):
                for d in range(2):
                    act.wait_ge(S("s_masked"), 2 * hd + d + 1)
                    if hd:
                        act.wait_ge(S("s_sums"), hd)
                    act.activation(wgt[:, d], arg[:, d], ACT.Exp).then_inc(S("s_exps"), 1)

            s_exps(0)
            for hd in range(8):
                copy_bank(f"g2_{8 + hd}", gates[:, 8 + hd, :], None, ACT.Tanh, scale=0.5)
                if hd < 7:
                    s_exps(hd + 1)

            act.wait_ge(S("s_sums"), 8)
            act.activation(sq[:, 0:4, :], ym, ACT.Square).then_inc(S("branch_squares"), 1)
            copy_bank("aq0", aq[:, 0, :])
            act.wait_ge(S("ys_done"), 1)
            act.activation(tmp[:, 0:4, :], ys, ACT.Square).then_inc(S("branch_squares"), 1)
            copy_bank("aq1", aq[:, 1, :])
            act.wait_ge(S("branch_sums"), 1)
            act.activation(tmp[:, 4:8, :], psum[:, 2:4, :], ACT.Sqrt, scale=1.0 / 128, bias=eps).then_inc(S("branch_roots"), 1)
            copy_bank("aq2", aq[:, 2, :])
            act.wait_ge(S("branch_sums"), 2)
            act.activation(hidden, psum[:, 6, :], ACT.Sqrt, scale=1.0 / 256, bias=eps).then_inc(S("branch_roots"), 1)
            copy_bank("aq3", aq[:, 3, :])
            for n in range(4):
                copy_bank(f"ak{n}", ak[:, n, :], bank(f"ak{n}"))
            for n in (2, 3):
                evacuated(act, f"aq{n}", f"ak{n}")
            act.activation(sqa, ak, ACT.Square).then_inc(S("a_squares"), 1)
            act.activation(sqq, aq, ACT.Square).then_inc(S("a_squares"), 1)
            act.wait_ge(S("tiles_used"), AT[("av", 3)] + 1)
            for n in range(4):
                act.activation(av[:, n, :], psum[:, n, :], ACT.Copy).then_inc(S("av_copied"), 1)
            act.wait_ge(S("branches"), 5)
            copy_bank("krow", krow_r, bank("krow")[0:8, :], ACT.Sqrt, scale=1.0 / 64, bias=eps[0:8, :])
            copy_bank("rq", rq, bank("rq")[:, 0:16], ACT.Sqrt, scale=1.0 / 64, bias=eps)
            copy_bank("g2_16", gates[:, 16, :], None, ACT.Tanh, scale=0.5)

            def a_exps(i):
                act.wait_ge(S("a_negmax"), i + 1)
                if i >= 2:
                    act.wait_ge(S("a_turned"), i - 1)
                x = 2 * (i % 2)
                for b in range(2):
                    act.activation(prob2[:, i % 2, b, :], psum[:, (0 if i % 2 == 0 else 6) + b, :], ACT.Exp,
                                   bias=negmax[:, x + b:x + b + 1], scale=rq[:, 2 * i + b:2 * i + b + 1],
                                   accum_out=den[:, x + b:x + b + 1]).then_inc(S("a_exps"), 1)

            a_exps(0)
            for i in range(8):
                if i < 7:
                    copy_bank(f"g2_{17 + i}", gates[:, 17 + i, :], None, ACT.Tanh, scale=0.5)
                if i < 7:
                    a_exps(i + 1)
                act.wait_ge(S("a_turned"), i + 1)
                if i >= 2:
                    act.wait_ge(S("a_values"), i - 1)
                act.activation(probt2[:, i % 2], psum[:, 2, :], ACT.Copy).then_inc(S("a_turned_copied"), 1)

            def head_squares(hd):
                act.wait_ge(S("a_out"), 2 * hd + 2)
                act.activation(sq[:, hd, :], ya[:, hd, :], ACT.Square).then_inc(S("branch_squares"), 1)

            def head_root(hd):
                act.wait_ge(S("branch_sums"), 3 + hd)
                act.activation(tmp[:, 4 + hd, :], half_bank((0, 1, 6, 7)[hd], 0), ACT.Sqrt, scale=1.0 / 128, bias=eps)\
                   .then_inc(S("branch_roots"), 1)

            for hd in range(3):
                head_squares(hd)
            head_root(0)
            head_squares(3)
            for hd in range(1, 4):
                head_root(hd)

            uppers(2, 0, 4)
            squares("norm2", lambda k: h[:, 2 * k:2 * k + 2, :], lambda k: act.wait_ge(S("added"), 2 * k + 2))
            take_root("norm2", D)

            def shift(n):
                act.wait_ge(S("prescaled"), 16 + n + 1)
                act.activation(u1[:, n, :], u1[:, n, :], ACT.Identity, bias=modc[:, 24 + n, 0:1]).then_inc(S("modulated"), 1)

            input_uppers(2, "modulated", 16, shift)
            uppers(2, 4, RING)
            act.preload_act_table(ACT.Silu)
            ffn_conv()

        @block.vector
        def _(dve):
            steps = [0]

            def link(ins):
                steps[0] += 1
                ins.then_inc(S("vector_steps"), 1)
                dve.wait_ge(S("vector_steps"), steps[0])

            inverse_used = {"ffn1_post": ("scaled", 8), "mix_pre": ("post_scaled", 8), "q_norm": ("scaled", 16),
                            "kv_norm": ("q_scaled", 3), "mix_post": ("kv_scaled", 2), "ffn2_pre": ("post_scaled", 16),
                            "ffn2_post": ("scaled", 24), "ctx": ("post_scaled", 24), "norm1": ("prescaled", 8)}

            def invert(name):
                i = NORM_AT[name]
                if name in inverse_used:
                    dve.wait_ge(S(inverse_used[name][0]), inverse_used[name][1])
                dve.wait_ge(S("roots"), i + 1)
                dve.reciprocal(inv, root).then_inc(S("inverses"), 1)
                dve.wait_ge(S("inverses"), i + 1)

            def scale_into(name, dst, src, g, sem, between=lambda n: None):
                invert(name)
                for n in range(len(src)):
                    dve.scalar_tensor_tensor(out=dst[n], in0=src[n], scalar=g(n), in1=inv, op0=ALU.mult,
                                             op1=ALU.mult).then_inc(S(sem), 1)
                    between(n)

            def post(name, g):
                p = POSTS.index(name)
                invert(name)
                for n in range(DC + 1):
                    if n < DC:
                        dve.scalar_tensor_tensor(out=tmp[:, n, :], in0=acc[n], scalar=v(g, n), in1=inv, op0=ALU.mult,
                                                 op1=ALU.mult).then_inc(S("post_scaled"), 1)
                    if n:
                        dve.wait_ge(S("post_scaled"), 8 * p + n)
                        dve.scalar_tensor_tensor(out=h[:, n - 1, :], in0=tmp[:, n - 1, :], scalar=0.5,
                                                 in1=h[:, n - 1, :], op0=ALU.mult, op1=ALU.add)\
                           .then_inc(S("residual"), 1)

            def lower(k, j, more=0):
                t = AT[(f"gate{FFNS[k]}", 0)] + j
                dve.wait_ge(S("upper_ready"), more * RING + (3 * FC * k + j + 1))
                dve.tensor_tensor(ring_lo[:, j % RING, :], ring[:, t % RING, :], ring_hi[:, j % RING, :],
                                  ALU.subtract).then_inc(S("lower_ready"), 1)

            def lower_hidden(par, count):
                dve.wait_ge(S("hidden_upper"), count + 1)
                dve.tensor_tensor(hidden_lo[:, par, :], hidden[:, par, :], hidden_hi[:, par, :],
                                  ALU.subtract).then_inc(S("hidden_split"), 1)

            def lower_input(k, n):
                dve.wait_ge(S("input_upper"), DC * k + n + 1)
                dve.tensor_tensor(u_lo[:, n, :], u1[:, n, :], u_hi[:, n, :], ALU.subtract)\
                   .then_inc(S("input_split"), 1)

            def begin_feed_forward(k, norm, early, late, g, sem):
                for j in early:
                    lower(k, j)
                scale_into(norm, [u1[:, n, :] for n in range(DC)], [h[:, n, :] for n in range(DC)], g, sem,
                           lambda n: lower_input(k, n - 2) if n >= 2 else None)
                lower_input(k, DC - 2)
                lower_input(k, DC - 1)
                for j in late:
                    lower(k, j)

            def feed_forward(k, product):
                for par in range(2):
                    product(par, par)
                    lower(k, 6 + 3 * par)
                    lower_hidden(par, FC * k + par)
                    lower(k, 7 + 3 * par)
                    lower(k, 8 + 3 * par)
                with dve.Fori(0, FC // 2 - 2) as i:
                    for par in range(2):
                        product(par, i * 2 + (2 + par))
                        lower(k, 12 + 3 * par, i)
                        lower_hidden(par, i * 2 + (FC * k + 2 + par))
                        lower(k, 13 + 3 * par, i)
                        lower(k, 14 + 3 * par, i)
                for par in range(2):
                    product(par, FC - 2 + par)
                    lower_hidden(par, FC * k + FC - 2 + par)

            def ffn(k):
                def multiply(par, f):
                    dve.wait_ge(S("silus"), f + (FC * k + 1))
                    dve.tensor_tensor(hidden[:, par, :], silu[:, par, :], half_bank(PJ[par], 1), ALU.mult)\
                       .then_inc(S("hidden_ready"), 1)

                feed_forward(k, multiply)

            def ffn_conv():
                base = 2 * FC

                def side(dst, s, par, f, tap):
                    a, b = (slice(1, T), slice(0, T - 1)) if tap == 0 else (slice(0, T - 1), slice(1, T))
                    w = vec[:, bass.ds(f + (VEC["fconv"] + FC * (2 * tap + s)), 1)]
                    dve.scalar_tensor_tensor(out=dst[:, par, a], in0=half_bank(PJ[par], s)[:, b], scalar=w,
                                             in1=dst[:, par, a], op0=ALU.mult, op1=ALU.add).then_inc(S("conv_sides"), 1)

                def chunk(par, f):
                    dve.wait_ge(S("conv_centers"), f * 2 + 2)
                    side(cg, 0, par, f, 0)
                    side(ca, 1, par, f, 0)
                    dve.wait_ge(S("conv_sides"), f * 4 + 1)
                    side(cg, 0, par, f, 2)
                    dve.wait_ge(S("conv_sides"), f * 4 + 2)
                    side(ca, 1, par, f, 2)
                    dve.wait_ge(S("conv_sides"), f * 4 + 4)
                    dve.wait_ge(S("silus"), f + (base + 1))
                    dve.tensor_tensor(hidden[:, par, :], silu[:, par, :], ca[:, par, :], ALU.mult)\
                       .then_inc(S("hidden_ready"), 1)

                feed_forward(2, chunk)

            def mod_copy(n0, n1):
                dve.wait_ge(S("tiles_used"), AT[("mod", n1 - 1)] + 1)
                b = vec[:, VEC["bmod"] + n0:VEC["bmod"] + n1].unsqueeze(2).broadcast_to([P, n1 - n0, 2])
                dve.tensor_tensor(modc[:, n0:n1, :],
                                  psum[:, MOD, 2 * n0:2 * n1].rearrange("p (n b) -> p n b", b=2), b, ALU.add)\
                   .then_inc(S("mod_ready"), 1)

            dve.memset(eps, EPS).then_inc(S("ones_part"), 1)
            dve.wait_ge(S("ones_part"), 1)
            dve.memset(ones, 1.0).then_inc(S("ones_ready"), 1)
            dve.wait_ge(S("tables_loaded"), 64)
            begin_feed_forward(0, "ffn1_pre", range(1), range(1, RING), lambda n: v("ffn1_pre", n), "scaled")
            ffn(0)
            post("ffn1_post", "ffn1_post")

            link(dve.tensor_scalar(row_bias, v("row_bias"), c("sign", 1), None, ALU.mult))
            link(dve.tensor_scalar(bhalf, vec[:, VEC["bgate"]:VEC["bgate"] + 16], 0.5, None, ALU.mult))
            link(dve.tensor_scalar(g_half, vec[:, VEC["mnorm"]:VEC["mnorm"] + 4], 0.5, None, ALU.mult))
            link(dve.tensor_scalar(g_sub, v("subln"), 1.0 - LAM_INIT, None, ALU.mult))
            lp = lam_p.rearrange("p (a b n) -> p a b n", a=2, b=2)
            link(dve.tensor_tensor(lp[:, :, 0, :], lp[:, :, 0, :], lp[:, :, 1, :], ALU.mult))
            dve.tensor_reduce(lam[:, 0:2], lp[:, :, 0, :], AX_X, ALU.add).then_inc(S("lam_sums"), 1)
            dve.wait_ge(S("early"), 2)
            link(dve.tensor_scalar(row_coef, row_exp, -1.0, None, ALU.mult))
            link(dve.tensor_tensor(lam[:, 4:5], lam[:, 3:4], lam[:, 2:3], ALU.subtract))
            link(dve.tensor_scalar(lam[:, 5:6], lam[:, 4:5], -LAM_INIT, None, ALU.add))
            link(dve.tensor_copy(posf, pos_i))
            for n in range(2):
                for s in range(2):
                    link(dve.tensor_scalar(ang[:, n, s, :], posf, c("freq", 2)[:, n:n + 1], None, ALU.mult))
            turns = tab.rearrange("p (n s) t -> p n s t", n=2)
            link(dve.tensor_scalar(turns, ang, 1.0 / TWO_PI, None, ALU.mult))
            link(dve.tensor_scalar(turns[:, :, 1, :], turns[:, :, 1, :], 0.25, None, ALU.add))
            link(dve.tensor_scalar(turns, turns, MAGIC, None, ALU.add))
            link(dve.tensor_scalar(turns, turns, -MAGIC, None, ALU.add))
            for part in two_pi_parts():
                link(dve.scalar_tensor_tensor(out=ang, in0=turns, scalar=-part, in1=ang, op0=ALU.mult, op1=ALU.add))
            link(dve.tensor_scalar(ang[:, :, 1, :], ang[:, :, 1, :], float(np.pi / 2), None, ALU.add))
            dve.tensor_scalar(ang, ang, 3.1415925, -3.1415925, ALU.min, ALU.max).then_inc(S("angles_ready"), 1)

            mod_copy(0, 18)
            scale_into("mix_pre", [u1[:, n, :] for n in range(DC)], [h[:, n, :] for n in range(DC)],
                       lambda n: v("mix_pre", n), "scaled")

            scale_into("q_norm", [cq[:, n, :] for n in range(3)], [cq[:, n, :] for n in range(3)],
                       lambda n: v("q_norm", n), "q_scaled")
            scale_into("kv_norm", [ckv[:, n, :] for n in range(2)], [ckv[:, n, :] for n in range(2)],
                       lambda n: v("kv_norm", n), "kv_scaled")

            def rotate(x, rows, name, sin, cos, t, heads, done):
                product_ready(dve, name)
                width = heads * T
                rot = bank(name)[rows, 0:width].rearrange("p (a b) -> p a b", a=heads)
                wide_ = lambda a: a.unsqueeze(1).broadcast_to([rows.stop - rows.start, heads, T])
                tt = t[rows, 0:width].rearrange("p (a b) -> p a b", a=heads)
                dve.tensor_tensor(tt, rot, wide_(sin), ALU.mult).then_inc(read_done(name), 1)
                link(dve.tensor_tensor(x, x, wide_(cos), ALU.mult))
                evacuated(dve, name)
                dve.tensor_tensor(x, x, tt, ALU.add).then_inc(S(done), 1)

            all_rows, mla_rows = slice(0, P), slice(64, 96)
            dve.wait_ge(S("tab_ready"), 1)
            for n, (x, name) in enumerate([(qd, "rdq0"), (qd, "rdq1"), (kd, "rdk0"), (kd, "rdk1")]):
                if n:
                    dve.wait_ge(S("dil_roped"), n)
                rotate(x[:, 2 * (n % 2):2 * (n % 2) + 2, :], all_rows, name, tab[:, 2, :], tab[:, 3, :], rt, 2, "dil_roped")
            dve.wait_ge(S("dil_roped"), 4)
            for n in range(4):
                if n:
                    dve.wait_ge(S("mla_roped"), n)
                rotate(q[64:96, 2 * n:2 * n + 2, :], mla_rows, f"ruq{n}", tab[64:96, 0, :], tab[64:96, 1, :], rt, 2, "mla_roped")
            dve.wait_ge(S("mla_roped"), 4)
            rotate(kr[64:96, :].unsqueeze(1), mla_rows, "rkr", tab[64:96, 0, :], tab[64:96, 1, :], rt, 1, "kr_roped")
            dve.wait_ge(S("kr_roped"), 1)
            dve.tensor_copy(kh[64:96, :, :], kr[64:96, :].unsqueeze(1).broadcast_to([32, 8, T])).then_inc(S("mla_roped"), 1)

            def maxima(k):
                dve.wait_ge(S("scores"), k + 1)
                x = 2 * (k % 2)
                src = psum[:, k % 2, :].rearrange("p (j n) -> p j n", j=2)
                if k >= 2:
                    dve.wait_ge(S("exps"), 2 * (k - 1))
                if k < 8:
                    link(dve.scalar_tensor_tensor(out=sbias[:, k % 2], in0=src, scalar=SCALE_64,
                                                  in1=c("dil_bias", TT).rearrange("p (j n) -> p j n", j=2),
                                                  op0=ALU.mult, op1=ALU.add))
                    src = sbias[:, k % 2]
                link(dve.tensor_reduce(dmax[:, x:x + 2], src, AX_X, ALU.max))
                dve.tensor_scalar(negmax[:, x:x + 2], dmax[:, x:x + 2], -1.0 if k < 8 else -SCALE_MLA, None, ALU.mult)\
                   .then_inc(S("negmax"), 1)

            def normalise(k):
                x = 2 * (k % 2)
                dve.wait_ge(S("exps"), 2 * k + 2)
                link(dve.reciprocal(rden[:, x:x + 2], den[:, x:x + 2]))
                for j in range(2):
                    dve.tensor_scalar(prob[:, k % 2, j, :], prob[:, k % 2, j, :], rden[:, x + j:x + j + 1], None, ALU.mult)\
                       .then_inc(S("probs"), 1)

            def out(k):
                r = slice(64 * (k % 2), 64 * (k % 2) + 64)
                dve.wait_ge(S("outs"), k + 1)
                dst = ob[r, k // 2, :] if k < 8 else oa[r, (k - 8) // 2, :]
                dve.tensor_copy(dst, psum[r, 6 + k % 2, 0:T]).then_inc(S("outs_copied"), 1)

            maxima(0)
            for k in range(16):
                normalise(k)
                if k < 15:
                    maxima(k + 1)
                if k:
                    out(k - 1)
            out(15)

            for n in range(8):
                name = f"m1_{n}"
                product_ready(dve, name)
                link(dve.scalar_tensor_tensor(out=rt[:, 0:T], in0=gates[:, n, :], scalar=1.0, in1=bank(name)[:, 0:T],
                                              op0=ALU.add, op1=ALU.mult))
                dve.scalar_tensor_tensor(out=rt[:, T:TT], in0=gates[:, 8 + n, :], scalar=1.0, in1=bank(name)[:, T:TT],
                                         op0=ALU.add, op1=ALU.mult).then_inc(read_done(name), 1)
                evacuated(dve, name)
                dve.tensor_tensor(merged1[:, n, :], rt[:, 0:T], rt[:, T:TT], ALU.add).then_inc(S("merged"), 1)
                dve.wait_ge(S("merged"), n + 1)
            post("mix_post", "mix_post")
            mod_copy(18, 36)
            begin_feed_forward(1, "ffn2_pre", range(2), range(2, RING), lambda n: v("ffn2_pre", n), "scaled")
            ffn(1)
            post("ffn2_post", "ffn2_post")

            def modulated_gain(n, m, who, g):
                link(dve.scalar_tensor_tensor(out=gmod[:, 8 * n:8 * n + 8], in0=modc[:, m:m + 8, who], scalar=1.0,
                                              in1=vec[:, VEC[g]:VEC[g] + 8], op0=ALU.add, op1=ALU.mult))

            modulated_gain(0, 8, 1, "norm1")
            modulated_gain(1, 8, 0, "norm1")
            scale_into("ctx", [u2[:, n, 0:T] for n in range(DC)], [ctx_raw[:, n, :] for n in range(DC)],
                       lambda n: gmod[:, n:n + 1], "prescaled")
            mod_copy(36, 48)
            dve.wait_ge(S("mod_ready"), 3)
            modulated_gain(2, 32, 0, "norm2")
            link(dve.tensor_scalar(mhalf, modc[:, 16:24, 0], 0.5, None, ALU.mult))
            scale_into("norm1", [u2[:, n, T:TT] for n in range(DC)], [h[:, n, :] for n in range(DC)],
                       lambda n: gmod[:, 8 + n:9 + n], "prescaled")

            product_ready(dve, "rows")
            rows = bank("rows")
            for a, swap in ((0, False), (64, False), (32, True), (96, True)):
                for s in range(2):
                    o = T * (1 - s if swap else s)
                    ins = dve.tensor_copy(raw[a:a + 32, o:o + T], rows[a:a + 32, s * T:(s + 1) * T])
                    if a == 96 and s == 1:
                        ins.then_inc(read_done("rows"), 1)
                        evacuated(dve, "rows")
                    else:
                        link(ins)
            dve.tensor_scalar(z, raw, c("sign", 1), row_bias, ALU.mult, ALU.add).then_inc(S("rows_z"), 1)

            def conv(i):
                m, n, wt = CONV[i]
                name = f"{m}{n}"
                wide_ = m in ("mk", "sx", "sb")
                table = "mconv" if m in ("mk", "mq") else "sconv"
                dst = conv_dst[m][:, n, :]
                src = bank(name) if wide_ else bank(name)[:, 0:T]
                if wide_:
                    dst, src = (a.rearrange("p (s t) -> p s t", s=2) for a in (dst, src))
                lo, hi = ((slice(None), slice(None), slice(0, T - 1)), (slice(None), slice(None), slice(1, T))) if wide_ \
                    else ((slice(None), slice(0, T - 1)), (slice(None), slice(1, T)))
                dve.wait_ge(S("conv_center2"), i + 1)
                link(dve.scalar_tensor_tensor(out=dst[hi], in0=src[lo], scalar=v(table, wt), in1=dst[hi], op0=ALU.mult,
                                              op1=ALU.add))
                dve.scalar_tensor_tensor(out=dst[lo], in0=src[hi], scalar=v(table, 16 + wt), in1=dst[lo], op0=ALU.mult,
                                         op1=ALU.add).then_inc(read_done(name), 1)

            for i in range(8):
                conv(i)
            dve.wait_ge(S("rows_log"), 1)
            link(dve.scalar_tensor_tensor(out=sp, in0=z, scalar=0.0, in1=sp, op0=ALU.max, op1=ALU.add))
            link(dve.tensor_scalar(da, sp, row_coef, None, ALU.mult))
            fw, bw = slice(0, 32), slice(32, 64)
            one = lambda n, a: ones[a:a + 32, 0:1].broadcast_to([32, n])
            link(dve.tensor_tensor_scan(bsum[fw, :], one(TT, 0), da[fw, :], 0.0, ALU.mult, ALU.add))
            link(dve.tensor_tensor_scan(bsum[bw, ::-1], one(TT, 32), da[bw, ::-1], 0.0, ALU.mult, ALU.add))
            product_ready(dve, "ish")
            dve.scalar_tensor_tensor(out=r0[0:64, :], in0=bank("ish")[0:64, :], scalar=v("row_ibias", 0, 0, 64),
                                     in1=bsum[0:64, :], op0=ALU.add, op1=ALU.subtract).then_inc(read_done("ish"), 1)
            evacuated(dve, "ish")
            link(dve.tensor_tensor_scan(mrow[fw, :], r0[fw, :], r0[fw, :], 0.0, ALU.max, ALU.max))
            link(dve.tensor_tensor_scan(mrow[bw, ::-1], r0[bw, ::-1], r0[bw, ::-1], 0.0, ALU.max, ALU.max))
            for rows_, o in ((fw, T), (bw, 0)):
                link(dve.tensor_scalar(rowm[rows_, 0, :], mrow[rows_, o:o + T], -1.0, None, ALU.mult))
                link(dve.scalar_tensor_tensor(out=rowm[rows_, 1, :], in0=bsum[rows_, o:o + T], scalar=-1.0,
                                              in1=mrow[rows_, o:o + T], op0=ALU.mult, op1=ALU.subtract))
            dve.tensor_copy(r0[64:P, :], sp[64:P, :]).then_inc(S("cols_in"), 1)
            link(dve.tensor_tensor_scan(rowl[64:96, :], c("reset", T, 64, 96), da[64:96, T:TT], 0.0, ALU.mult, ALU.add))
            link(dve.tensor_tensor_scan(rowl[96:P, ::-1], c("reset", T, 96, P)[:, ::-1], da[96:P, 0:T][:, ::-1], 0.0,
                                        ALU.mult, ALU.add))
            dve.wait_ge(S("colr_zero"), 1)
            for j in range(4):
                a = T + CHUNK * j
                b = CHUNK * (j + 1)
                link(dve.tensor_tensor_scan(colr[64:96, j, 0:a - 1][:, ::-1], one(a - 1, 64), da[64:96, 1:a][:, ::-1],
                                            0.0, ALU.mult, ALU.add))
                link(dve.tensor_scalar(colr[64:96, j, a:a + CHUNK], rowl[64:96, j * CHUNK:b], -1.0, None, ALU.mult))
                link(dve.tensor_tensor_scan(colr[96:P, j, b + 1:TT], one(TT - b - 1, 96), da[96:P, b:TT - 1],
                                            0.0, ALU.mult, ALU.add))
                ins = dve.tensor_scalar(colr[96:P, j, b - CHUNK:b], rowl[96:P, j * CHUNK:b], -1.0, None, ALU.mult)
                if j < 3:
                    link(ins)
                else:
                    ins.then_inc(S("cols_in"), 1)
            for i in range(8, 16):
                conv(i)

            def m_args(i):
                hd, d = i // 2, i % 2
                dve.wait_ge(S("m_rows"), i + 1)
                if i == 0:
                    dve.wait_ge(S("cols_copied"), 1)
                if i >= 2:
                    dve.wait_ge(S("m_exps"), i - 1)
                row = 32 * d + hd
                dve.tensor_tensor(arg[:, i % 2], psum[:, i % 2, 0:T].unsqueeze(1).broadcast_to([P, 4, T]),
                                  t0[:, :, row:row + 1].broadcast_to([P, 4, T]), ALU.add).then_inc(S("m_args"), 1)

            def m_weights(i):
                d = i % 2
                dve.wait_ge(S("m_exps"), i + 1)
                dve.wait_ge(S("m_scores_copied"), i // 2 + 1)
                dve.tensor_tensor(wgt[:, d], wgt[:, d], mst[:, 2 * d:2 * d + 4, :], ALU.mult).then_inc(S("m_weights"), 1)

            def m_out(i):
                hd, d = i // 2, i % 2
                dve.wait_ge(S("m_abs"), i + 1)
                link(dve.tensor_tensor(silu[:, d, :], silu[:, d, :], hidden[:, d, :], ALU.max))
                link(dve.reciprocal(silu[:, d, :], silu[:, d, :]))
                dst = inv if d else ym[:, hd, :]
                dve.tensor_tensor(dst, psum[:, 6 + d, 0:T], silu[:, d, :], ALU.mult).then_inc(S("m_out"), 1)
                if d:
                    dve.wait_ge(S("m_out"), i + 1)
                    link(dve.tensor_tensor(ym[:, hd, :], ym[:, hd, :], inv, ALU.add))

            m_args(0)
            for i in range(8):
                if i < 7:
                    m_args(i + 1)
                m_weights(i)
                if i:
                    m_out(i - 1)
            m_out(7)

            for s in range(4):
                dve.wait_ge(S("x_turned"), s + 1)
                for d in range(2):
                    dtc = t0[:, (s + 2 * d) % 4, 64 + 32 * d:72 + 32 * d].unsqueeze(2).broadcast_to([P, 8, 64])
                    dve.tensor_tensor(xdt[:, d, s, :].rearrange("p (h f) -> p h f", h=8),
                                      psum[:, s % 2, :].rearrange("p (h f) -> p h f", h=8), dtc, ALU.mult)\
                       .then_inc(S("xdt_ready"), 1)

            def s_args(hd):
                dve.wait_ge(S("s_rows"), hd + 1)
                dve.wait_ge(S("cols_copied"), 3)
                for d in range(2):
                    if hd:
                        dve.wait_ge(S("s_exps"), 2 * (hd - 1) + d + 1)
                    row = psum[:, hd % 2, d * T:(d + 1) * T].rearrange("p (j t) -> p j t", j=4)
                    col = tc[:, :, :, 32 * d + hd].rearrange("p j s -> p s j").unsqueeze(3)
                    dve.tensor_tensor(arg[:, d].rearrange("p s (j t) -> p s j t", j=4),
                                      row.unsqueeze(1).broadcast_to([P, 4, 4, CHUNK]),
                                      col.broadcast_to([P, 4, 4, CHUNK]), ALU.add).then_inc(S("s_args"), 1)

            def s_weights(hd):
                for d in range(2):
                    dve.wait_ge(S("s_exps"), 2 * hd + d + 1)
                    if hd == 0:
                        dve.wait_ge(S("sg_copied"), 2)
                    dve.tensor_tensor(wgt[:, d], wgt[:, d], sg[:, hd // 4, 2 * d:2 * d + 4, :], ALU.mult)\
                       .then_inc(S("s_weights"), 1)

            def s_out(hd):
                r = slice(64 * (hd % 2), 64 * (hd % 2) + 64)
                dve.wait_ge(S("s_sums"), hd + 1)
                dve.tensor_copy(ys[r, hd // 2, :], psum[r, 6 + hd % 2, 0:T]).then_inc(S("s_out"), 1)

            s_args(0)
            for hd in range(8):
                s_weights(hd)
                if hd < 7:
                    s_args(hd + 1)
                if hd:
                    s_out(hd - 1)
            s_out(7)
            dve.wait_ge(S("s_out"), 8)
            for f in range(4):
                link(dve.scalar_tensor_tensor(out=ys[:, f, :], in0=sx[:, f, T:TT], scalar=v("sskip", f), in1=ys[:, f, :],
                                              op0=ALU.mult, op1=ALU.add))
            dve.tensor_tensor(ys, ys, sz, ALU.mult).then_inc(S("ys_done"), 1)

            dve.wait_ge(S("branch_roots"), 1)
            link(dve.reciprocal(tmp[:, 4:8, :], tmp[:, 4:8, :]))
            for n in range(4):
                link(dve.scalar_tensor_tensor(out=ym[:, n, :], in0=ym[:, n, :], scalar=g_half[:, n:n + 1],
                                              in1=tmp[:, 4 + n, :], op0=ALU.mult, op1=ALU.mult))
            dve.scalar_tensor_tensor(out=ym, in0=mo, scalar=1.0, in1=ym, op0=ALU.add, op1=ALU.mult)\
               .then_inc(S("branches"), 1)
            dve.wait_ge(S("branch_roots"), 2)
            link(dve.reciprocal(hidden, hidden))
            for f in range(4):
                dve.scalar_tensor_tensor(out=ys[:, f, :], in0=ys[:, f, :], scalar=v("snorm", f), in1=hidden[:, f // 2, :],
                                         op0=ALU.mult, op1=ALU.mult).then_inc(S("branches"), 1)

            dve.wait_ge(S("a_squares"), 2)
            dve.tensor_scalar(aq, aq, v("aqn"), None, ALU.mult).then_inc(S("aq_scaled"), 1)
            evacuated(dve, "krow")
            dve.reciprocal(krow_i, krow_r).then_inc(S("k_inverse"), 1)
            evacuated(dve, "rq")
            link(dve.reciprocal(rq, rq))
            link(dve.tensor_scalar(rq, rq, SCALE_64, None, ALU.mult))
            for n in range(4):
                product_ready(dve, f"kb{n}")
                dve.scalar_tensor_tensor(out=ak[:, n, :], in0=ak[:, n, :], scalar=v("akn"), in1=bank(f"kb{n}"),
                                         op0=ALU.mult, op1=ALU.mult).then_inc(read_done(f"kb{n}"), 1)
            rt2 = place(MEM["silu"][0], 2 * T)
            for n in range(2):
                if n:
                    dve.wait_ge(S("att_roped"), 1)
                rotate(aq[:, 2 * n:2 * n + 2, :], all_rows, f"raq{n}", c("sin_att", T), c("cos_att", T), rt2, 2, "att_roped")
            for n in range(2):
                dve.wait_ge(S("att_roped"), 2 + n)
                rotate(ak[:, 2 * n:2 * n + 2, T:TT], all_rows, f"rak{n}", c("sin_att", T), c("cos_att", T), rt2, 2,
                       "att_roped")

            def a_maxima(i):
                x = 2 * (i % 2)
                b = 0 if i % 2 == 0 else 6
                dve.wait_ge(S("a_scores"), i + 1)
                if i >= 2:
                    dve.wait_ge(S("a_exps"), 2 * (i - 1))
                link(dve.tensor_reduce(dmax[:, x:x + 2], psum[:, b:b + 2, :], AX_X, ALU.max))
                dve.scalar_tensor_tensor(out=negmax[:, x:x + 2], in0=dmax[:, x:x + 2], scalar=-1.0,
                                         in1=rq[:, 2 * i:2 * i + 2], op0=ALU.mult, op1=ALU.mult).then_inc(S("a_negmax"), 1)

            def a_combine(i):
                x = 2 * (i % 2)
                dve.wait_ge(S("a_exps"), 2 * i + 2)
                link(dve.reciprocal(rden[:, x:x + 2], den[:, x:x + 2]))
                link(dve.tensor_scalar(rden[:, x + 1:x + 2], rden[:, x + 1:x + 2], lam[:, 5:6], None, ALU.mult))
                link(dve.tensor_scalar(prob2[:, i % 2, 0, :], prob2[:, i % 2, 0, :], rden[:, x:x + 1], None, ALU.mult))
                dve.scalar_tensor_tensor(out=prob2[:, i % 2, 0, :], in0=prob2[:, i % 2, 1, :], scalar=rden[:, x + 1:x + 2],
                                         in1=prob2[:, i % 2, 0, :], op0=ALU.mult, op1=ALU.add).then_inc(S("a_probs"), 1)

            def a_out(i):
                dve.wait_ge(S("a_values"), i + 1)
                dve.tensor_copy(ya[:, i // 2, i % 2 * P:(i % 2 + 1) * P], psum[:, 3, 0:P]).then_inc(S("a_out"), 1)

            a_maxima(0)
            for i in range(8):
                a_combine(i)
                if i < 7:
                    a_maxima(i + 1)
                if i:
                    a_out(i - 1)

            def head_norm(hd):
                dve.wait_ge(S("branch_roots"), 3 + hd)
                link(dve.reciprocal(tmp[:, 4 + hd, :], tmp[:, 4 + hd, :]))
                dve.scalar_tensor_tensor(out=ya[:, hd, :], in0=ya[:, hd, :], scalar=g_sub, in1=tmp[:, 4 + hd, :],
                                         op0=ALU.mult, op1=ALU.mult).then_inc(S("branches"), 1)

            a_out(7)
            head_norm(0)

            for hd in range(1, 4):
                head_norm(hd)
            dve.wait_ge(S("branches"), 9)

            for n in range(8):
                for s in range(3):
                    name = f"m2_{n}{'aab'[s]}"
                    if s != 1:
                        product_ready(dve, name)
                    dst = hidden[:, s, :] if s < 2 else silu[:, 0, :]
                    ins = dve.scalar_tensor_tensor(out=dst, in0=gates[:, 8 * s + n, :], scalar=1.0,
                                                   in1=bank(name)[:, s % 2 * T:(s % 2 + 1) * T], op0=ALU.add, op1=ALU.mult)
                    if s == 0:
                        link(ins)
                    else:
                        ins.then_inc(read_done(name), 1)
                        evacuated(dve, name)
                link(dve.tensor_tensor(hidden[:, 0, :], hidden[:, 0, :], hidden[:, 1, :], ALU.add))
                dve.tensor_tensor(merged2[:, n, :], hidden[:, 0, :], silu[:, 0, :], ALU.add).then_inc(S("merged"), 1)
                dve.wait_ge(S("merged"), 8 + n + 1)
            for j in range(4):
                lower(2, j)
            dve.wait_ge(S("tiles_used"), AT[("out2", 7)] + 1)
            for n in range(DC):
                dve.scalar_tensor_tensor(out=h[:, n, :], in0=acc[n], scalar=mhalf[:, n:n + 1], in1=h[:, n, :],
                                         op0=ALU.mult, op1=ALU.add).then_inc(S("added"), 1)
            dve.wait_ge(S("added"), 8)
            begin_feed_forward(2, "norm2", (), range(4, RING), lambda n: gmod[:, 16 + n:17 + n], "prescaled")
            ffn_conv()
            dve.wait_ge(S("tiles_used"), AT[("down3", FC - 1)] + 1)
            for n in range(DC):
                dve.scalar_tensor_tensor(out=h[:, n, :], in0=acc[n], scalar=modc[:, 40 + n, 0:1], in1=h[:, n, :],
                                         op0=ALU.mult, op1=ALU.add).then_inc(S("result_ready"), 1)

        @block.gpsimd
        def _(pool):
            pool.wait_ge(S("residual"), 16)
            pool.dma_start(ctx_raw, dram["ctx"]).then_inc(S("ctx_loaded"), 16)
            pool.memset(colr[64:P], 0.0).then_inc(S("colr_zero"), 1)

            def causal(name, n, x, d):
                pool.wait_ge(S(f"{name}_args"), n + 1)
                a = arg[:, x, 2:4, :] if d == 0 else arg[:, x, 0:2, :]
                sgn = 1 - 2 * d
                pool.affine_select(out=a, in_=a, compare_op=ALU.is_ge, fill=NEG, base=0,
                                   pattern=[[-sgn * P, 2], [sgn, T]], channel_multiplier=-sgn)\
                    .then_inc(S(f"{name}_masked"), 1)

            for i in range(8):
                causal("m", i, i % 2, i % 2)
            for hd in range(8):
                for d in range(2):
                    causal("s", 2 * hd + d, d, d)


def two_pi_parts():
    parts, rest = [], TWO_PI
    for _ in range(3):
        e = 2.0 ** (int(np.floor(np.log2(rest))) - 7)
        parts.append(float(np.floor(rest / e) * e))
        rest -= parts[-1]
    return parts + [float(np.float32(rest))]


def _chunks(a):
    return np.ascontiguousarray(np.asarray(a).reshape(-1, P).T)


def _stream(x):
    w1, w2 = x["w_in"][0], x["w_in_2"][0]
    o1 = np.cumsum([0, Q_RANK, KV_RANK, ROPE_D, 512, 512, 512, 2048])
    o2 = np.cumsum([0, 1024, 512, 512, 16, 512, 512, 512, 512, 1024, 16, 3072])
    rows = np.zeros((D, P), np.float32)
    for d in range(2):
        rows[:, ROW_I[d]:ROW_I[d] + 4] = w2[:, o2[3] + 8 * d:o2[3] + 8 * d + 4]
        rows[:, ROW_F[d]:ROW_F[d] + 4] = w2[:, o2[3] + 8 * d + 4:o2[3] + 8 * d + 8]
        rows[:, ROW_DT[d]:ROW_DT[d] + 8] = w2[:, o2[9] + 8 * d:o2[9] + 8 * d + 8]
    up = x["w_up_2"][0]
    mats = {
        "gate1": x["ffn1_w_gate"][0], "up1": x["ffn1_w_up"][0], "down1": x["ffn1_w_down"][0],
        "gate2": x["ffn2_w_gate"][0], "up2": x["ffn2_w_up"][0], "down2": x["ffn2_w_down"][0],
        "gate3": up[:, FF:], "up3": up[:, :FF], "down3": x["w_down_2"][0], "mod": x["w_mod_2"][0],
        "cq": w1[:, o1[0]:o1[1]], "ckv": w1[:, o1[1]:o1[2]], "dq": w1[:, o1[3]:o1[4]], "dk": w1[:, o1[4]:o1[5]],
        "dv": w1[:, o1[5]:o1[6]], "g1": w1[:, o1[6]:], "uk": x["w_uk"][0], "uv": x["w_uv"][0],
        "wa": x["w_branch_a"][0], "wb": x["w_branch_b"][0], "out1": x["w_out"][0],
        "rows": rows, "mq": w2[:, 0:512], "mk": w2[:, 512:1024], "mv": w2[:, o2[1]:o2[2]],
        "mo": w2[:, o2[2]:o2[3]], "aq": w2[:, o2[4]:o2[5]], "ak": w2[:, o2[5]:o2[6]], "av": w2[:, o2[6]:o2[7]],
        "sz": w2[:, o2[7]:o2[8]], "sx": w2[:, o2[8]:o2[8] + 512], "sb": w2[:, o2[8] + 512:o2[8] + 768],
        "sc": w2[:, o2[8] + 768:o2[9]], "g2": w2[:, o2[10]:], "wm": x["w_branch_m_2"][0],
        "wat": x["w_branch_a_2"][0], "ws": x["w_branch_s_2"][0], "out2": x["w_out_2"][0]}
    out = np.empty((NT, P, TILE), np.float32)
    for t, (m, kind, n) in enumerate(ORDER):
        w = mats[m]
        if kind == "cols":
            a = w[:, n * P:(n + 1) * P].reshape(DC, P, P).transpose(1, 0, 2)
        elif kind == "down":
            a = w[n * P:(n + 1) * P]
        elif kind == "wide":
            a = w[2 * n * P:2 * (n + 1) * P].reshape(2, P, 512).transpose(1, 0, 2)
        elif kind == "small":
            a = w.reshape(2, P, 512).transpose(1, 0, 2)
        else:
            a = w[:, 2 * n * P:2 * (n + 1) * P].reshape(4, P, 2, P).transpose(1, 2, 0, 3)
        out[t] = a.reshape(P, TILE)
    return out


def _vectors(x):
    vec = np.zeros((P, NVEC), np.float32)

    def put(name, a):
        vec[:a.shape[0], VEC[name]:VEC[name] + a.shape[1]] = a

    for name, src in [("ffn1_pre", "ffn1_pre_g"), ("ffn1_post", "ffn1_post_g"), ("mix_pre", "mix_pre_g"),
                      ("mix_post", "mix_post_g"), ("ffn2_pre", "ffn2_pre_g"), ("ffn2_post", "ffn2_post_g"),
                      ("bgate", "b_gate"), ("q_norm", "q_norm_g"), ("kv_norm", "kv_norm_g"), ("norm1", "norm1_g_2"),
                      ("norm2", "norm2_g_2"), ("bmod", "b_mod_2"), ("mconv", "m_conv_w_2"), ("mconv_b", "m_conv_b_2"),
                      ("mnorm", "m_norm_g_2"), ("subln", "a_subln_g_2"), ("sconv", "s_conv_w_2"),
                      ("sconv_b", "s_conv_b_2"), ("snorm", "s_norm_g_2")]:
        put(name, _chunks(x[src]))
    put("aqn", np.tile(x["a_qnorm_g_2"].reshape(64, 1), (2, 1)))
    put("akn", np.tile(x["a_knorm_g_2"].reshape(64, 1), (2, 1)))
    put("sskip", _chunks(np.repeat(x["s_d_2"].reshape(-1), 64)))
    fc = x["ffn_conv_w_2"][0].reshape(3, 2, FC, P)[:, ::-1]
    put("fconv", fc.reshape(-1, P).T)
    for d in range(2):
        vec[ROW_F[d]:ROW_F[d] + 4, VEC["row_bias"]] = x["m_fgate_b_2"][0, d]
        vec[ROW_F[d]:ROW_F[d] + 4, VEC["row_ibias"]] = x["m_igate_b_2"][0, d]
        vec[ROW_DT[d]:ROW_DT[d] + 8, VEC["row_bias"]] = x["s_dt_bias_2"][0, d]
        vec[ROW_DT[d]:ROW_DT[d] + 8, VEC["row_alog"]] = x["s_a_log_2"][0, d]
    cond = np.stack([x["c_2"].reshape(DC, P), x["c_ctx_2"].reshape(DC, P)])
    put("cond", cond.transpose(2, 1, 0).reshape(P, 2 * DC))
    return vec


def kernel(**inputs):
    import concourse.bacc as bacc
    from concourse.bass_utils import run_bass_kernel_spmd

    x = {k: np.asarray(a) for k, a in inputs.items()}
    tokens = lambda a: np.ascontiguousarray(a[0].T.reshape(DC, P, T).transpose(1, 0, 2))
    w1 = x["w_in"][0]
    kr0 = Q_RANK + KV_RANK
    arrays = {
        "stream": _stream(x), "vec": _vectors(x), "cst": table_constants(),
        "x": tokens(x["x"]), "ctx": tokens(x["ctx_2"]),
        "wuq": np.ascontiguousarray(x["w_uq"][0].reshape(3, P, 768).transpose(1, 0, 2)),
        "wkr": np.ascontiguousarray(w1[:, kr0:kr0 + ROPE_D].reshape(DC, P, ROPE_D).transpose(1, 0, 2)),
        "lam": np.ascontiguousarray(x["a_lambda_2"].reshape(-1)),
        "pos": np.ascontiguousarray(x["positions"].reshape(-1)),
    }
    nc = bacc.Bacc("TRN2", target_bir_lowering=False, num_devices=1)
    dram = {n: nc.dram_tensor(n, a.shape, I32 if n == "pos" else F32, kind="ExternalInput").ap()
            for n, a in arrays.items()}
    dram["out"] = nc.dram_tensor("out", (DC, P, T), F32, kind="ExternalOutput").ap()
    two_blocks(nc, dram)
    r = run_bass_kernel_spmd(nc, [arrays], core_ids=[0])
    got = r.results[0]["out"]
    return np.ascontiguousarray(got.reshape(1, D, T).transpose(0, 2, 1))
```

```python
from contextlib import ExitStack

import numpy as np

import concourse.bass as bass
from concourse import mybir

F32 = mybir.dt.float32
F32R = mybir.dt.float32r
I32 = mybir.dt.int32
ALU = mybir.AluOpType
ACT = mybir.ActivationFunctionType
AX_X = mybir.AxisListType.X

P = 128
T = 256
TT = 2 * T
D = 1024
DC = D // P
FF = 2816
FC = FF // P
TILE = 1024
RING = 6
EPS = 1e-6
NEG = -1e30
HEADS = 8
Q_RANK, KV_RANK, NOPE, ROPE_D = 384, 256, 64, 32
SCALE_MLA = float(NOPE + ROPE_D) ** -0.5
SCALE_64 = 64.0 ** -0.5
SCALE_M = 128.0 ** -0.5
LAM_INIT = 0.8 - 0.6
CHUNK = 64
TWO_PI = 2.0 * np.pi
MAGIC = 12582912.0


def weight_order():
    order = []

    def ffn(gate, up, down):
        order.extend([(gate, "cols", 0), (up, "cols", 0), (gate, "cols", 1), (up, "cols", 1)])
        for f in range(2, FC):
            order.extend([(down, "down", f - 2), (gate, "cols", f), (up, "cols", f)])
        order.extend([(down, "down", FC - 2), (down, "down", FC - 1)])

    ffn("gate1", "up1", "down1")
    order.extend(("cq", "cols", n) for n in range(3))
    order.extend(("ckv", "cols", n) for n in range(2))
    order.extend(("dq", "cols", n) for n in range(4))
    order.extend(("dk", "cols", n) for n in range(4))
    order.extend(("dv", "wide", n) for n in range(4))
    order.extend([("uk", "small", 0), ("uv", "small", 0)])
    order.extend(("g1", "cols", n) for n in range(16))
    for n in range(4):
        order.extend([("wa", "pair", n), ("wb", "pair", n)])
    order.extend(("out1", "cols", n) for n in range(8))
    ffn("gate2", "up2", "down2")
    order.append(("rows", "cols", 0))
    order.extend(("mk", "cols", n) for n in range(4))
    order.extend(("mq", "cols", n) for n in range(4))
    order.extend(("mv", "wide", n) for n in range(4))
    order.extend(("mo", "cols", n) for n in range(4))
    order.extend(("sx", "cols", n) for n in range(4))
    order.extend(("sb", "cols", n) for n in range(2))
    order.extend(("sc", "cols", n) for n in range(2))
    order.extend(("sz", "cols", n) for n in range(4))
    order.extend(("g2", "cols", n) for n in range(8))
    order.extend(("g2", "cols", n) for n in range(8, 16))
    order.extend(("aq", "cols", n) for n in range(4))
    order.extend(("ak", "cols", n) for n in range(4))
    order.extend(("av", "wide", n) for n in range(4))
    order.extend(("g2", "cols", n) for n in range(16, 24))
    for n in range(4):
        order.extend([("wm", "pair", n), ("wat", "pair", n), ("ws", "pair", n)])
    order.extend(("out2", "cols", n) for n in range(8))
    ffn("gate3", "up3", "down3")
    return order


ORDER = weight_order()
NT = len(ORDER)
AT = {(m, n): t for t, (m, _, n) in enumerate(ORDER)}


def columns(names):
    at, n = {}, 0
    for name, width in names:
        at[name] = n
        n += width
    return at, n


VEC, NVEC = columns([
    ("ffn1_pre", 8), ("ffn1_post", 8), ("mix_pre", 8), ("mix_post", 8), ("ffn2_pre", 8), ("ffn2_post", 8),
    ("bgate", 16), ("q_norm", 3), ("kv_norm", 2), ("norm1", 8), ("norm2", 8), ("bmod", 48),
    ("mconv", 24), ("mconv_b", 8), ("mnorm", 4), ("aqn", 1), ("akn", 1), ("subln", 1),
    ("sconv", 24), ("sconv_b", 8), ("sskip", 4), ("snorm", 4), ("fconv", 3 * 2 * FC),
    ("row_bias", 1), ("row_ibias", 1), ("row_alog", 1), ("cond", 16)])

CST, NCST = columns([
    ("ident", P), ("rot_mla", ROPE_D), ("rot_dil", P), ("rot_att", P), ("cos_att", T), ("sin_att", T),
    ("freq", 2), ("dil_bias", 2 * T), ("sign", 1), ("reset", T), ("sel_k", 32), ("sel_kt", 4 * P), ("half", 2)])

ROW_F = (0, 32)
ROW_I = (16, 48)
ROW_DT = (64, 96)


def table_constants():
    c = np.zeros((P, NCST), np.float32)
    put = lambda name, a: c.__setitem__((slice(0, a.shape[0]), slice(CST[name], CST[name] + a.shape[1])), a)
    put("ident", np.eye(P, dtype=np.float32))
    r = np.zeros((P, ROPE_D), np.float32)
    half = ROPE_D // 2
    for m in range(half):
        r[64 + m + half, m] = -1.0
        r[64 + m, m + half] = 1.0
    put("rot_mla", r)
    r = np.zeros((P, P), np.float32)
    for base in (0, 64):
        for m in range(8):
            r[base + m + 8, base + m] = -1.0
            r[base + m, base + m + 8] = 1.0
    put("rot_dil", r)
    r = np.zeros((P, P), np.float32)
    for base in range(0, P, 32):
        for m in range(16):
            r[base + m + 16, base + m] = -1.0
            r[base + m, base + m + 16] = 1.0
    put("rot_att", r)
    grid_w, freqs = 64, 16
    inv = (np.float32(10000.0) ** (-np.arange(freqs, dtype=np.float32) / freqs)).astype(np.float32)
    t = np.arange(T)
    place = np.stack([t // grid_w, t % grid_w]).astype(np.float32)
    p = np.arange(P)
    ang = place[(p % 64) // 32][:, :] * inv[p % 16][:, None]
    put("cos_att", np.cos(ang).astype(np.float32))
    put("sin_att", np.sin(ang).astype(np.float32))
    f = np.zeros((P, 2), np.float32)
    inv_m = 1.0 / (10000.0 ** (np.arange(16) / 16.0))
    f[64:80, 0] = f[80:96, 0] = inv_m
    inv_d = 1.0 / (500000.0 ** (np.arange(8) / 8.0))
    for base in (0, 64):
        f[base:base + 8, 1] = f[base + 8:base + 16, 1] = inv_d
    put("freq", f)
    i = np.arange(T)[:, None]
    j = np.arange(T)[None, :]
    count = (abs(i - j) <= 64) * 1.0 + ((i - j) % 4 == 0) * (abs(i - j) <= 256) + ((i - j) % 16 == 0)
    bias = np.where(count > 0, np.log(np.maximum(count, 1.0)), NEG).astype(np.float32)
    put("dil_bias", bias.reshape(2, P, T).transpose(1, 0, 2).reshape(P, 2 * T))
    s = np.ones((P, 1), np.float32)
    s[0:64] = -1.0
    put("sign", s)
    m = np.ones((P, T), np.float32)
    m[:96, 0::CHUNK] = 0.0
    m[96:, CHUNK - 1::CHUNK] = 0.0
    put("reset", m)
    k = np.zeros((P, 4, 8), np.float32)
    for n in range(4):
        for b in range(2):
            k[64 * b:64 * b + 64, n, 2 * n + b] = 1.0
    put("sel_k", k.reshape(P, 32))
    put("sel_kt", k.transpose(2, 1, 0).reshape(8, 4 * P))
    h = np.zeros((P, 2), np.float32)
    h[0:64, 0] = h[64:, 1] = 1.0
    put("half", h)
    return c


def regions(names, start=0):
    at, n = {}, start
    for name, width in names:
        at[name] = (n, width)
        n += width
    return at, n


MEM, END_COMMON = regions([
    ("ring", RING * TILE), ("h", DC * T), ("u", DC * TT), ("vec", NVEC), ("cst", NCST),
    ("hidden", 2 * T), ("silu", 2 * T), ("root", T), ("inv", T), ("ones", P), ("small", 448), ("modc", 96),
    ("scratch", 4096), ("gates", 24 * T)])
SPLIT_AT = MEM["gates"][0]
ARENA_1, END_1 = regions([
    ("cq", 768), ("ckv", 512), ("q", 2048), ("kh", 2048), ("qd", 1024), ("kd", 1024), ("va", 1024),
    ("vd", 1024), ("p", 1024), ("pt", 1024), ("oa", 1024), ("ob", 1024), ("merged1", 2048),
    ("tab", 1024), ("sb", 1024), ("rt", 512), ("kr", 256), ("wuq", 2304), ("wkr", 256)], END_COMMON)
ARENA_2, END_2 = regions([
    ("mq", 1024), ("mk", 2048), ("mv", 2048), ("mo", 1024), ("mst", 1536), ("ym", 1024),
    ("sx", 2048), ("sB", 1024), ("sC", 512), ("sz", 1024), ("ys", 1024), ("xdt", 4096), ("sg", 3072),
    ("t0", 512), ("tc", 1024), ("rowm", 512), ("rowl", 256)], END_COMMON)
ATT, _ = regions([("aq", 1024), ("ak", 2048), ("av", 2048), ("mo", 1024), ("ya", 1024)], ARENA_2["mq"][0])
ROWS, END_ROWS = regions([
    ("raw", 512), ("z", 512), ("sp", 512), ("da", 512), ("b", 512), ("m", 512), ("r0", 512),
    ("colr", 2048)], ARENA_2["xdt"][0])



PARTS, END_PARTS = regions([("ring_hi", RING * TILE), ("ring_lo", RING * TILE), ("u_hi", DC * T), ("u_lo", DC * T),
                            ("hidden_hi", 2 * T), ("hidden_lo", 2 * T)], 0)
assert SPLIT_AT + END_PARTS <= ARENA_1["tab"][0]
assert END_1 + DC * T <= END_2
COND_SUMS = SPLIT_AT + END_PARTS
COND_PLACES = (COND_SUMS + 3 * TILE, END_1, END_1 + TILE)
COND_SUMS_CTX = END_1 + 2 * TILE
END_ALL = COND_SUMS_CTX + 2 * TILE
assert COND_PLACES[0] + TILE <= ARENA_1["tab"][0]
COND_TURN = (5, 3)
COND_FROM = (5, 5 + DC * 5 + 3)
COND_DONE = tuple(a + DC * b for a, b in zip(COND_FROM, COND_TURN))

def tiles_between(a, b):
    return range(AT[a], AT[b] + 1)


SPLIT_TILES, SPLIT_PLACE = [], {}
for tiles, places in ((tiles_between(("cq", 0), ("dv", 3)), range(6)), (tiles_between(("g1", 0), ("g1", 15)), (4, 5)),
                      (tiles_between(("out1", 0), ("out1", 7)), (4, 5, 0, 1, 2, 3)),
                      (tiles_between(("rows", 0), ("sz", 3)), range(6)),
                      (tiles_between(("wm", 0), ("ws", 3)), range(6, 12)),
                      (tiles_between(("out2", 2), ("out2", 7)), range(6))):
    for i, t in enumerate(tiles):
        SPLIT_TILES.append(t)
        SPLIT_PLACE[t] = places[i % len(places)]
SPLIT_INDEX = {t: i for i, t in enumerate(SPLIT_TILES)}
INPUT_PARTS = {"mix_pre": 0, "merged1": DC, "ctx": 2 * DC, "norm1": 3 * DC, "merged2": 4 * DC}


LOWERS_2 = FC - 2


def gpsimd_lowers(j):
    return j >= 8 and j % 3 == 2


NORMS = ["ffn1_pre", "ffn1_post", "mix_pre", "q_norm", "kv_norm", "mix_post", "ffn2_pre", "ffn2_post",
         "ctx", "norm1", "norm2"]
NORM_AT = {name: i for i, name in enumerate(NORMS)}
SQUARES = {"q_norm": 3, "kv_norm": 2}
SQ_BASE = {name: sum(SQUARES.get(m, 4) for m in NORMS[:i]) for i, name in enumerate(NORMS)}
SCALED = ["ffn1_pre", "mix_pre", "ffn2_pre", "norm2"]
POSTS = ["ffn1_post", "mix_post", "ffn2_post"]
FFNS = ["1", "2", "3"]

BANKED = ([f"cq{n}" for n in range(3)] + [f"ckv{n}" for n in range(2)] + ["kr"]
          + [f"dq{n}" for n in range(4)] + [f"dk{n}" for n in range(4)]
          + ["rdq0", "rdq1", "rdk0", "rdk1"] + [f"uk{n}" for n in range(4)] + [f"uq{n}" for n in range(4)]
          + [f"ruq{n}" for n in range(4)] + ["rkr"] + [f"g1_{n}" for n in range(16)]
          + [f"m1_{n}" for n in range(8)]
          + ["rows"] + [f"mk{n}" for n in range(4)] + [f"mq{n}" for n in range(4)] + ["ish"]
          + [f"mo{n}" for n in range(4)] + [f"sx{n}" for n in range(4)] + [f"sb{n}" for n in range(2)]
          + [f"sc{n}" for n in range(2)] + [f"sz{n}" for n in range(4)] + [f"g2_{n}" for n in range(16)]
          + [f"aq{n}" for n in range(4)] + [f"ak{n}" for n in range(4)]
          + ["krow", "rq", "g2_16", "kb0", "kb1", "kb2", "kb3", "raq0", "raq1", "rak0", "rak1"]
          + [f"g2_{n}" for n in range(17, 24)]
          + [f"m2_{n}{s}" for n in range(8) for s in "ab"])
BANK_AT = {name: i for i, name in enumerate(BANKED)}
SMALL = ["kr", "rdq0", "rdq1", "rdk0", "rdk1", "uk0", "uk1", "uk2"] + [f"uq{n}" for n in range(4)] + [
    f"ruq{n}" for n in range(4)] + ["rkr"] + [f"m1_{n}" for n in (0, 2, 4, 6)] + [
    "ish", "krow", "rq", "kb0", "kb1", "kb2", "kb3", "raq0", "raq1", "rak0", "rak1"] + [
    f"m2_{n}a" for n in range(0, 8)] + [f"m2_{n}b" for n in (0, 2, 4, 6)]
SMALL.sort(key=lambda n: BANK_AT[n])
SMALL_AT = {name: i for i, name in enumerate(SMALL)}
CONV = ([("mk", n, 4 + n) for n in range(4)] + [("mq", n, n) for n in range(4)]
        + [("sx", n, n) for n in range(4)] + [("sb", n, 4 + n) for n in range(2)]
        + [("sc", n, 6 + n) for n in range(2)])


def tile_of(name):
    for m in ("g1_", "g2_"):
        if name.startswith(m):
            return AT[(m[:2], int(name[3:]))]
    if name == "uk3":
        return AT[("uk", 0)]
    if name.startswith("m1_"):
        return AT[("wb", int(name[3:]) // 2)]
    if name.startswith("m2_"):
        return AT[("ws", int(name[3]) // 2)]
    if name == "rows":
        return AT[("rows", 0)]
    return AT[(name.rstrip("0123456789"), int(name[len(name.rstrip("0123456789")):]))]


def two_blocks(nc, dram):
    with ExitStack() as ctx:
        start = -(-nc.sbuf_base // 32) * 32
        low = ctx.enter_context(nc.sbuf_tensor("low", [P, SPLIT_AT], F32))
        high = ctx.enter_context(nc.sbuf_tensor("high", [P, END_ALL - SPLIT_AT], F32))
        parts = nc.alloc_sbuf_tensor_at("parts", [P, END_PARTS], F32R, offset=start + 4 * SPLIT_AT)
        psum = ctx.enter_context(nc.psum_tensor("psum", [P, 8, 512], F32))
        sems = {}

        def S(name):
            if name not in sems:
                sems[name] = ctx.enter_context(nc.semaphore(name))
            return sems[name]

        def place(at, width):
            if at < SPLIT_AT:
                return low[:, at:at + width]
            return high[:, at - SPLIT_AT:at - SPLIT_AT + width]

        def view(table, name, n=None, m=None):
            at, width = table[name]
            v = place(at, width)
            if m is not None:
                return v.rearrange("p (a b c) -> p a b c", a=n, b=m)
            return v if n is None else v.rearrange("p (a b) -> p a b", a=n)

        ring = view(MEM, "ring", RING)
        cond_places = [place(at, TILE) for at in COND_PLACES]
        cond_sums = [place(COND_SUMS + g * TILE, TILE) for g in range(3)]
        cond_sums_ctx = [place(COND_SUMS_CTX + g * TILE, TILE) for g in range(2)]
        h = view(MEM, "h", DC)
        u1 = place(MEM["u"][0], DC * T).rearrange("p (a b) -> p a b", a=DC)
        u2 = view(MEM, "u", DC)
        vec = view(MEM, "vec")
        cst = view(MEM, "cst")
        gates = view(MEM, "gates", 24)
        ctx_raw = place(ROWS["colr"][0] - DC * T, DC * T).rearrange("p (a b) -> p a b", a=DC)
        hidden = view(MEM, "hidden", 2)
        silu = view(MEM, "silu", 2)
        own_parts = nc.alloc_sbuf_tensor_at("own_parts", [P, RING * TILE], F32R, offset=start + 4 * MEM["ring"][0])
        u_parts = nc.alloc_sbuf_tensor_at("u_parts", [P, DC * TT], F32R, offset=start + 4 * MEM["u"][0])
        scratch_parts = nc.alloc_sbuf_tensor_at("scratch_parts", [P, DC * TT], F32R, offset=start + 4 * MEM["scratch"][0])
        late_parts = nc.alloc_sbuf_tensor_at("late_parts", [P, DC * T], F32R, offset=start + 4 * END_1)
        tile_lo = own_parts[:, :].rearrange("p (a b) -> p a b", a=RING)
        upper_places = parts[:, 0:12 * TILE].rearrange("p (a b) -> p a b", a=12)
        branch_parts = nc.alloc_sbuf_tensor_at("branch_parts", [P, 6 * 4 * T], F32R,
                                               offset=start + 4 * ARENA_2["xdt"][0])
        bp = branch_parts[:, :].rearrange("p (b x c t) -> p b x c t", b=3, x=2, c=4)
        p1_hi = u_parts[:, DC * T:2 * DC * T].rearrange("p (a b) -> p a b", a=DC)
        p1_lo = late_parts[:, :].rearrange("p (a b) -> p a b", a=DC)
        p2_hi = scratch_parts[:, :].rearrange("p (s c t) -> p c s t", s=2, c=DC)
        p2_lo = u_parts[:, :].rearrange("p (c s t) -> p c s t", c=DC, s=2)

        ring_hi, ring_lo, u_hi, u_lo, hidden_hi, hidden_lo = (
            parts[:, a:a + width].rearrange("p (a b) -> p a b", a=n)
            for (a, width), n in zip(PARTS.values(), (RING, RING, DC, DC, 2, 2)))
        root = view(MEM, "root")
        inv = view(MEM, "inv")
        ones = view(MEM, "ones")
        small = view(MEM, "small")
        modc = view(MEM, "modc", 48)
        sq = place(MEM["scratch"][0], 2048).rearrange("p (a b) -> p a b", a=DC)
        tmp = place(MEM["scratch"][0] + 2048, 2048).rearrange("p (a b) -> p a b", a=DC)
        cond = small[:, 0:16].rearrange("p (c b) -> p c b", b=2)
        bhalf = small[:, 16:32]
        negmax = small[:, 32:48]
        den = small[:, 48:64]
        rden = small[:, 64:80]
        gmod = small[:, 80:104]
        row_bias = small[:, 104:105]
        row_coef = small[:, 105:106]
        lam = small[:, 106:112]
        g_half = small[:, 112:116]
        g_sub = small[:, 116:117]
        rq = small[:, 120:136]
        dmax = small[:, 136:144]
        bh2 = small[:, 160:184]
        mhalf = small[:, 144:152]
        lam_p = small[:, 184:440]
        eps = small[:, 440:441]
        row_exp = small[:, 441:442]
        ident = cst[:, CST["ident"]:CST["ident"] + P]

        def c(name, width, a=0, b=P):
            return cst[a:b, CST[name]:CST[name] + width]

        def v(name, i=0, a=0, b=P):
            return vec[a:b, VEC[name] + i:VEC[name] + i + 1]

        def half_bank(b, n):
            return psum[:, b, n * T:(n + 1) * T]

        acc = [half_bank(n // 2, n % 2) for n in range(DC)]
        PJ = (4, 5)
        SUMS, MOD = 6, 7

        A1 = lambda name, *n: view(ARENA_1, name, *n)
        A2 = lambda name, *n: view(ARENA_2, name, *n)
        cq, ckv, kr = A1("cq", 3), A1("ckv", 2), A1("kr")
        wuq, wkr = A1("wuq", 3), A1("wkr", 8)
        q, kh, qd, kd = A1("q", 8), A1("kh", 8), A1("qd", 4), A1("kd", 4)
        va, vd = A1("va", 2), A1("vd", 2)
        prob, probt = A1("p", 2, 2), A1("pt", 2, 2)
        oa, ob, tab, sbias, rt = A1("oa", 4), A1("ob", 4), A1("tab", 4), A1("sb", 2, 2), A1("rt")
        merged1 = A1("merged1", 8)
        merged2 = tmp
        sq_late = place(END_1, DC * T).rearrange("p (a b) -> p a b", a=DC)
        mq, mk, mv, mo = A2("mq", 4), A2("mk", 4), A2("mv", 4), A2("mo", 4)
        mst, ym = A2("mst", 6), A2("ym", 4)
        sx, sB, sC, sz, ys = A2("sx", 4), A2("sB", 2), A2("sC", 2), A2("sz", 4), A2("ys", 4)
        xdt = A2("xdt").rearrange("p (d s f) -> p d s f", d=2, s=4)
        sg = A2("sg").rearrange("p (g s t) -> p g s t", g=2, s=6)
        t0, tc = A2("t0", 4), A2("tc").rearrange("p (j s r) -> p j s r", j=4, s=4)
        rowm, rowl = A2("rowm", 2), A2("rowl")
        conv_dst = {"mk": mk, "mq": mq, "sx": sx, "sb": sB, "sc": sC}
        aq, ak, av, ya = (view(ATT, n, 4) for n in ("aq", "ak", "av", "ya"))
        raw, z, sp, da, bsum, mrow, r0 = (view(ROWS, n) for n in ("raw", "z", "sp", "da", "b", "m", "r0"))
        colr = view(ROWS, "colr", 4)
        sc0 = MEM["scratch"][0]
        arg = low[:, sc0:sc0 + 2048].rearrange("p (x s t) -> p x s t", x=2, s=4)
        wgt = low[:, sc0 + 2048:sc0 + 4096].rearrange("p (x s t) -> p x s t", x=2, s=4)
        prob2 = low[:, sc0:sc0 + 2048].rearrange("p (x b k) -> p x b k", x=2, b=2)
        probt2 = low[:, sc0 + 2048:sc0 + 3072].rearrange("p (x s t) -> p x s t", x=2, s=4)
        sqa = low[:, sc0:sc0 + 2048].rearrange("p (a b) -> p a b", a=4)
        sqq = low[:, sc0 + 2048:sc0 + 3072].rearrange("p (a b) -> p a b", a=4)
        krow_r = low[0:8, sc0 + 3072:sc0 + 3584]
        krow_i = low[0:8, sc0 + 3584:sc0 + 4096]
        pos_i = A1("kr").bitcast(I32)
        ang = A1("sb", 2, 2)
        posf = rt[:, 0:T]
        cg, ca = (place(ARENA_2["sz"][0] + n * TT, TT).rearrange("p (a b) -> p a b", a=2)
                  for n in range(2))

        def bank_free(eng, name):
            i = BANK_AT[name]
            if i >= 2:
                eng.wait_ge(S(f"bank{i % 2}_read"), i // 2)

        def product_ready(eng, name):
            if name in SMALL_AT:
                eng.wait_ge(S("small_products"), SMALL_AT[name] + 1)
            else:
                eng.wait_ge(S("tiles_used"), tile_of(name) + 1)

        def evacuated(eng, *names):
            for name in names:
                i = BANK_AT[name]
                eng.wait_ge(S(f"bank{i % 2}_read"), i // 2 + 1)

        def bank(name):
            return psum[:, PJ[BANK_AT[name] % 2], :]

        def read_done(name):
            return S(f"bank{BANK_AT[name] % 2}_read")

        block = ctx.enter_context(nc.Block())

        @block.sync
        def _(sp_):
            sp_.dma_start(h, dram["x"]).then_inc(S("x_loaded"), 16)
            for s in range(RING):
                sp_.dma_start(ring[:, s, :], dram["stream"][s]).then_inc(S(f"slot{s}_loaded"), 16)
            with sp_.Fori(1, NT // RING) as i:
                for s in range(RING):
                    sp_.wait_ge(S("tiles_used"), (i - 1) * RING + s + 1)
                    sp_.dma_start(ring[:, s, :], dram["stream"][bass.ds(i * RING + s, 1)].rearrange("a p n -> (a p) n"))\
                       .then_inc(S(f"slot{s}_loaded"), 16)
            for t in range(NT // RING * RING, NT):
                sp_.wait_ge(S("tiles_used"), t - RING + 1)
                sp_.dma_start(ring[:, t % RING, :], dram["stream"][t]).then_inc(S(f"slot{t % RING}_loaded"), 16)
            for n in range(DC):
                sp_.wait_ge(S("result_ready"), n + 1)
                sp_.dma_start(dram["out"][n], h[:, n, :]).then_inc(S("stored"), 16)
            sp_.wait_ge(S("stored"), 16 * DC)

        @block.tensor
        def _(pe):
            def tile_wait(t, more=0):
                pe.wait_ge(S(f"slot{t % RING}_loaded"), more * 16 + 16 * (t // RING + 1))
                return ring[:, t % RING, :]

            def cols(t, out, rhs, more=0, chunk_ready=lambda k: None):
                w = tile_wait(t, more)
                for k in range(DC):
                    chunk_ready(k)
                    mm = pe.matmul(out, w[:, k * P:(k + 1) * P], rhs(k), start=k == 0, stop=k == DC - 1)
                mm.then_inc(S("tiles_used"), 1)

            def split_weights(t):
                pe.wait_ge(S("weights_split"), SPLIT_INDEX[t] + 1)
                return upper_places[:, SPLIT_PLACE[t], :], tile_lo[:, t % RING, :]

            def split_cols(t, out, hi, lo, chunk_ready=lambda k: None):
                w = split_weights(t)
                for k in range(DC):
                    chunk_ready(k)
                    mm = split_product(out, w, slice(k * P, (k + 1) * P), (hi(k), lo(k)), k == 0, k == DC - 1)
                mm.then_inc(S("tiles_used"), 1)

            def split_tile(k, j, more=0):
                if not isinstance(more, int):
                    j, more = j + RING, more - 1
                if gpsimd_lowers(j):
                    pe.wait_ge(S("lower_ready_2"), more * 2 + (LOWERS_2 * k + (j - 8) // 3 + 1))
                else:
                    pe.wait_ge(S("lower_ready"), more * 4 + ((3 * FC - LOWERS_2) * k + j + 1 - max(0, (j - 8) // 3 + 1)))
                return ring_hi[:, j % RING, :], ring_lo[:, j % RING, :]

            def split_product(out, w, cols_, x, start, stop, **kw):
                (w_hi, w_lo), (x_hi, x_lo) = w, x
                pe.matmul(out, w_hi[:, cols_], x_hi, start=start, stop=False, **kw)
                pe.matmul(out, w_hi[:, cols_], x_lo, start=False, stop=False, **kw)
                return pe.matmul(out, w_lo[:, cols_], x_hi, start=False, stop=stop, **kw)

            def split_wide(name, toks, hi, lo, banks):
                for kk in range(4):
                    w_hi, w_lo = split_weights(AT[(name, kk)])
                    for n in range(toks):
                        for j in range(2):
                            k, cols_ = 2 * kk + j, slice(j * 512, (j + 1) * 512)
                            out = psum[:, banks[n], :]
                            pe.matmul(out, hi(k, n), w_hi[:, cols_], start=k == 0, stop=False)
                            pe.matmul(out, hi(k, n), w_lo[:, cols_], start=False, stop=False)
                            mm = pe.matmul(out, lo(k, n), w_hi[:, cols_], start=False, stop=k == DC - 1)
                    mm.then_inc(S("tiles_used"), 1)

            def sums(name, chunk, n):
                i = NORM_AT[name]
                if i:
                    pe.wait_ge(S("roots"), i)
                for k in range(n):
                    step = k if name in SQUARES else k // 2
                    pe.wait_ge(S("squares"), SQ_BASE[name] + step + 1)
                    mm = pe.matmul(half_bank(SUMS, 0), ones, chunk(k), start=k == 0, stop=k == n - 1)
                mm.then_inc(S("sums"), 1)

            def sums_wide(name, squared=sq):
                sums(name, lambda k: squared[:, k, :], DC)

            def ffn(k):
                base = FC * k

                def gate_up(par, t, more=0, hid=None):
                    if hid is not None:
                        pe.wait_ge(S("hidden_ready"), hid)
                    for a in range(2):
                        w = split_tile(k, t + a, more)
                        for c_ in range(DC):
                            if t < 2:
                                pe.wait_ge(S("input_split"), DC * k + c_ + 1)
                            mm = split_product(half_bank(PJ[par], a), w, slice(c_ * P, (c_ + 1) * P),
                                               (u_hi[:, c_, :], u_lo[:, c_, :]),
                                               c_ == 0, c_ == DC - 1)
                        mm.then_inc(S("tiles_used"), 1)

                def down(par, t, hid, first, last, more=0):
                    w = split_tile(k, t, more)
                    pe.wait_ge(S("hidden_split"), hid)
                    for n in range(DC):
                        mm = split_product(acc[n], w, slice(n * P, (n + 1) * P),
                                           (hidden_hi[:, par, :], hidden_lo[:, par, :]),
                                           first and n % 2 == 0, last, skip_group_check=True)
                    mm.then_inc(S("tiles_used"), 1)

                for par in range(2):
                    gate_up(par, 2 * par)
                if k == 1:
                    pe.wait_ge(S("residual"), 16)
                if k == 2:
                    pe.wait_ge(S("added"), 8)
                down(0, 4, base + 1, True, False)
                gate_up(0, 5, hid=base + 1)
                down(1, 7, base + 2, False, False)
                gate_up(1, 8, hid=base + 2)
                with pe.Fori(1, FC // 2 - 1) as i:
                    down(0, 4, i * 2 + (base + 1), False, False, i)
                    gate_up(0, 5, i, i * 2 + (base + 1))
                    down(1, 7, i * 2 + (base + 2), False, False, i)
                    gate_up(1, 8, i, i * 2 + (base + 2))
                down(0, 3 * FC - 2, base + FC - 1, False, False)
                down(1, 3 * FC - 1, base + FC, False, True)

            def modulation(k, who):
                pe.wait_ge(S("cond_steps"), COND_DONE[k])
                for g in range(2 if who else 3):
                    for i in range(DC):
                        col = 2 * (24 * k + DC * g + i) + who
                        mm = pe.matmul(psum[:, MOD, col:col + 1], (cond_sums_ctx if who else cond_sums)[g][:, i * P:(i + 1) * P],
                                       ones[:, 0:1], start=True, stop=True)
                mm.then_inc(S("cond_products"), 1)

            def wide(name, toks, lhs, banks):
                for kk in range(4):
                    w = tile_wait(AT[(name, kk)])
                    for n in range(toks):
                        for j in range(2):
                            mm = pe.matmul(psum[:, banks[n], :], lhs(2 * kk + j, n), w[:, j * 512:(j + 1) * 512],
                                           start=kk + j == 0, stop=kk + j == 4)
                    mm.then_inc(S("tiles_used"), 1)

            pe.wait_ge(S("ones_ready"), 1)
            sums_wide("ffn1_pre")
            ffn(0)
            sums_wide("ffn1_post")
            pe.wait_ge(S("tables_loaded"), 48)
            modulation(0, 0)
            sums_wide("mix_pre")

            u1k = lambda k: u1[:, k, :]

            def project(name, out=None, rhs=u1k, **kw):
                bank_free(pe, name)
                cols(tile_of(name), bank(name)[:, 0:T] if out is None else out, rhs, **kw)

            def split_project(name, out=None, hi=lambda k: p1_hi[:, k, :], lo=lambda k: p1_lo[:, k, :], **kw):
                bank_free(pe, name)
                split_cols(tile_of(name), bank(name)[:, 0:T] if out is None else out, hi, lo, **kw)

            for n in range(3):
                split_project(f"cq{n}", chunk_ready=lambda k: pe.wait_ge(S("input_parts"), INPUT_PARTS["mix_pre"] + k + 1))
            for n in range(2):
                split_project(f"ckv{n}")
            bank_free(pe, "kr")
            pe.wait_ge(S("small_weights"), 32)
            for k in range(DC):
                mm = pe.matmul(bank("kr")[64:96, 0:T], wkr[:, k, :], u1[:, k, :], start=k == 0, stop=k == DC - 1)
            mm.then_inc(S("small_products"), 1)
            sums("q_norm", lambda k: sq[:, k, :], 3)
            for n in range(4):
                split_project(f"dq{n}")
            sums("kv_norm", lambda k: sq[:, 3 + k, :], 2)
            for n in range(4):
                split_project(f"dk{n}")
            pe.wait_ge(S("residual"), 8)
            split_wide("dv", 2, lambda k, n: p1_hi[:, k, n * P:(n + 1) * P], lambda k, n: p1_lo[:, k, n * P:(n + 1) * P],
                       (0, 1))
            for n, (x, name) in enumerate([(qd, "rdq0"), (qd, "rdq1"), (kd, "rdk0"), (kd, "rdk1")]):
                bank_free(pe, name)
                evacuated(pe, *(f"{name[1:3]}{2 * (n % 2) + a}" for a in range(2)))
                pe.matmul(bank(name), c("rot_dil", P), x[:, 2 * (n % 2):2 * (n % 2) + 2, :],
                          start=True, stop=True).then_inc(S("small_products"), 1)
            w = tile_wait(AT[("uk", 0)])
            pe.wait_ge(S("kv_scaled"), 2)
            for n in range(4):
                bank_free(pe, f"uk{n}")
                for a in range(2):
                    hd = 2 * n + a
                    for k in range(2):
                        mm = pe.matmul(bank(f"uk{n}")[0:64, a * T:(a + 1) * T],
                                       w[:, k * 512 + hd * 64:k * 512 + (hd + 1) * 64], ckv[:, k, :],
                                       start=k == 0, stop=k == 1)
                mm.then_inc(S("tiles_used" if n == 3 else "small_products"), 1)
            w = tile_wait(AT[("uv", 0)])
            for n in range(2):
                for k in range(2):
                    mm = pe.matmul(psum[:, 2 + n, :], ckv[:, k, n * P:(n + 1) * P], w[:, k * 512:(k + 1) * 512],
                                   start=k == 0, stop=k == 1)
            mm.then_inc(S("tiles_used"), 1)
            pe.wait_ge(S("q_scaled"), 3)
            for n in range(4):
                bank_free(pe, f"uq{n}")
                for a in range(2):
                    hd = 2 * n + a
                    for k in range(3):
                        mm = pe.matmul(bank(f"uq{n}")[0:96, a * T:(a + 1) * T], wuq[:, k, hd * 96:(hd + 1) * 96],
                                       cq[:, k, :], start=k == 0, stop=k == 2)
                mm.then_inc(S("small_products"), 1)
            for n in range(4):
                bank_free(pe, f"ruq{n}")
                evacuated(pe, f"uq{n}")
                pe.matmul(bank(f"ruq{n}")[64:96, :], c("rot_mla", ROPE_D, 64, 96), q[64:96, 2 * n:2 * n + 2, :],
                          start=True, stop=True).then_inc(S("small_products"), 1)
            bank_free(pe, "rkr")
            pe.matmul(bank("rkr")[64:96, 0:T], c("rot_mla", ROPE_D, 64, 96), kr[64:96, :],
                      start=True, stop=True).then_inc(S("small_products"), 1)

            def scores(k):
                if k == 0:
                    pe.wait_ge(S("vd_copied"), 2)
                    pe.wait_ge(S("dil_roped"), 4)
                if k == 8:
                    pe.wait_ge(S("mla_roped"), 5)
                if k >= 2:
                    pe.wait_ge(S("exps"), 2 * (k - 1))
                for j in range(2):
                    if k < 8:
                        r = slice(64 * (k % 2), 64 * (k % 2) + 64)
                        a, b = qd[r, k // 2, j * P:(j + 1) * P], kd[r, k // 2, :]
                    else:
                        a, b = q[0:96, k - 8, j * P:(j + 1) * P], kh[0:96, k - 8, :]
                    mm = pe.matmul(psum[:, k % 2, j * T:(j + 1) * T], a, b, start=True, stop=True)
                mm.then_inc(S("scores"), 1)

            def turn(k):
                pe.wait_ge(S("probs"), 2 * k + 2)
                if k >= 2:
                    pe.wait_ge(S("turned_copied"), k - 1)
                else:
                    pe.wait_ge(S("va_copied"), 2)
                for s in range(2):
                    for j in range(2):
                        mm = pe.transpose(psum[:, 2 + k % 2, s * T + j * P:s * T + (j + 1) * P],
                                          prob[:, k % 2, j, s * P:(s + 1) * P], ident)
                mm.then_inc(S("turned"), 1)

            def values(k):
                pe.wait_ge(S("turned_copied"), k + 1)
                if k >= 2:
                    pe.wait_ge(S("outs_copied"), k - 1)
                elif k == 1:
                    pe.wait_ge(S("mod_ready"), 1)
                else:
                    pe.wait_ge(S("roots"), NORM_AT["kv_norm"] + 1)
                x, hd = (vd, k) if k < 8 else (va, k - 8)
                r = 64 * (k % 2)
                for s in range(2):
                    mm = pe.matmul(psum[r:r + 64, 6 + k % 2, 0:T], x[:, s, hd * 64:(hd + 1) * 64],
                                   probt[:, k % 2, s, :], start=s == 0, stop=s == 1)
                mm.then_inc(S("outs"), 1)

            scores(0)
            for k in range(16):
                if k < 15:
                    scores(k + 1)
                split_project(f"g1_{k}")
                turn(k)
                if k:
                    values(k - 1)
            values(15)

            for n in range(8):
                name = f"m1_{n}"
                bank_free(pe, name)
                for s, (m, o, last) in enumerate([("wa", oa, n % 2), ("wb", ob, n % 2)]):
                    w = tile_wait(AT[(m, n // 2)])
                    if n == 0 and s == 0:
                        pe.wait_ge(S("outs_copied"), 16)
                    for k in range(4):
                        mm = pe.matmul(bank(name)[:, s * T:(s + 1) * T],
                                       w[:, (n % 2 * 4 + k) * P:(n % 2 * 4 + k + 1) * P], o[:, k, :],
                                       start=k == 0, stop=k == 3)
                    if last:
                        mm.then_inc(S("tiles_used"), 1)
                if not n % 2:
                    mm.then_inc(S("small_products"), 1)
            pe.wait_ge(S("turned_copied"), 16)
            for n in range(8):
                split_cols(AT[("out1", n)], acc[n], lambda k: p1_hi[:, k, :], lambda k: p1_lo[:, k, :],
                           lambda k: pe.wait_ge(S("input_parts"), INPUT_PARTS["merged1"] + k + 1))
            sums_wide("mix_post")
            pe.wait_ge(S("outs_copied"), 16)
            modulation(0, 1)
            sums_wide("ffn2_pre")

            ffn(1)
            sums_wide("ffn2_post")
            sums_wide("ctx")
            pe.wait_ge(S("mod_ready"), 2)
            modulation(1, 0)
            sums_wide("norm1", sq_late)

            both = lambda k: u2[:, k, :]
            lat = lambda k: u2[:, k, T:TT]
            both_parts = (lambda k: p2_hi[:, k], lambda k: p2_lo[:, k])
            lat_parts = (lambda k: p2_hi[:, k, 1], lambda k: p2_lo[:, k, 1])
            split_project("rows", bank("rows"), *both_parts,
                          chunk_ready=lambda k: pe.wait_ge(S("input_parts"), INPUT_PARTS["norm1"] + k + 1))
            for n in range(4):
                split_project(f"mk{n}", bank(f"mk{n}"), *both_parts)
            for n in range(4):
                split_project(f"mq{n}", None, *lat_parts)
            bank_free(pe, "ish")
            evacuated(pe, "rows")
            pe.matmul(bank("ish")[0:64, :], ident[:, 16:80], raw[:, :], start=True, stop=True)\
              .then_inc(S("small_products"), 1)
            pe.wait_ge(S("residual"), 24)
            split_wide("mv", 4, lambda k, n: p2_hi[:, k, n // 2, n % 2 * P:(n % 2 + 1) * P],
                       lambda k, n: p2_lo[:, k, n // 2, n % 2 * P:(n % 2 + 1) * P], (0, 1, 2, 3))
            for n in range(4):
                split_project(f"mo{n}", None, *lat_parts)
            for n in range(4):
                split_project(f"sx{n}", bank(f"sx{n}"), *both_parts)
            for n in range(2):
                split_project(f"sb{n}", bank(f"sb{n}"), *both_parts)
            for n in range(2):
                split_project(f"sc{n}", None, *lat_parts)
            pe.wait_ge(S("mv_copied"), 4)
            pe.wait_ge(S("cols_in"), 1)
            for s in range(4):
                mm = pe.transpose(psum[:, 0, s * P:(s + 1) * P], r0[:, s * P:(s + 1) * P], ident)
            mm.then_inc(S("cols_turned"), 1)
            pe.wait_ge(S("cols_in"), 2)
            for j in range(4):
                for s in range(4):
                    i = 4 * j + s
                    mm = pe.transpose(psum[:, 1 + i // 8, i % 8 * 64:i % 8 * 64 + 64],
                                      colr[64:P, j, s * P:(s + 1) * P], ident[64:P, 64:P])
            mm.then_inc(S("cols_turned"), 1)
            for n in range(4):
                split_project(f"sz{n}", None, *lat_parts)

            def m_scores(hd):
                if hd == 0:
                    pe.wait_ge(S("conv_done"), 8)
                    pe.wait_ge(S("cols_copied"), 3)
                else:
                    pe.wait_ge(S("m_scores_copied"), hd)
                for s in range(4):
                    mm = pe.matmul(psum[:, 2 + s // 2, s % 2 * T:(s % 2 + 1) * T], mk[:, hd, s * P:(s + 1) * P],
                                   mq[:, hd, :], start=True, stop=True)
                mm.then_inc(S("m_scores"), 1)

            def m_rows(i):
                hd, d = i // 2, i % 2
                if i >= 2:
                    pe.wait_ge(S("m_floor"), i - 1)
                row = 32 * d + hd
                for x in range(2):
                    mm = pe.matmul(psum[:, i % 2, x * T:(x + 1) * T], ident[0:64, row:row + 1].broadcast_to([64, P]),
                                   rowm[0:64, x, :], start=True, stop=True)
                mm.then_inc(S("m_rows"), 1)

            def m_sums(i):
                hd, d = i // 2, i % 2
                pe.wait_ge(S("m_weights"), i + 1)
                if i >= 2:
                    pe.wait_ge(S("m_out"), i - 1)
                for x in range(2):
                    for s in range(4):
                        blk = (s + 2 * d) % 4
                        lhs = ones if x else mv[:, blk, hd * P:(hd + 1) * P]
                        mm = pe.matmul(psum[:, 6 + i % 2, x * T:(x + 1) * T], lhs, wgt[:, i % 2, s, :],
                                       start=s == 0, stop=s == 3)
                mm.then_inc(S("m_sums"), 1)

            m_scores(0)
            m_rows(0)
            for i in range(8):
                if i < 7:
                    m_rows(i + 1)
                if i % 2 == 1 and i < 7:
                    m_scores(i // 2 + 1)
                if i == 0:
                    pe.wait_ge(S("input_whole"), 1)
                project(f"g2_{i}", None, lat)
                m_sums(i)

            pe.wait_ge(S("m_scores_copied"), 4)
            pe.wait_ge(S("conv_done"), 16)
            for g in range(2):
                if g:
                    pe.wait_ge(S("sg_copied"), 1)
                for s in range(4):
                    mm = pe.matmul(psum[:, 2 + s // 2, s % 2 * T:(s % 2 + 1) * T], sB[:, g, s * P:(s + 1) * P],
                                   sC[:, g, :], start=True, stop=True)
                mm.then_inc(S("sg_ready"), 1)
            pe.wait_ge(S("m_floor"), 8)
            for s in range(4):
                if s >= 2:
                    pe.wait_ge(S("xdt_ready"), 2 * (s - 1))
                for f in range(4):
                    mm = pe.transpose(psum[:, s % 2, f * P:(f + 1) * P], sx[:, f, s * P:(s + 1) * P], ident)
                mm.then_inc(S("x_turned"), 1)

            def s_rows(hd):
                if hd < 2:
                    pe.wait_ge(S("xdt_ready"), 8)
                else:
                    pe.wait_ge(S("s_args"), 2 * (hd - 1))
                for d in range(2):
                    row = 32 * d + hd
                    mm = pe.matmul(psum[:, hd % 2, d * T:(d + 1) * T],
                                   ident[64:P, 64 + row:65 + row].broadcast_to([64, P]), rowl[64:P, :],
                                   start=True, stop=True)
                mm.then_inc(S("s_rows"), 1)

            def s_sums(hd):
                r = 64 * (hd % 2)
                if hd >= 2:
                    pe.wait_ge(S("s_out"), hd - 1)
                else:
                    pe.wait_ge(S("m_out"), 7 + hd)
                for d in range(2):
                    pe.wait_ge(S("s_weights"), 2 * hd + d + 1)
                    for s in range(4):
                        blk = (s + 2 * d) % 4
                        mm = pe.matmul(psum[r:r + 64, 6 + hd % 2, 0:T], xdt[:, d, blk, hd * 64:(hd + 1) * 64],
                                       wgt[:, d, s, :], start=d == 0 and s == 0, stop=d == 1 and s == 3)
                mm.then_inc(S("s_sums"), 1)

            s_rows(0)
            for hd in range(8):
                if hd < 7:
                    s_rows(hd + 1)
                project(f"g2_{8 + hd}", None, lat)
                s_sums(hd)

            def memory_sums():
                pe.wait_ge(S("branch_squares"), 1)
                for hd in range(4):
                    mm = pe.matmul(psum[:, 2 + hd // 2, hd % 2 * T:(hd % 2 + 1) * T], ones, sq[:, hd, :],
                                   start=True, stop=True)
                mm.then_inc(S("branch_sums"), 1)

            def space_sums():
                pe.wait_ge(S("branch_squares"), 2)
                for f in range(4):
                    mm = pe.matmul(psum[:, 6, f // 2 * T:(f // 2 + 1) * T], ones, tmp[:, f, :],
                                   start=f % 2 == 0, stop=f % 2 == 1)
                mm.then_inc(S("branch_sums"), 1)

            for n in range(4):
                project(f"aq{n}", None, lat)
                if n == 1:
                    memory_sums()
                elif n == 2:
                    space_sums()
            for n in range(4):
                project(f"ak{n}", bank(f"ak{n}"), both)
            pe.wait_ge(S("s_args"), 16)
            pe.wait_ge(S("sg_copied"), 2)
            wide("av", 4, lambda k, n: u2[:, k, n * P:(n + 1) * P], (0, 1, 2, 3))
            bank_free(pe, "krow")
            pe.wait_ge(S("a_squares"), 2)
            for n in range(4):
                mm = pe.matmul(bank("krow")[0:8, :], c("sel_k", 32)[:, 8 * n:8 * n + 8], sqa[:, n, :],
                               start=n == 0, stop=n == 3)
            mm.then_inc(S("small_products"), 1)
            bank_free(pe, "rq")
            for hd in range(4):
                for j in range(2):
                    i = 2 * hd + j
                    mm = pe.matmul(bank("rq")[:, 2 * i:2 * i + 2], sqq[:, hd, j * P:(j + 1) * P], c("half", 2),
                                   start=True, stop=True)
            mm.then_inc(S("small_products"), 1)
            project("g2_16", None, lat)
            pe.wait_ge(S("k_inverse"), 1)
            for n in range(4):
                bank_free(pe, f"kb{n}")
                pe.matmul(bank(f"kb{n}"), cst[0:8, CST["sel_kt"] + n * P:CST["sel_kt"] + (n + 1) * P], krow_i,
                          start=True, stop=True).then_inc(S("small_products"), 1)
            for n in range(2):
                bank_free(pe, f"raq{n}")
                pe.wait_ge(S("aq_scaled"), 1)
                pe.matmul(bank(f"raq{n}"), c("rot_att", P), aq[:, 2 * n:2 * n + 2, :], start=True, stop=True)\
                  .then_inc(S("small_products"), 1)
            for n in range(2):
                bank_free(pe, f"rak{n}")
                evacuated(pe, "kb2", "kb3")
                pe.matmul(bank(f"rak{n}"), c("rot_att", P), ak[:, 2 * n:2 * n + 2, T:TT], start=True, stop=True)\
                  .then_inc(S("small_products"), 1)

            def a_scores(i):
                hd, j = i // 2, i % 2
                if i < 2:
                    pe.wait_ge(S("att_roped"), 4)
                    pe.wait_ge(S("av_copied"), 4)
                    pe.wait_ge(S("s_out"), 8)
                else:
                    pe.wait_ge(S("a_exps"), 2 * (i - 1))
                for b in range(2):
                    mm = pe.matmul(psum[:, (0 if i % 2 == 0 else 6) + b, :], aq[64 * b:64 * b + 64, hd, j * P:(j + 1) * P],
                                   ak[64 * b:64 * b + 64, hd, :], start=True, stop=True)
                mm.then_inc(S("a_scores"), 1)

            def a_turn(i):
                pe.wait_ge(S("a_probs"), i + 1)
                if i:
                    pe.wait_ge(S("a_turned_copied"), i)
                for s in range(4):
                    mm = pe.transpose(psum[:, 2, s * P:(s + 1) * P], prob2[:, i % 2, 0, s * P:(s + 1) * P], ident)
                mm.then_inc(S("a_turned"), 1)

            def a_values(i):
                pe.wait_ge(S("a_turned_copied"), i + 1)
                if i:
                    pe.wait_ge(S("a_out"), i)
                for s in range(4):
                    mm = pe.matmul(psum[:, 3, 0:P], av[:, s, i // 2 * P:(i // 2 + 1) * P], probt2[:, i % 2, s, :],
                                   start=s == 0, stop=s == 3)
                mm.then_inc(S("a_values"), 1)

            def head_sums(hd):
                pe.wait_ge(S("branch_squares"), 3 + hd)
                pe.matmul(half_bank((0, 1, 6, 7)[hd], 0), ones, sq[:, hd, :], start=True, stop=True)\
                  .then_inc(S("branch_sums"), 1)

            a_scores(0)
            for i in range(8):
                if i < 7:
                    a_scores(i + 1)
                if i < 7:
                    project(f"g2_{17 + i}", None, lat)
                a_turn(i)
                if i:
                    a_values(i - 1)
                if i == 7:
                    for hd in range(3):
                        head_sums(hd)
            a_values(7)
            head_sums(3)

            for n in range(8):
                for s, m in enumerate(["wm", "wat", "ws"]):
                    name = f"m2_{n}{'aab'[s]}"
                    if s != 1:
                        bank_free(pe, name)
                    w = split_weights(AT[(m, n // 2)])
                    for k in range(4):
                        pe.wait_ge(S("branch_parts"), (1, 3 + k, 2)[s])
                        mm = split_product(bank(name)[:, s % 2 * T:(s % 2 + 1) * T], w,
                                           slice((n % 2 * 4 + k) * P, (n % 2 * 4 + k + 1) * P),
                                           (bp[:, s, 0, k], bp[:, s, 1, k]), k == 0, k == 3)
                    if s == 0 and n % 2:
                        mm.then_inc(S("tiles_used"), 1)
                    if s == 1:
                        mm.then_inc(S("small_products"), 1)
                    if s == 2:
                        if n % 2:
                            mm.then_inc(S("tiles_used"), 2)
                        else:
                            mm.then_inc(S("small_products"), 1)
            pe.wait_ge(S("branch_roots"), 3)
            for n in range(8):
                pe.wait_ge(S("merged"), 16)
                if n < 2:
                    cols(AT[("out2", n)], acc[n], lambda k: merged2[:, k, :])
                else:
                    split_cols(AT[("out2", n)], acc[n], lambda k: p1_hi[:, k, :], lambda k: p1_lo[:, k, :],
                               lambda k: pe.wait_ge(S("input_parts"), INPUT_PARTS["merged2"] + k + 1))
            sums_wide("norm2")

            ffn(2)

        @block.scalar
        def _(act):
            steps = [0]

            def link(ins):
                steps[0] += 1
                ins.then_inc(S("scalar_steps"), 1)
                act.wait_ge(S("scalar_steps"), steps[0])

            def squares(name, chunk2, ready, scale=1.0, to=sq):
                for k in range(4):
                    ready(k)
                    act.activation(to[:, 2 * k:2 * k + 2, :], chunk2(k), ACT.Square, scale=scale).then_inc(S("squares"), 1)

            def take_root(name, features):
                i = NORM_AT[name]
                act.wait_ge(S("sums"), i + 1)
                if i:
                    act.wait_ge(S("inverses"), i)
                act.activation(root, half_bank(SUMS, 0), ACT.Sqrt, scale=1.0 / features, bias=eps)\
                   .then_inc(S("roots"), 1)

            def input_uppers(k, name, count):
                for n in range(DC):
                    act.wait_ge(S(name), count + n + 1)
                    act.activation(u_hi[:, n, :], u1[:, n, :], ACT.Copy).then_inc(S("input_upper"), 1)

            def uppers(k, first, last):
                for j in range(first, last):
                    upper(k, j)

            def upper(k, j, more=0):
                t = AT[(f"gate{FFNS[k]}", 0)] + j
                act.wait_ge(S(f"slot{t % RING}_loaded"), more * 16 + 16 * (t // RING + 1))
                if k or j >= RING or not isinstance(more, int):
                    act.wait_ge(S("tiles_used"), more * RING + (t - RING + 1))
                act.activation(ring_hi[:, j % RING, :], ring[:, t % RING, :], ACT.Copy)\
                   .then_inc(S("upper_ready"), 1)

            def upper_hidden(par, count):
                act.wait_ge(S("hidden_ready"), count + 1)
                act.activation(hidden_hi[:, par, :], hidden[:, par, :], ACT.Copy)\
                   .then_inc(S("hidden_upper"), 1)

            def feed_forward(k, gate):
                for par in range(2):
                    gate(par, par, k > 0)
                    upper(k, 6 + 3 * par)
                    upper_hidden(par, FC * k + par)
                    upper(k, 7 + 3 * par)
                    upper(k, 8 + 3 * par)
                with act.Fori(0, FC // 2 - 2) as i:
                    for par in range(2):
                        gate(par, i * 2 + (2 + par), True, i)
                        upper(k, 12 + 3 * par, i)
                        upper_hidden(par, i * 2 + (FC * k + 2 + par))
                        upper(k, 13 + 3 * par, i)
                        upper(k, 14 + 3 * par, i)
                for par in range(2):
                    gate(par, FC - 2 + par, True)
                    upper_hidden(par, FC * k + FC - 2 + par)

            def ffn(k):
                base = FC * k

                def gate(par, f, reuse, more=None):
                    used = AT[(f"up{FFNS[k]}", f)] + 1 if more is None else \
                        more * RING + (AT[(f"up{FFNS[k]}", 2 + par)] + 1)
                    act.wait_ge(S("tiles_used"), used)
                    if reuse:
                        act.wait_ge(S("hidden_ready"), f + (base - 1))
                    act.activation(silu[:, par, :], half_bank(PJ[par], 0), ACT.Silu).then_inc(S("silus"), 1)

                feed_forward(k, gate)

            def ffn_conv():
                base = 2 * FC

                def gate(par, f, reuse, more=None):
                    used = AT[("up3", f)] + 1 if more is None else more * RING + (AT[("up3", 2 + par)] + 1)
                    act.wait_ge(S("tiles_used"), used)
                    act.wait_ge(S("hidden_ready"), f + (base - 1))
                    for s, dst in enumerate((cg, ca)):
                        act.activation(dst[:, par, :], half_bank(PJ[par], s), ACT.Identity,
                                       scale=vec[:, bass.ds(f + (VEC["fconv"] + FC * (2 + s)), 1)])\
                           .then_inc(S("conv_centers"), 1)
                    act.wait_ge(S("conv_sides"), f * 4 + 3)
                    act.activation(silu[:, par, :], cg[:, par, :], ACT.Silu).then_inc(S("silus"), 1)

                feed_forward(2, gate)

            def weight_upper(t):
                i = SPLIT_INDEX[t]
                act.wait_ge(S(f"slot{t % RING}_loaded"), 16 * (t // RING + 1))
                last = [u for u in SPLIT_TILES[:i] if SPLIT_PLACE[u] == SPLIT_PLACE[t]]
                act.wait_ge(S("tiles_used"), max([t - RING] + last[-1:]) + 1)
                act.activation(upper_places[:, SPLIT_PLACE[t], :], ring[:, t % RING, :], ACT.Copy)\
                   .then_inc(S("weight_uppers"), 1)

            def merged_upper(merged, name, tiles={}):
                for n in range(DC):
                    act.wait_ge(S("merged"), (8 if name == "merged2" else 0) + n + 1)
                    act.activation(p1_hi[:, n, :], merged[:, n, :], ACT.Copy).then_inc(S("input_uppers"), 1)
                    for t in tiles.get(n, ()):
                        weight_upper(t)

            def copy_bank(name, dst, src=None, func=ACT.Copy, **kw):
                product_ready(act, name)
                act.activation(dst, bank(name)[:, 0:T] if src is None else src, func, **kw).then_inc(read_done(name), 1)

            act.dma_start(vec, dram["vec"]).then_inc(S("vectors_loaded"), 16)
            act.preload_act_table(ACT.Sqrt)
            act.wait_ge(S("x_loaded"), 16)
            act.wait_ge(S("ones_ready"), 1)
            squares("ffn1_pre", lambda k: h[:, 2 * k:2 * k + 2, :], lambda k: None)
            uppers(0, 0, 1)
            take_root("ffn1_pre", D)
            input_uppers(0, "scaled", 0)
            uppers(0, 1, RING)
            act.dma_start(cst, dram["cst"]).then_inc(S("tables_loaded"), 16)
            act.dma_start(lam_p, dram["lam"].partition_broadcast(P)).then_inc(S("tables_loaded"), 16)
            act.dma_start(pos_i, dram["pos"].partition_broadcast(P)).then_inc(S("tables_loaded"), 16)
            act.dma_start(wuq, dram["wuq"]).then_inc(S("small_weights"), 16)
            act.dma_start(wkr, dram["wkr"]).then_inc(S("small_weights"), 16)
            act.activation(cond, vec[:, VEC["cond"]:VEC["cond"] + 16], ACT.Silu).then_inc(S("cond_ready"), 1)
            act.preload_act_table(ACT.Silu)
            ffn(0)

            def post_squares(name, last_tile, scale=1.0):
                squares(name, lambda k: psum[:, k, :], lambda k: act.wait_ge(S("tiles_used"), last_tile + 1), scale)
                take_root(name, D)

            post_squares("ffn1_post", AT[("down1", FC - 1)])
            squares("mix_pre", lambda k: h[:, 2 * k:2 * k + 2, :], lambda k: act.wait_ge(S("residual"), 2 * k + 2))
            weight_upper(AT[("cq", 0)])
            take_root("mix_pre", D)

            for n in range(DC):
                act.wait_ge(S("scaled"), DC + n + 1)
                act.activation(p1_hi[:, n, :], u1[:, n, :], ACT.Copy).then_inc(S("input_uppers"), 1)
            for i in range(1, 4):
                weight_upper(AT[("cq", 0)] + i)
            for n in range(3):
                weight_upper(AT[("cq", 0)] + 4 + n)
                product_ready(act, f"cq{n}")
                act.activation(sq[:, n, :], bank(f"cq{n}")[:, 0:T], ACT.Square).then_inc(S("squares"), 1)
                copy_bank(f"cq{n}", cq[:, n, :])
            for n in range(2):
                weight_upper(AT[("cq", 0)] + 7 + n)
                product_ready(act, f"ckv{n}")
                act.activation(sq[:, 3 + n, :], bank(f"ckv{n}")[:, 0:T], ACT.Square).then_inc(S("squares"), 1)
                copy_bank(f"ckv{n}", ckv[:, n, :])
            copy_bank("kr", kr[64:96, :], bank("kr")[64:96, 0:T])
            take_root("q_norm", Q_RANK)
            for n in range(4):
                weight_upper(AT[("cq", 0)] + 9 + n)
                copy_bank(f"dq{n}", qd[:, n, :])
            take_root("kv_norm", KV_RANK)
            act.wait_ge(S("angles_ready"), 1)
            act.activation(tab, ang, ACT.Sin).then_inc(S("tab_ready"), 1)
            for n in range(4):
                weight_upper(AT[("cq", 0)] + 13 + n)
                copy_bank(f"dk{n}", kd[:, n, :])
            act.wait_ge(S("tiles_used"), AT[("dv", 3)] + 1)
            for n in range(2):
                act.activation(vd[:, n, :], psum[:, n, :], ACT.Copy).then_inc(S("vd_copied"), 1)
            for n in range(4):
                copy_bank(f"uk{n}", kh[0:64, 2 * n:2 * n + 2, :], bank(f"uk{n}")[0:64, :])
            act.wait_ge(S("tiles_used"), AT[("uv", 0)] + 1)
            for n in range(2):
                act.activation(va[:, n, :], psum[:, 2 + n, :], ACT.Copy).then_inc(S("va_copied"), 1)
            weight_upper(AT[("g1", 0)])
            weight_upper(AT[("g1", 1)])
            for n in range(4):
                copy_bank(f"uq{n}", q[0:96, 2 * n:2 * n + 2, :], bank(f"uq{n}")[0:96, :])

            def exps(k):
                act.wait_ge(S("negmax"), k + 1)
                if k >= 2:
                    act.wait_ge(S("turned"), k - 1)
                x = 2 * (k % 2)
                for j in range(2):
                    src = sbias[:, k % 2, j, :] if k < 8 else psum[:, k % 2, j * T:(j + 1) * T]
                    act.activation(prob[:, k % 2, j, :], src, ACT.Exp, bias=negmax[:, x + j:x + j + 1],
                                   scale=1.0 if k < 8 else SCALE_MLA, accum_out=den[:, x + j:x + j + 1])\
                       .then_inc(S("exps"), 1)

            def turned(k):
                act.wait_ge(S("turned"), k + 1)
                if k >= 2:
                    act.wait_ge(S("outs"), k - 1)
                act.activation(probt[:, k % 2, :, :], psum[:, 2 + k % 2, :], ACT.Copy).then_inc(S("turned_copied"), 1)

            act.activation(row_exp, v("row_alog"), ACT.Exp).then_inc(S("early"), 1)
            act.activation(lam[:, 2:4], lam[:, 0:2], ACT.Exp).then_inc(S("early"), 1)
            exps(0)
            for k in range(16):
                copy_bank(f"g1_{k}", gates[:, k, :], None, ACT.Tanh, scale=0.5, bias=bhalf[:, k:k + 1])
                if k < 14:
                    weight_upper(AT[("g1", k + 2)])
                if k < 15:
                    exps(k + 1)
                turned(k)

            merged_upper(merged1, "merged1", {4: [AT[("out1", 0)]], 5: [AT[("out1", 1)]]})
            for n in range(2, 8):
                weight_upper(AT[("out1", n)])
            post_squares("mix_post", AT[("out1", 7)], 0.5)
            squares("ffn2_pre", lambda k: h[:, 2 * k:2 * k + 2, :], lambda k: act.wait_ge(S("residual"), 8 + 2 * k + 2))
            uppers(1, 0, 2)
            take_root("ffn2_pre", D)
            input_uppers(1, "scaled", 16)
            uppers(1, 2, RING)
            act.preload_act_table(ACT.Silu)
            ffn(1)
            post_squares("ffn2_post", AT[("down2", FC - 1)])

            act.wait_ge(S("ctx_loaded"), 16)
            squares("ctx", lambda k: ctx_raw[:, 2 * k:2 * k + 2, :], lambda k: act.wait_ge(S("sums"), 8))
            take_root("ctx", D)

            def shift_half(s):
                for n in range(DC):
                    act.wait_ge(S("prescaled"), 8 * s + n + 1)
                    act.activation(p2_hi[:, n, s], u2[:, n, s * T:(s + 1) * T], ACT.Identity,
                                   bias=modc[:, n, 1 - s:2 - s]).then_inc(S("input_uppers"), 1)

            squares("norm1", lambda k: h[:, 2 * k:2 * k + 2, :], lambda k: act.wait_ge(S("residual"), 16 + 2 * k + 2),
                    to=sq_late)
            shift_half(0)
            weight_upper(AT[("rows", 0)])
            take_root("norm1", D)
            shift_half(1)
            for i in range(1, 5):
                weight_upper(AT[("rows", 0)] + i)

            def conv(i, between=None):
                m, n, wt = CONV[i]
                name = f"{m}{n}"
                wide_ = m in ("mk", "sx") or m == "sb"
                product_ready(act, name)
                table = "mconv" if m in ("mk", "mq") else "sconv"
                dst = conv_dst[m][:, n, :]
                src = bank(name) if wide_ else bank(name)[:, 0:T]
                act.activation(dst, src, ACT.Identity, scale=v(table, 8 + wt)).then_inc(S("conv_center2"), 1)
                evacuated(act, name)
                act.activation(dst, dst, ACT.Silu, bias=v(table + "_b", wt)).then_inc(S("conv_done"), 1)

            for i in range(8):
                weight_upper(AT[("rows", 0)] + i + 5)
                conv(i)
            act.wait_ge(S("rows_z"), 1)
            link(act.activation(sp, z, ACT.Abs))
            link(act.activation(sp, sp, ACT.Exp, scale=-1.0))
            act.activation(sp, sp, ACT.Ln, bias=1.0).then_inc(S("rows_log"), 1)
            for i in range(13, 17):
                weight_upper(AT[("rows", 0)] + i)
            act.wait_ge(S("tiles_used"), AT[("mv", 3)] + 1)
            for n in range(4):
                act.activation(mv[:, n, :], psum[:, n, :], ACT.Copy).then_inc(S("mv_copied"), 1)
            for n in range(4):
                weight_upper(AT[("rows", 0)] + 17 + n)
                copy_bank(f"mo{n}", mo[:, n, :], None, ACT.Tanh, scale=0.5)
            for i in range(8, 16):
                weight_upper(AT[("rows", 0)] + 13 + i)
                conv(i)
            act.wait_ge(S("cols_turned"), 1)
            act.activation(t0, psum[:, 0, :], ACT.Copy).then_inc(S("cols_copied"), 1)
            act.wait_ge(S("cols_turned"), 2)
            for n in range(2):
                act.activation(tc[:, 2 * n:2 * n + 2], psum[:, 1 + n, :], ACT.Copy).then_inc(S("cols_copied"), 1)
            for n in range(4):
                copy_bank(f"sz{n}", sz[:, n, :], None, ACT.Silu)

            def m_scores(hd):
                act.wait_ge(S("m_scores"), hd + 1)
                if hd:
                    act.wait_ge(S("m_weights"), 2 * hd)
                act.activation(mst[:, 0:4, :], psum[:, 2:4, :], ACT.Copy, scale=SCALE_M).then_inc(S("m_scores_part"), 1)
                act.activation(mst[:, 4:6, :], psum[:, 2, :], ACT.Copy, scale=SCALE_M).then_inc(S("m_scores_copied"), 1)

            def m_exps(i):
                act.wait_ge(S("m_masked"), i + 1)
                if i >= 2:
                    act.wait_ge(S("m_sums"), i - 1)
                act.activation(wgt[:, i % 2], arg[:, i % 2], ACT.Exp).then_inc(S("m_exps"), 1)
                if i >= 2:
                    act.wait_ge(S("m_out"), i - 1)
                act.activation(hidden[:, i % 2, :], psum[:, i % 2, T:TT], ACT.Exp).then_inc(S("m_floor"), 1)

            m_scores(0)
            m_exps(0)
            for i in range(8):
                if i < 7:
                    m_exps(i + 1)
                copy_bank(f"g2_{i}", gates[:, i, :], None, ACT.Tanh, scale=0.5)
                if i % 2 == 1 and i < 7:
                    m_scores(i // 2 + 1)
                act.wait_ge(S("m_sums"), i + 1)
                act.activation(silu[:, i % 2, :], psum[:, 6 + i % 2, T:TT], ACT.Abs).then_inc(S("m_abs"), 1)

            for g in range(2):
                act.wait_ge(S("sg_ready"), g + 1)
                act.activation(sg[:, g, 0:4, :], psum[:, 2:4, :], ACT.Copy).then_inc(S("sg_part"), 1)
                act.activation(sg[:, g, 4:6, :], psum[:, 2, :], ACT.Copy).then_inc(S("sg_copied"), 1)

            def s_exps(hd):
                for d in range(2):
                    act.wait_ge(S("s_masked"), 2 * hd + d + 1)
                    if hd:
                        act.wait_ge(S("s_sums"), hd)
                    act.activation(wgt[:, d], arg[:, d], ACT.Exp).then_inc(S("s_exps"), 1)

            s_exps(0)
            for hd in range(8):
                copy_bank(f"g2_{8 + hd}", gates[:, 8 + hd, :], None, ACT.Tanh, scale=0.5)
                if hd < 7:
                    s_exps(hd + 1)

            act.wait_ge(S("s_sums"), 8)
            act.activation(sq[:, 0:4, :], ym, ACT.Square).then_inc(S("branch_squares"), 1)
            copy_bank("aq0", aq[:, 0, :])
            act.wait_ge(S("ys_done"), 1)
            act.activation(tmp[:, 0:4, :], ys, ACT.Square).then_inc(S("branch_squares"), 1)
            copy_bank("aq1", aq[:, 1, :])
            act.wait_ge(S("branch_sums"), 1)
            act.activation(tmp[:, 4:8, :], psum[:, 2:4, :], ACT.Sqrt, scale=1.0 / 128, bias=eps).then_inc(S("branch_roots"), 1)
            copy_bank("aq2", aq[:, 2, :])
            act.wait_ge(S("branch_sums"), 2)
            act.activation(hidden, psum[:, 6, :], ACT.Sqrt, scale=1.0 / 256, bias=eps).then_inc(S("branch_roots"), 1)
            copy_bank("aq3", aq[:, 3, :])
            for n in range(4):
                copy_bank(f"ak{n}", ak[:, n, :], bank(f"ak{n}"))
                if n == 1:
                    act.wait_ge(S("branches"), 1)
                    act.activation(bp[:, 0, 0], ym, ACT.Copy).then_inc(S("branch_uppers"), 1)
                if n == 2:
                    act.wait_ge(S("branches"), 5)
                    act.activation(bp[:, 2, 0], ys, ACT.Copy).then_inc(S("branch_uppers"), 1)
            for n in (2, 3):
                evacuated(act, f"aq{n}", f"ak{n}")
            act.activation(sqa, ak, ACT.Square).then_inc(S("a_squares"), 1)
            act.activation(sqq, aq, ACT.Square).then_inc(S("a_squares"), 1)
            act.wait_ge(S("tiles_used"), AT[("av", 3)] + 1)
            for n in range(4):
                act.activation(av[:, n, :], psum[:, n, :], ACT.Copy).then_inc(S("av_copied"), 1)
            act.wait_ge(S("branches"), 5)
            copy_bank("krow", krow_r, bank("krow")[0:8, :], ACT.Sqrt, scale=1.0 / 64, bias=eps[0:8, :])
            copy_bank("rq", rq, bank("rq")[:, 0:16], ACT.Sqrt, scale=1.0 / 64, bias=eps)
            copy_bank("g2_16", gates[:, 16, :], None, ACT.Tanh, scale=0.5)

            def a_exps(i):
                act.wait_ge(S("a_negmax"), i + 1)
                if i >= 2:
                    act.wait_ge(S("a_turned"), i - 1)
                x = 2 * (i % 2)
                for b in range(2):
                    act.activation(prob2[:, i % 2, b, :], psum[:, (0 if i % 2 == 0 else 6) + b, :], ACT.Exp,
                                   bias=negmax[:, x + b:x + b + 1], scale=rq[:, 2 * i + b:2 * i + b + 1],
                                   accum_out=den[:, x + b:x + b + 1]).then_inc(S("a_exps"), 1)

            a_exps(0)
            for i in range(8):
                if i < 7:
                    copy_bank(f"g2_{17 + i}", gates[:, 17 + i, :], None, ACT.Tanh, scale=0.5)
                if i < 7:
                    a_exps(i + 1)
                act.wait_ge(S("a_turned"), i + 1)
                if i >= 2:
                    act.wait_ge(S("a_values"), i - 1)
                act.activation(probt2[:, i % 2], psum[:, 2, :], ACT.Copy).then_inc(S("a_turned_copied"), 1)

            def head_squares(hd):
                act.wait_ge(S("a_out"), 2 * hd + 2)
                act.activation(sq[:, hd, :], ya[:, hd, :], ACT.Square).then_inc(S("branch_squares"), 1)

            def head_root(hd):
                act.wait_ge(S("branch_sums"), 3 + hd)
                act.activation(tmp[:, 4 + hd, :], half_bank((0, 1, 6, 7)[hd], 0), ACT.Sqrt, scale=1.0 / 128, bias=eps)\
                   .then_inc(S("branch_roots"), 1)

            def head_upper(hd):
                act.wait_ge(S("branches"), 6 + hd)
                act.activation(bp[:, 1, 0, hd], ya[:, hd, :], ACT.Copy).then_inc(S("branch_uppers"), 1)

            for hd in range(3):
                head_squares(hd)
            head_root(0)
            weight_upper(AT[("wm", 0)])
            head_squares(3)
            for hd in range(1, 4):
                head_root(hd)
            head_upper(0)
            weight_upper(AT[("wat", 0)])
            head_upper(1)
            weight_upper(AT[("ws", 0)])
            head_upper(2)
            head_upper(3)
            for m in ("wm", "wat", "ws"):
                weight_upper(AT[(m, 1)])

            merged_upper(merged2, "merged2", {1: [AT[("wm", 2)]], 2: [AT[("wat", 2)], AT[("ws", 2)]],
                                              3: [AT[("wm", 3)]], 4: [AT[("wat", 3)], AT[("ws", 3)]]})
            for n in range(2, 8):
                weight_upper(AT[("out2", n)])
            uppers(2, 0, 4)
            squares("norm2", lambda k: h[:, 2 * k:2 * k + 2, :], lambda k: act.wait_ge(S("added"), 2 * k + 2))
            take_root("norm2", D)
            for n in range(DC):
                act.wait_ge(S("prescaled"), 16 + n + 1)
                act.activation(u_hi[:, n, :], u1[:, n, :], ACT.Identity, bias=modc[:, 24 + n, 0:1])\
                   .then_inc(S("input_upper"), 1)
            uppers(2, 4, RING)
            act.preload_act_table(ACT.Silu)
            ffn_conv()

        @block.vector
        def _(dve):
            steps = [0]

            def link(ins):
                steps[0] += 1
                ins.then_inc(S("vector_steps"), 1)
                dve.wait_ge(S("vector_steps"), steps[0])

            inverse_used = {"ffn1_post": ("scaled", 8), "mix_pre": ("post_scaled", 8), "q_norm": ("scaled", 16),
                            "kv_norm": ("q_scaled", 3), "mix_post": ("kv_scaled", 2), "ffn2_pre": ("post_scaled", 16),
                            "ffn2_post": ("scaled", 24), "ctx": ("post_scaled", 24), "norm1": ("prescaled", 8)}

            def invert(name):
                i = NORM_AT[name]
                if name in inverse_used:
                    dve.wait_ge(S(inverse_used[name][0]), inverse_used[name][1])
                dve.wait_ge(S("roots"), i + 1)
                dve.reciprocal(inv, root).then_inc(S("inverses"), 1)
                dve.wait_ge(S("inverses"), i + 1)

            def scale_into(name, dst, src, g, sem, between=lambda n: None):
                invert(name)
                for n in range(len(src)):
                    dve.scalar_tensor_tensor(out=dst[n], in0=src[n], scalar=g(n), in1=inv, op0=ALU.mult,
                                             op1=ALU.mult).then_inc(S(sem), 1)
                    between(n)

            def post(name, g):
                p = POSTS.index(name)
                invert(name)
                for n in range(DC + 1):
                    if n < DC:
                        dve.scalar_tensor_tensor(out=tmp[:, n, :], in0=acc[n], scalar=v(g, n), in1=inv, op0=ALU.mult,
                                                 op1=ALU.mult).then_inc(S("post_scaled"), 1)
                    if n:
                        dve.wait_ge(S("post_scaled"), 8 * p + n)
                        dve.scalar_tensor_tensor(out=h[:, n - 1, :], in0=tmp[:, n - 1, :], scalar=0.5,
                                                 in1=h[:, n - 1, :], op0=ALU.mult, op1=ALU.add)\
                           .then_inc(S("residual"), 1)

            def lower(k, j, more=0):
                t = AT[(f"gate{FFNS[k]}", 0)] + j
                dve.wait_ge(S("upper_ready"), more * RING + (3 * FC * k + j + 1))
                dve.tensor_tensor(ring_lo[:, j % RING, :], ring[:, t % RING, :], ring_hi[:, j % RING, :],
                                  ALU.subtract).then_inc(S("lower_ready"), 1)

            def lower_hidden(par, count):
                dve.wait_ge(S("hidden_upper"), count + 1)
                dve.tensor_tensor(hidden_lo[:, par, :], hidden[:, par, :], hidden_hi[:, par, :],
                                  ALU.subtract).then_inc(S("hidden_split"), 1)

            def lower_input(k, n):
                dve.wait_ge(S("input_upper"), DC * k + n + 1)
                if k == 2:
                    dve.scalar_tensor_tensor(out=u_lo[:, n, :], in0=u1[:, n, :], scalar=modc[:, 24 + n, 0:1],
                                             in1=u_hi[:, n, :], op0=ALU.add, op1=ALU.subtract)\
                       .then_inc(S("input_split"), 1)
                    return
                dve.tensor_tensor(u_lo[:, n, :], u1[:, n, :], u_hi[:, n, :], ALU.subtract)\
                   .then_inc(S("input_split"), 1)

            def begin_feed_forward(k, norm, early, late, g, sem):
                for j in early:
                    lower(k, j)
                scale_into(norm, [u1[:, n, :] for n in range(DC)], [h[:, n, :] for n in range(DC)], g, sem,
                           lambda n: lower_input(k, n - 2) if n >= 2 else None)
                lower_input(k, DC - 2)
                lower_input(k, DC - 1)
                for j in late:
                    lower(k, j)

            def feed_forward(k, product):
                def condition(i, par):
                    for g in ((0,), (1, 2))[par]:
                        dve.wait_ge(S(f"cond_tile{g}"), i * 16 + (16 * DC * k + 16))
                        dve.wait_ge(S("cond_steps"), i * COND_TURN[k] + COND_FROM[k])
                        for who in ((1, 0) if k == 0 and g < 2 else (0,)):
                            acc_ = (cond_sums_ctx if who else cond_sums)[g]
                            dve.scalar_tensor_tensor(out=acc_, in0=cond_places[g], scalar=small[:, bass.ds(i * 2 + who, 1)],
                                                     in1=acc_, op0=ALU.mult, op1=ALU.add).then_inc(S("cond_steps"), 1)

                for par in range(2):
                    product(par, par)
                    lower(k, 6 + 3 * par)
                    lower_hidden(par, FC * k + par)
                    lower(k, 7 + 3 * par)
                def turn(i, beside):
                    for par in range(2):
                        product(par, i * 2 + (2 + par))
                        lower(k, 12 + 3 * par, i)
                        lower_hidden(par, i * 2 + (FC * k + 2 + par))
                        lower(k, 13 + 3 * par, i)
                        beside(i, par)

                if k < 2:
                    with dve.Fori(0, DC) as i:
                        turn(i, condition)
                    turn(DC, lambda i, par: None)
                else:
                    with dve.Fori(0, FC // 2 - 2) as i:
                        turn(i, lambda i, par: None)
                for par in range(2):
                    product(par, FC - 2 + par)
                    lower_hidden(par, FC * k + FC - 2 + par)

            def ffn(k):
                def multiply(par, f):
                    dve.wait_ge(S("silus"), f + (FC * k + 1))
                    dve.tensor_tensor(hidden[:, par, :], silu[:, par, :], half_bank(PJ[par], 1), ALU.mult)\
                       .then_inc(S("hidden_ready"), 1)

                feed_forward(k, multiply)

            def ffn_conv():
                base = 2 * FC

                def side(dst, s, par, f, tap):
                    a, b = (slice(1, T), slice(0, T - 1)) if tap == 0 else (slice(0, T - 1), slice(1, T))
                    w = vec[:, bass.ds(f + (VEC["fconv"] + FC * (2 * tap + s)), 1)]
                    dve.scalar_tensor_tensor(out=dst[:, par, a], in0=half_bank(PJ[par], s)[:, b], scalar=w,
                                             in1=dst[:, par, a], op0=ALU.mult, op1=ALU.add).then_inc(S("conv_sides"), 1)

                def chunk(par, f):
                    dve.wait_ge(S("conv_centers"), f * 2 + 2)
                    side(cg, 0, par, f, 0)
                    side(ca, 1, par, f, 0)
                    dve.wait_ge(S("conv_sides"), f * 4 + 1)
                    side(cg, 0, par, f, 2)
                    dve.wait_ge(S("conv_sides"), f * 4 + 2)
                    side(ca, 1, par, f, 2)
                    dve.wait_ge(S("conv_sides"), f * 4 + 4)
                    dve.wait_ge(S("silus"), f + (base + 1))
                    dve.tensor_tensor(hidden[:, par, :], silu[:, par, :], ca[:, par, :], ALU.mult)\
                       .then_inc(S("hidden_ready"), 1)

                feed_forward(2, chunk)

            def mod_copy(n0, n1, who, count):
                dve.wait_ge(S("cond_products"), count)
                dve.tensor_tensor(modc[:, n0:n1, who],
                                  psum[:, MOD, 2 * n0:2 * n1].rearrange("p (n b) -> p n b", b=2)[:, :, who],
                                  vec[:, VEC["bmod"] + n0:VEC["bmod"] + n1], ALU.add).then_inc(S("mod_ready"), 1)

            def clear_sums(k):
                for a in cond_sums + (cond_sums_ctx if k == 0 else []):
                    dve.memset(a, 0.0).then_inc(S("cond_steps"), 1)


            dve.memset(eps, EPS).then_inc(S("ones_part"), 1)
            dve.wait_ge(S("ones_part"), 1)
            dve.memset(ones, 1.0).then_inc(S("ones_ready"), 1)
            clear_sums(0)
            dve.wait_ge(S("vectors_loaded"), 16)
            begin_feed_forward(0, "ffn1_pre", range(1), range(1, RING), lambda n: v("ffn1_pre", n), "scaled")
            dve.wait_ge(S("tables_loaded"), 48)
            link(dve.tensor_copy(posf, pos_i))
            dve.wait_ge(S("cond_ready"), 1)
            ffn(0)
            post("ffn1_post", "ffn1_post")

            mod_copy(0, 24, 0, 1)

            def input_lower(i, dst, whole, upper_):
                dve.wait_ge(S("input_uppers"), i + 1)
                dve.tensor_tensor(dst, whole, upper_, ALU.subtract).then_inc(S("input_parts"), 1)

            def input_lower_1(n):
                input_lower(INPUT_PARTS["mix_pre"] + n, p1_lo[:, n, :], u1[:, n, :], p1_hi[:, n, :])

            def input_lower_2(s, n):
                dve.wait_ge(S("input_uppers"), INPUT_PARTS[("ctx", "norm1")[s]] + n + 1)
                dve.scalar_tensor_tensor(out=p2_lo[:, n, s], in0=u2[:, n, s * T:(s + 1) * T],
                                         scalar=modc[:, n, 1 - s:2 - s], in1=p2_hi[:, n, s], op0=ALU.add,
                                         op1=ALU.subtract).then_inc(S("input_parts"), 1)

            scale_into("mix_pre", [u1[:, n, :] for n in range(DC)], [h[:, n, :] for n in range(DC)],
                       lambda n: v("mix_pre", n), "scaled", lambda n: input_lower_1(n - 2) if n >= 2 else None)
            input_lower_1(DC - 2)
            input_lower_1(DC - 1)

            link(dve.tensor_scalar(row_bias, v("row_bias"), c("sign", 1), None, ALU.mult))
            link(dve.tensor_scalar(bhalf, vec[:, VEC["bgate"]:VEC["bgate"] + 16], 0.5, None, ALU.mult))
            link(dve.tensor_scalar(g_half, vec[:, VEC["mnorm"]:VEC["mnorm"] + 4], 0.5, None, ALU.mult))
            link(dve.tensor_scalar(g_sub, v("subln"), 1.0 - LAM_INIT, None, ALU.mult))
            lp = lam_p.rearrange("p (a b n) -> p a b n", a=2, b=2)
            link(dve.tensor_tensor(lp[:, :, 0, :], lp[:, :, 0, :], lp[:, :, 1, :], ALU.mult))
            dve.tensor_reduce(lam[:, 0:2], lp[:, :, 0, :], AX_X, ALU.add).then_inc(S("lam_sums"), 1)
            for n in range(2):
                for s in range(2):
                    link(dve.tensor_scalar(ang[:, n, s, :], posf, c("freq", 2)[:, n:n + 1], None, ALU.mult))
            turns = tab.rearrange("p (n s) t -> p n s t", n=2)
            link(dve.tensor_scalar(turns, ang, 1.0 / TWO_PI, None, ALU.mult))
            link(dve.tensor_scalar(turns[:, :, 1, :], turns[:, :, 1, :], 0.25, None, ALU.add))
            link(dve.tensor_scalar(turns, turns, MAGIC, None, ALU.add))
            link(dve.tensor_scalar(turns, turns, -MAGIC, None, ALU.add))
            for part in two_pi_parts():
                link(dve.scalar_tensor_tensor(out=ang, in0=turns, scalar=-part, in1=ang, op0=ALU.mult, op1=ALU.add))
            link(dve.tensor_scalar(ang[:, :, 1, :], ang[:, :, 1, :], float(np.pi / 2), None, ALU.add))
            dve.tensor_scalar(ang, ang, 3.1415925, -3.1415925, ALU.min, ALU.max).then_inc(S("angles_ready"), 1)

            scale_into("q_norm", [cq[:, n, :] for n in range(3)], [cq[:, n, :] for n in range(3)],
                       lambda n: v("q_norm", n), "q_scaled")
            scale_into("kv_norm", [ckv[:, n, :] for n in range(2)], [ckv[:, n, :] for n in range(2)],
                       lambda n: v("kv_norm", n), "kv_scaled")

            def rotate(x, rows, name, sin, cos, t, heads, done):
                product_ready(dve, name)
                width = heads * T
                rot = bank(name)[rows, 0:width].rearrange("p (a b) -> p a b", a=heads)
                wide_ = lambda a: a.unsqueeze(1).broadcast_to([rows.stop - rows.start, heads, T])
                tt = t[rows, 0:width].rearrange("p (a b) -> p a b", a=heads)
                dve.tensor_tensor(tt, rot, wide_(sin), ALU.mult).then_inc(read_done(name), 1)
                link(dve.tensor_tensor(x, x, wide_(cos), ALU.mult))
                evacuated(dve, name)
                dve.tensor_tensor(x, x, tt, ALU.add).then_inc(S(done), 1)

            all_rows, mla_rows = slice(0, P), slice(64, 96)
            dve.wait_ge(S("tab_ready"), 1)
            for n, (x, name) in enumerate([(qd, "rdq0"), (qd, "rdq1"), (kd, "rdk0"), (kd, "rdk1")]):
                if n:
                    dve.wait_ge(S("dil_roped"), n)
                rotate(x[:, 2 * (n % 2):2 * (n % 2) + 2, :], all_rows, name, tab[:, 2, :], tab[:, 3, :], rt, 2, "dil_roped")
            dve.wait_ge(S("dil_roped"), 4)
            for n in range(4):
                if n:
                    dve.wait_ge(S("mla_roped"), n)
                rotate(q[64:96, 2 * n:2 * n + 2, :], mla_rows, f"ruq{n}", tab[64:96, 0, :], tab[64:96, 1, :], rt, 2, "mla_roped")
            dve.wait_ge(S("mla_roped"), 4)
            rotate(kr[64:96, :].unsqueeze(1), mla_rows, "rkr", tab[64:96, 0, :], tab[64:96, 1, :], rt, 1, "kr_roped")
            dve.wait_ge(S("kr_roped"), 1)
            dve.tensor_copy(kh[64:96, :, :], kr[64:96, :].unsqueeze(1).broadcast_to([32, 8, T])).then_inc(S("mla_roped"), 1)

            def maxima(k):
                dve.wait_ge(S("scores"), k + 1)
                x = 2 * (k % 2)
                src = psum[:, k % 2, :].rearrange("p (j n) -> p j n", j=2)
                if k >= 2:
                    dve.wait_ge(S("exps"), 2 * (k - 1))
                if k < 8:
                    link(dve.scalar_tensor_tensor(out=sbias[:, k % 2], in0=src, scalar=SCALE_64,
                                                  in1=c("dil_bias", TT).rearrange("p (j n) -> p j n", j=2),
                                                  op0=ALU.mult, op1=ALU.add))
                    src = sbias[:, k % 2]
                link(dve.tensor_reduce(dmax[:, x:x + 2], src, AX_X, ALU.max))
                dve.tensor_scalar(negmax[:, x:x + 2], dmax[:, x:x + 2], -1.0 if k < 8 else -SCALE_MLA, None, ALU.mult)\
                   .then_inc(S("negmax"), 1)

            def normalise(k):
                x = 2 * (k % 2)
                dve.wait_ge(S("exps"), 2 * k + 2)
                link(dve.reciprocal(rden[:, x:x + 2], den[:, x:x + 2]))
                for j in range(2):
                    dve.tensor_scalar(prob[:, k % 2, j, :], prob[:, k % 2, j, :], rden[:, x + j:x + j + 1], None, ALU.mult)\
                       .then_inc(S("probs"), 1)

            def out(k):
                r = slice(64 * (k % 2), 64 * (k % 2) + 64)
                dve.wait_ge(S("outs"), k + 1)
                dst = ob[r, k // 2, :] if k < 8 else oa[r, (k - 8) // 2, :]
                dve.tensor_copy(dst, psum[r, 6 + k % 2, 0:T]).then_inc(S("outs_copied"), 1)

            maxima(0)
            dve.wait_ge(S("early"), 2)
            link(dve.tensor_scalar(row_coef, row_exp, -1.0, None, ALU.mult))
            link(dve.tensor_tensor(lam[:, 4:5], lam[:, 3:4], lam[:, 2:3], ALU.subtract))
            link(dve.tensor_scalar(lam[:, 5:6], lam[:, 4:5], -LAM_INIT, None, ALU.add))
            for k in range(16):
                normalise(k)
                if k < 15:
                    maxima(k + 1)
                if k:
                    out(k - 1)
            out(15)

            for n in range(8):
                name = f"m1_{n}"
                product_ready(dve, name)
                link(dve.scalar_tensor_tensor(out=rt[:, 0:T], in0=gates[:, n, :], scalar=1.0, in1=bank(name)[:, 0:T],
                                              op0=ALU.add, op1=ALU.mult))
                dve.scalar_tensor_tensor(out=rt[:, T:TT], in0=gates[:, 8 + n, :], scalar=1.0, in1=bank(name)[:, T:TT],
                                         op0=ALU.add, op1=ALU.mult).then_inc(read_done(name), 1)
                evacuated(dve, name)
                dve.tensor_tensor(merged1[:, n, :], rt[:, 0:T], rt[:, T:TT], ALU.add).then_inc(S("merged"), 1)
                dve.wait_ge(S("merged"), n + 1)
                if n:
                    input_lower(INPUT_PARTS["merged1"] + n - 1, p1_lo[:, n - 1, :], merged1[:, n - 1, :], p1_hi[:, n - 1, :])
            input_lower(INPUT_PARTS["merged1"] + 7, p1_lo[:, 7, :], merged1[:, 7, :], p1_hi[:, 7, :])
            dve.wait_ge(S("input_parts"), INPUT_PARTS["merged1"] + DC)
            clear_sums(1)
            post("mix_post", "mix_post")
            mod_copy(0, 16, 1, 2)
            begin_feed_forward(1, "ffn2_pre", range(2), range(2, RING), lambda n: v("ffn2_pre", n), "scaled")
            ffn(1)
            post("ffn2_post", "ffn2_post")

            def modulated_gain(n, m, who, g):
                link(dve.scalar_tensor_tensor(out=gmod[:, 8 * n:8 * n + 8], in0=modc[:, m:m + 8, who], scalar=1.0,
                                              in1=vec[:, VEC[g]:VEC[g] + 8], op0=ALU.add, op1=ALU.mult))

            modulated_gain(0, 8, 1, "norm1")
            modulated_gain(1, 8, 0, "norm1")
            scale_into("ctx", [u2[:, n, 0:T] for n in range(DC)], [ctx_raw[:, n, :] for n in range(DC)],
                       lambda n: gmod[:, n:n + 1], "prescaled", lambda n: input_lower_2(0, n - 2) if n >= 2 else None)
            input_lower_2(0, DC - 2)
            input_lower_2(0, DC - 1)
            mod_copy(24, 48, 0, 3)
            dve.wait_ge(S("mod_ready"), 3)
            modulated_gain(2, 32, 0, "norm2")
            link(dve.tensor_scalar(mhalf, modc[:, 16:24, 0], 0.5, None, ALU.mult))
            scale_into("norm1", [u2[:, n, T:TT] for n in range(DC)], [h[:, n, :] for n in range(DC)],
                       lambda n: gmod[:, 8 + n:9 + n], "prescaled", lambda n: input_lower_2(1, n - 2) if n >= 2 else None)
            input_lower_2(1, DC - 2)
            input_lower_2(1, DC - 1)

            product_ready(dve, "rows")
            rows = bank("rows")
            for a, swap in ((0, False), (64, False), (32, True), (96, True)):
                for s in range(2):
                    o = T * (1 - s if swap else s)
                    ins = dve.tensor_copy(raw[a:a + 32, o:o + T], rows[a:a + 32, s * T:(s + 1) * T])
                    if a == 96 and s == 1:
                        ins.then_inc(read_done("rows"), 1)
                        evacuated(dve, "rows")
                    else:
                        link(ins)
            dve.tensor_scalar(z, raw, c("sign", 1), row_bias, ALU.mult, ALU.add).then_inc(S("rows_z"), 1)

            def conv(i):
                m, n, wt = CONV[i]
                name = f"{m}{n}"
                wide_ = m in ("mk", "sx", "sb")
                table = "mconv" if m in ("mk", "mq") else "sconv"
                dst = conv_dst[m][:, n, :]
                src = bank(name) if wide_ else bank(name)[:, 0:T]
                if wide_:
                    dst, src = (a.rearrange("p (s t) -> p s t", s=2) for a in (dst, src))
                lo, hi = ((slice(None), slice(None), slice(0, T - 1)), (slice(None), slice(None), slice(1, T))) if wide_ \
                    else ((slice(None), slice(0, T - 1)), (slice(None), slice(1, T)))
                dve.wait_ge(S("conv_center2"), i + 1)
                link(dve.scalar_tensor_tensor(out=dst[hi], in0=src[lo], scalar=v(table, wt), in1=dst[hi], op0=ALU.mult,
                                              op1=ALU.add))
                dve.scalar_tensor_tensor(out=dst[lo], in0=src[hi], scalar=v(table, 16 + wt), in1=dst[lo], op0=ALU.mult,
                                         op1=ALU.add).then_inc(read_done(name), 1)

            for i in range(8):
                conv(i)
            dve.wait_ge(S("rows_log"), 1)
            link(dve.scalar_tensor_tensor(out=sp, in0=z, scalar=0.0, in1=sp, op0=ALU.max, op1=ALU.add))
            link(dve.tensor_scalar(da, sp, row_coef, None, ALU.mult))
            fw, bw = slice(0, 32), slice(32, 64)
            one = lambda n, a: ones[a:a + 32, 0:1].broadcast_to([32, n])
            link(dve.tensor_tensor_scan(bsum[fw, :], one(TT, 0), da[fw, :], 0.0, ALU.mult, ALU.add))
            link(dve.tensor_tensor_scan(bsum[bw, ::-1], one(TT, 32), da[bw, ::-1], 0.0, ALU.mult, ALU.add))
            product_ready(dve, "ish")
            dve.scalar_tensor_tensor(out=r0[0:64, :], in0=bank("ish")[0:64, :], scalar=v("row_ibias", 0, 0, 64),
                                     in1=bsum[0:64, :], op0=ALU.add, op1=ALU.subtract).then_inc(read_done("ish"), 1)
            evacuated(dve, "ish")
            link(dve.tensor_tensor_scan(mrow[fw, :], r0[fw, :], r0[fw, :], 0.0, ALU.max, ALU.max))
            link(dve.tensor_tensor_scan(mrow[bw, ::-1], r0[bw, ::-1], r0[bw, ::-1], 0.0, ALU.max, ALU.max))
            for rows_, o in ((fw, T), (bw, 0)):
                link(dve.tensor_scalar(rowm[rows_, 0, :], mrow[rows_, o:o + T], -1.0, None, ALU.mult))
                link(dve.scalar_tensor_tensor(out=rowm[rows_, 1, :], in0=bsum[rows_, o:o + T], scalar=-1.0,
                                              in1=mrow[rows_, o:o + T], op0=ALU.mult, op1=ALU.subtract))
            dve.tensor_copy(r0[64:P, :], sp[64:P, :]).then_inc(S("cols_in"), 1)
            link(dve.tensor_tensor_scan(rowl[64:96, :], c("reset", T, 64, 96), da[64:96, T:TT], 0.0, ALU.mult, ALU.add))
            link(dve.tensor_tensor_scan(rowl[96:P, ::-1], c("reset", T, 96, P)[:, ::-1], da[96:P, 0:T][:, ::-1], 0.0,
                                        ALU.mult, ALU.add))
            dve.wait_ge(S("colr_zero"), 1)
            for j in range(4):
                a = T + CHUNK * j
                b = CHUNK * (j + 1)
                link(dve.tensor_tensor_scan(colr[64:96, j, 0:a - 1][:, ::-1], one(a - 1, 64), da[64:96, 1:a][:, ::-1],
                                            0.0, ALU.mult, ALU.add))
                link(dve.tensor_scalar(colr[64:96, j, a:a + CHUNK], rowl[64:96, j * CHUNK:b], -1.0, None, ALU.mult))
                link(dve.tensor_tensor_scan(colr[96:P, j, b + 1:TT], one(TT - b - 1, 96), da[96:P, b:TT - 1],
                                            0.0, ALU.mult, ALU.add))
                ins = dve.tensor_scalar(colr[96:P, j, b - CHUNK:b], rowl[96:P, j * CHUNK:b], -1.0, None, ALU.mult)
                if j < 3:
                    link(ins)
                else:
                    ins.then_inc(S("cols_in"), 1)
            for i in range(8, 16):
                conv(i)
            dve.wait_ge(S("tiles_used"), AT[("sz", 3)] + 1)
            for s in (1, 0):
                dve.tensor_tensor(u2[:, :, s * T:(s + 1) * T], p2_lo[:, :, s], p2_hi[:, :, s], ALU.add)\
                   .then_inc(S("input_whole"), 1)
            dve.wait_ge(S("input_whole"), 2)

            def m_args(i):
                hd, d = i // 2, i % 2
                dve.wait_ge(S("m_rows"), i + 1)
                if i == 0:
                    dve.wait_ge(S("cols_copied"), 1)
                if i >= 2:
                    dve.wait_ge(S("m_exps"), i - 1)
                row = 32 * d + hd
                dve.tensor_tensor(arg[:, i % 2], psum[:, i % 2, 0:T].unsqueeze(1).broadcast_to([P, 4, T]),
                                  t0[:, :, row:row + 1].broadcast_to([P, 4, T]), ALU.add).then_inc(S("m_args"), 1)

            def m_weights(i):
                d = i % 2
                dve.wait_ge(S("m_exps"), i + 1)
                dve.wait_ge(S("m_scores_copied"), i // 2 + 1)
                dve.tensor_tensor(wgt[:, d], wgt[:, d], mst[:, 2 * d:2 * d + 4, :], ALU.mult).then_inc(S("m_weights"), 1)

            def m_out(i):
                hd, d = i // 2, i % 2
                dve.wait_ge(S("m_abs"), i + 1)
                link(dve.tensor_tensor(silu[:, d, :], silu[:, d, :], hidden[:, d, :], ALU.max))
                link(dve.reciprocal(silu[:, d, :], silu[:, d, :]))
                dst = inv if d else ym[:, hd, :]
                dve.tensor_tensor(dst, psum[:, 6 + d, 0:T], silu[:, d, :], ALU.mult).then_inc(S("m_out"), 1)
                if d:
                    dve.wait_ge(S("m_out"), i + 1)
                    link(dve.tensor_tensor(ym[:, hd, :], ym[:, hd, :], inv, ALU.add))

            m_args(0)
            for i in range(8):
                if i < 7:
                    m_args(i + 1)
                m_weights(i)
                if i:
                    m_out(i - 1)
            m_out(7)

            for s in range(4):
                dve.wait_ge(S("x_turned"), s + 1)
                for d in range(2):
                    dtc = t0[:, (s + 2 * d) % 4, 64 + 32 * d:72 + 32 * d].unsqueeze(2).broadcast_to([P, 8, 64])
                    dve.tensor_tensor(xdt[:, d, s, :].rearrange("p (h f) -> p h f", h=8),
                                      psum[:, s % 2, :].rearrange("p (h f) -> p h f", h=8), dtc, ALU.mult)\
                       .then_inc(S("xdt_ready"), 1)

            def s_args(hd):
                dve.wait_ge(S("s_rows"), hd + 1)
                dve.wait_ge(S("cols_copied"), 3)
                for d in range(2):
                    if hd:
                        dve.wait_ge(S("s_exps"), 2 * (hd - 1) + d + 1)
                    row = psum[:, hd % 2, d * T:(d + 1) * T].rearrange("p (j t) -> p j t", j=4)
                    col = tc[:, :, :, 32 * d + hd].rearrange("p j s -> p s j").unsqueeze(3)
                    dve.tensor_tensor(arg[:, d].rearrange("p s (j t) -> p s j t", j=4),
                                      row.unsqueeze(1).broadcast_to([P, 4, 4, CHUNK]),
                                      col.broadcast_to([P, 4, 4, CHUNK]), ALU.add).then_inc(S("s_args"), 1)

            def s_weights(hd):
                for d in range(2):
                    dve.wait_ge(S("s_exps"), 2 * hd + d + 1)
                    if hd == 0:
                        dve.wait_ge(S("sg_copied"), 2)
                    dve.tensor_tensor(wgt[:, d], wgt[:, d], sg[:, hd // 4, 2 * d:2 * d + 4, :], ALU.mult)\
                       .then_inc(S("s_weights"), 1)

            def s_out(hd):
                r = slice(64 * (hd % 2), 64 * (hd % 2) + 64)
                dve.wait_ge(S("s_sums"), hd + 1)
                dve.tensor_copy(ys[r, hd // 2, :], psum[r, 6 + hd % 2, 0:T]).then_inc(S("s_out"), 1)

            s_args(0)
            for hd in range(8):
                s_weights(hd)
                if hd < 7:
                    s_args(hd + 1)
                if hd:
                    s_out(hd - 1)
            s_out(7)
            dve.wait_ge(S("s_out"), 8)
            for f in range(4):
                link(dve.scalar_tensor_tensor(out=ys[:, f, :], in0=sx[:, f, T:TT], scalar=v("sskip", f), in1=ys[:, f, :],
                                              op0=ALU.mult, op1=ALU.add))
            dve.tensor_tensor(ys, ys, sz, ALU.mult).then_inc(S("ys_done"), 1)

            dve.wait_ge(S("branch_roots"), 1)
            link(dve.reciprocal(tmp[:, 4:8, :], tmp[:, 4:8, :]))
            for n in range(4):
                link(dve.scalar_tensor_tensor(out=ym[:, n, :], in0=ym[:, n, :], scalar=g_half[:, n:n + 1],
                                              in1=tmp[:, 4 + n, :], op0=ALU.mult, op1=ALU.mult))
            dve.scalar_tensor_tensor(out=ym, in0=mo, scalar=1.0, in1=ym, op0=ALU.add, op1=ALU.mult)\
               .then_inc(S("branches"), 1)
            dve.wait_ge(S("branch_roots"), 2)
            link(dve.reciprocal(hidden, hidden))
            for f in range(4):
                dve.scalar_tensor_tensor(out=ys[:, f, :], in0=ys[:, f, :], scalar=v("snorm", f), in1=hidden[:, f // 2, :],
                                         op0=ALU.mult, op1=ALU.mult).then_inc(S("branches"), 1)

            for n, b, whole in ((1, 0, ym), (2, 2, ys)):
                dve.wait_ge(S("branch_uppers"), n)
                dve.tensor_tensor(bp[:, b, 1], whole, bp[:, b, 0], ALU.subtract).then_inc(S("branch_parts"), 1)

            dve.wait_ge(S("a_squares"), 2)
            dve.tensor_scalar(aq, aq, v("aqn"), None, ALU.mult).then_inc(S("aq_scaled"), 1)
            evacuated(dve, "krow")
            dve.reciprocal(krow_i, krow_r).then_inc(S("k_inverse"), 1)
            evacuated(dve, "rq")
            link(dve.reciprocal(rq, rq))
            link(dve.tensor_scalar(rq, rq, SCALE_64, None, ALU.mult))
            for n in range(4):
                product_ready(dve, f"kb{n}")
                dve.scalar_tensor_tensor(out=ak[:, n, :], in0=ak[:, n, :], scalar=v("akn"), in1=bank(f"kb{n}"),
                                         op0=ALU.mult, op1=ALU.mult).then_inc(read_done(f"kb{n}"), 1)
            rt2 = place(MEM["silu"][0], 2 * T)
            for n in range(2):
                if n:
                    dve.wait_ge(S("att_roped"), 1)
                rotate(aq[:, 2 * n:2 * n + 2, :], all_rows, f"raq{n}", c("sin_att", T), c("cos_att", T), rt2, 2, "att_roped")
            for n in range(2):
                dve.wait_ge(S("att_roped"), 2 + n)
                rotate(ak[:, 2 * n:2 * n + 2, T:TT], all_rows, f"rak{n}", c("sin_att", T), c("cos_att", T), rt2, 2,
                       "att_roped")

            def a_maxima(i):
                x = 2 * (i % 2)
                b = 0 if i % 2 == 0 else 6
                dve.wait_ge(S("a_scores"), i + 1)
                if i >= 2:
                    dve.wait_ge(S("a_exps"), 2 * (i - 1))
                link(dve.tensor_reduce(dmax[:, x:x + 2], psum[:, b:b + 2, :], AX_X, ALU.max))
                dve.scalar_tensor_tensor(out=negmax[:, x:x + 2], in0=dmax[:, x:x + 2], scalar=-1.0,
                                         in1=rq[:, 2 * i:2 * i + 2], op0=ALU.mult, op1=ALU.mult).then_inc(S("a_negmax"), 1)

            def a_combine(i):
                x = 2 * (i % 2)
                dve.wait_ge(S("a_exps"), 2 * i + 2)
                link(dve.reciprocal(rden[:, x:x + 2], den[:, x:x + 2]))
                link(dve.tensor_scalar(rden[:, x + 1:x + 2], rden[:, x + 1:x + 2], lam[:, 5:6], None, ALU.mult))
                link(dve.tensor_scalar(prob2[:, i % 2, 0, :], prob2[:, i % 2, 0, :], rden[:, x:x + 1], None, ALU.mult))
                dve.scalar_tensor_tensor(out=prob2[:, i % 2, 0, :], in0=prob2[:, i % 2, 1, :], scalar=rden[:, x + 1:x + 2],
                                         in1=prob2[:, i % 2, 0, :], op0=ALU.mult, op1=ALU.add).then_inc(S("a_probs"), 1)

            def a_out(i):
                dve.wait_ge(S("a_values"), i + 1)
                dve.tensor_copy(ya[:, i // 2, i % 2 * P:(i % 2 + 1) * P], psum[:, 3, 0:P]).then_inc(S("a_out"), 1)

            a_maxima(0)
            for i in range(8):
                a_combine(i)
                if i < 7:
                    a_maxima(i + 1)
                if i:
                    a_out(i - 1)

            def head_norm(hd):
                dve.wait_ge(S("branch_roots"), 3 + hd)
                link(dve.reciprocal(tmp[:, 4 + hd, :], tmp[:, 4 + hd, :]))
                dve.scalar_tensor_tensor(out=ya[:, hd, :], in0=ya[:, hd, :], scalar=g_sub, in1=tmp[:, 4 + hd, :],
                                         op0=ALU.mult, op1=ALU.mult).then_inc(S("branches"), 1)

            def head_lower(hd):
                dve.wait_ge(S("branch_uppers"), 3 + hd)
                dve.tensor_tensor(bp[:, 1, 1, hd], ya[:, hd, :], bp[:, 1, 0, hd], ALU.subtract)\
                   .then_inc(S("branch_parts"), 1)

            a_out(7)
            head_norm(0)

            for hd in range(1, 4):
                head_norm(hd)
                head_lower(hd - 1)
            head_lower(3)

            for n in range(8):
                for s in range(3):
                    name = f"m2_{n}{'aab'[s]}"
                    if s != 1:
                        product_ready(dve, name)
                    dst = hidden[:, s, :] if s < 2 else silu[:, 0, :]
                    ins = dve.scalar_tensor_tensor(out=dst, in0=gates[:, 8 * s + n, :], scalar=1.0,
                                                   in1=bank(name)[:, s % 2 * T:(s % 2 + 1) * T], op0=ALU.add, op1=ALU.mult)
                    if s == 0:
                        link(ins)
                    else:
                        ins.then_inc(read_done(name), 1)
                        evacuated(dve, name)
                link(dve.tensor_tensor(hidden[:, 0, :], hidden[:, 0, :], hidden[:, 1, :], ALU.add))
                dve.tensor_tensor(merged2[:, n, :], hidden[:, 0, :], silu[:, 0, :], ALU.add).then_inc(S("merged"), 1)
                dve.wait_ge(S("merged"), 8 + n + 1)
                if n:
                    input_lower(INPUT_PARTS["merged2"] + n - 1, p1_lo[:, n - 1, :], merged2[:, n - 1, :], p1_hi[:, n - 1, :])
            input_lower(INPUT_PARTS["merged2"] + 7, p1_lo[:, 7, :], merged2[:, 7, :], p1_hi[:, 7, :])
            for j in range(4):
                lower(2, j)
            dve.wait_ge(S("tiles_used"), AT[("out2", 7)] + 1)
            for n in range(DC):
                dve.scalar_tensor_tensor(out=h[:, n, :], in0=acc[n], scalar=mhalf[:, n:n + 1], in1=h[:, n, :],
                                         op0=ALU.mult, op1=ALU.add).then_inc(S("added"), 1)
            dve.wait_ge(S("added"), 8)
            begin_feed_forward(2, "norm2", (), range(4, RING), lambda n: gmod[:, 16 + n:17 + n], "prescaled")
            ffn_conv()
            dve.wait_ge(S("tiles_used"), AT[("down3", FC - 1)] + 1)
            for n in range(DC):
                dve.scalar_tensor_tensor(out=h[:, n, :], in0=acc[n], scalar=modc[:, 40 + n, 0:1], in1=h[:, n, :],
                                         op0=ALU.mult, op1=ALU.add).then_inc(S("result_ready"), 1)

        @block.gpsimd
        def _(pool):
            def weights_lower(first, last):
                for i in range(SPLIT_INDEX[first], SPLIT_INDEX[last] + 1):
                    t = SPLIT_TILES[i]
                    pool.wait_ge(S("weight_uppers"), i + 1)
                    pool.tensor_tensor(tile_lo[:, t % RING, :], ring[:, t % RING, :], upper_places[:, SPLIT_PLACE[t], :],
                                       ALU.subtract).then_inc(S("weights_split"), 1)
                pool.wait_ge(S("weights_split"), SPLIT_INDEX[last] + 1)

            def lower(k, j, more=0):
                t = AT[(f"gate{FFNS[k]}", 0)] + j
                pool.wait_ge(S("upper_ready"), more * RING + (3 * FC * k + j + 1))
                pool.tensor_tensor(ring_lo[:, j % RING, :], ring[:, t % RING, :], ring_hi[:, j % RING, :],
                                   ALU.subtract).then_inc(S("lower_ready_2"), 1)

            def feed_forward(k):
                after = (2, 4, 5) if k == 0 else (1, 2, 3)
                if k < 2:
                    for g in range(3):
                        pool.dma_start(cond_places[g], dram["conditioning"][3 * DC * k + g]).then_inc(S(f"cond_tile{g}"), 16)
                for par in range(2):
                    lower(k, 8 + 3 * par)
                if k < 2:
                    with pool.Fori(0, DC - 1) as i:
                        for par in range(2):
                            lower(k, 14 + 3 * par, i)
                            for g in ((0,), (1, 2))[par]:
                                pool.wait_ge(S("cond_steps"), i * COND_TURN[k] + (COND_FROM[k] + after[g]))
                                pool.dma_start(cond_places[g], dram["conditioning"][bass.ds(i * 3 + (3 * DC * k + 3 + g), 1)]
                                               .rearrange("a p n -> (a p) n")).then_inc(S(f"cond_tile{g}"), 16)
                    for i in (DC - 1, DC):
                        for par in range(2):
                            lower(k, 14 + 3 * par, i)
                else:
                    with pool.Fori(0, FC // 2 - 2) as i:
                        for par in range(2):
                            lower(k, 14 + 3 * par, i)
                pool.wait_ge(S("lower_ready_2"), LOWERS_2 * (k + 1))

            pool.wait_ge(S("cond_ready"), 1)
            feed_forward(0)
            weights_lower(AT[("cq", 0)], AT[("out1", 7)])
            pool.wait_ge(S("residual"), 16)
            pool.dma_start(ctx_raw, dram["ctx"]).then_inc(S("ctx_loaded"), 16)
            pool.memset(colr[64:P], 0.0).then_inc(S("colr_zero"), 1)
            pool.wait_ge(S("colr_zero"), 1)
            feed_forward(1)

            def causal(name, n, x, d):
                pool.wait_ge(S(f"{name}_args"), n + 1)
                a = arg[:, x, 2:4, :] if d == 0 else arg[:, x, 0:2, :]
                sgn = 1 - 2 * d
                pool.affine_select(out=a, in_=a, compare_op=ALU.is_ge, fill=NEG, base=0,
                                   pattern=[[-sgn * P, 2], [sgn, T]], channel_multiplier=-sgn)\
                    .then_inc(S(f"{name}_masked"), 1)

            weights_lower(AT[("rows", 0)], AT[("sz", 3)])
            for i in range(8):
                causal("m", i, i % 2, i % 2)
            for hd in range(8):
                for d in range(2):
                    causal("s", 2 * hd + d, d, d)
            pool.wait_ge(S("s_masked"), 16)
            weights_lower(AT[("wm", 0)], AT[("out2", 7)])
            feed_forward(2)


def two_pi_parts():
    parts, rest = [], TWO_PI
    for _ in range(3):
        e = 2.0 ** (int(np.floor(np.log2(rest))) - 7)
        parts.append(float(np.floor(rest / e) * e))
        rest -= parts[-1]
    return parts + [float(np.float32(rest))]


def _chunks(a):
    return np.ascontiguousarray(np.asarray(a).reshape(-1, P).T)


def _stream(x):
    w1, w2 = x["w_in"][0], x["w_in_2"][0]
    o1 = np.cumsum([0, Q_RANK, KV_RANK, ROPE_D, 512, 512, 512, 2048])
    o2 = np.cumsum([0, 1024, 512, 512, 16, 512, 512, 512, 512, 1024, 16, 3072])
    rows = np.zeros((D, P), np.float32)
    for d in range(2):
        rows[:, ROW_I[d]:ROW_I[d] + 4] = w2[:, o2[3] + 8 * d:o2[3] + 8 * d + 4]
        rows[:, ROW_F[d]:ROW_F[d] + 4] = w2[:, o2[3] + 8 * d + 4:o2[3] + 8 * d + 8]
        rows[:, ROW_DT[d]:ROW_DT[d] + 8] = w2[:, o2[9] + 8 * d:o2[9] + 8 * d + 8]
    up = x["w_up_2"][0]
    mats = {
        "gate1": x["ffn1_w_gate"][0], "up1": x["ffn1_w_up"][0], "down1": x["ffn1_w_down"][0],
        "gate2": x["ffn2_w_gate"][0], "up2": x["ffn2_w_up"][0], "down2": x["ffn2_w_down"][0],
        "gate3": up[:, FF:], "up3": up[:, :FF], "down3": x["w_down_2"][0],
        "cq": w1[:, o1[0]:o1[1]], "ckv": w1[:, o1[1]:o1[2]], "dq": w1[:, o1[3]:o1[4]], "dk": w1[:, o1[4]:o1[5]],
        "dv": w1[:, o1[5]:o1[6]], "g1": w1[:, o1[6]:], "uk": x["w_uk"][0], "uv": x["w_uv"][0],
        "wa": x["w_branch_a"][0], "wb": x["w_branch_b"][0], "out1": x["w_out"][0],
        "rows": rows, "mq": w2[:, 0:512], "mk": w2[:, 512:1024], "mv": w2[:, o2[1]:o2[2]],
        "mo": w2[:, o2[2]:o2[3]], "aq": w2[:, o2[4]:o2[5]], "ak": w2[:, o2[5]:o2[6]], "av": w2[:, o2[6]:o2[7]],
        "sz": w2[:, o2[7]:o2[8]], "sx": w2[:, o2[8]:o2[8] + 512], "sb": w2[:, o2[8] + 512:o2[8] + 768],
        "sc": w2[:, o2[8] + 768:o2[9]], "g2": w2[:, o2[10]:], "wm": x["w_branch_m_2"][0],
        "wat": x["w_branch_a_2"][0], "ws": x["w_branch_s_2"][0], "out2": x["w_out_2"][0]}
    out = np.empty((NT, P, TILE), np.float32)
    for t, (m, kind, n) in enumerate(ORDER):
        w = mats[m]
        if kind == "cols":
            a = w[:, n * P:(n + 1) * P].reshape(DC, P, P).transpose(1, 0, 2)
        elif kind == "down":
            a = w[n * P:(n + 1) * P]
        elif kind == "wide":
            a = w[2 * n * P:2 * (n + 1) * P].reshape(2, P, 512).transpose(1, 0, 2)
        elif kind == "small":
            a = w.reshape(2, P, 512).transpose(1, 0, 2)
        else:
            a = w[:, 2 * n * P:2 * (n + 1) * P].reshape(4, P, 2, P).transpose(1, 2, 0, 3)
        out[t] = a.reshape(P, TILE)
    return out


def _vectors(x):
    vec = np.zeros((P, NVEC), np.float32)

    def put(name, a):
        vec[:a.shape[0], VEC[name]:VEC[name] + a.shape[1]] = a

    for name, src in [("ffn1_pre", "ffn1_pre_g"), ("ffn1_post", "ffn1_post_g"), ("mix_pre", "mix_pre_g"),
                      ("mix_post", "mix_post_g"), ("ffn2_pre", "ffn2_pre_g"), ("ffn2_post", "ffn2_post_g"),
                      ("bgate", "b_gate"), ("q_norm", "q_norm_g"), ("kv_norm", "kv_norm_g"), ("norm1", "norm1_g_2"),
                      ("norm2", "norm2_g_2"), ("bmod", "b_mod_2"), ("mconv", "m_conv_w_2"), ("mconv_b", "m_conv_b_2"),
                      ("mnorm", "m_norm_g_2"), ("subln", "a_subln_g_2"), ("sconv", "s_conv_w_2"),
                      ("sconv_b", "s_conv_b_2"), ("snorm", "s_norm_g_2")]:
        put(name, _chunks(x[src]))
    put("aqn", np.tile(x["a_qnorm_g_2"].reshape(64, 1), (2, 1)))
    put("akn", np.tile(x["a_knorm_g_2"].reshape(64, 1), (2, 1)))
    put("sskip", _chunks(np.repeat(x["s_d_2"].reshape(-1), 64)))
    fc = x["ffn_conv_w_2"][0].reshape(3, 2, FC, P)[:, ::-1]
    put("fconv", fc.reshape(-1, P).T)
    for d in range(2):
        vec[ROW_F[d]:ROW_F[d] + 4, VEC["row_bias"]] = x["m_fgate_b_2"][0, d]
        vec[ROW_F[d]:ROW_F[d] + 4, VEC["row_ibias"]] = x["m_igate_b_2"][0, d]
        vec[ROW_DT[d]:ROW_DT[d] + 8, VEC["row_bias"]] = x["s_dt_bias_2"][0, d]
        vec[ROW_DT[d]:ROW_DT[d] + 8, VEC["row_alog"]] = x["s_a_log_2"][0, d]
    cond = np.stack([x["c_2"].reshape(DC, P), x["c_ctx_2"].reshape(DC, P)])
    put("cond", cond.transpose(2, 1, 0).reshape(P, 2 * DC))
    return vec


def kernel(**inputs):
    import concourse.bacc as bacc
    from concourse.bass_utils import run_bass_kernel_spmd

    x = {k: np.asarray(a) for k, a in inputs.items()}
    tokens = lambda a: np.ascontiguousarray(a[0].T.reshape(DC, P, T).transpose(1, 0, 2))
    w1 = x["w_in"][0]
    kr0 = Q_RANK + KV_RANK
    arrays = {
        "conditioning": np.ascontiguousarray(
            np.asarray(x["w_mod_2"])[0].reshape(DC, P, 2, 3, TILE).transpose(2, 0, 3, 1, 4)).reshape(6 * DC, P, TILE),
        "stream": _stream(x), "vec": _vectors(x), "cst": table_constants(),
        "x": tokens(x["x"]), "ctx": tokens(x["ctx_2"]),
        "wuq": np.ascontiguousarray(x["w_uq"][0].reshape(3, P, 768).transpose(1, 0, 2)),
        "wkr": np.ascontiguousarray(w1[:, kr0:kr0 + ROPE_D].reshape(DC, P, ROPE_D).transpose(1, 0, 2)),
        "lam": np.ascontiguousarray(x["a_lambda_2"].reshape(-1)),
        "pos": np.ascontiguousarray(x["positions"].reshape(-1)),
    }
    nc = bacc.Bacc("TRN2", target_bir_lowering=False, num_devices=1)
    dram = {n: nc.dram_tensor(n, a.shape, I32 if n == "pos" else F32, kind="ExternalInput").ap()
            for n, a in arrays.items()}
    dram["out"] = nc.dram_tensor("out", (DC, P, T), F32, kind="ExternalOutput").ap()
    two_blocks(nc, dram)
    r = run_bass_kernel_spmd(nc, [arrays], core_ids=[0])
    got = r.results[0]["out"]
    return np.ascontiguousarray(got.reshape(1, D, T).transpose(0, 2, 1))
```
